# Optimizing a Trainium2 kernel written in Bass

```python
import jax, jax.numpy as jnp
from jax import lax
import numpy as np

D_MODEL = 1024
BATCH = 1
SEQ = 256
DEPTH = 1

CHUNK = 64
Q_BLOCK = 128
SB_HEADS = 8
SB_HEAD_DIM = 64
SB_WIDTH = SB_HEADS * SB_HEAD_DIM
RW_HEADS = 8
RW_HEAD_DIM = 64
RW_WIDTH = RW_HEADS * RW_HEAD_DIM
W_LORA = 64
A_LORA = 64
G_LORA = 128
GN_EPS = RW_HEAD_DIM * 1e-5
N_BRANCH = 2
SB_COLS = 3 * SB_WIDTH
RW_COLS = 3 * RW_WIDTH + W_LORA + A_LORA + G_LORA
GATE_COLS = N_BRANCH * D_MODEL
IN_COLS = SB_COLS + RW_COLS + GATE_COLS
D_FF = ((8 * D_MODEL + 3 * 256 - 1) // (3 * 256)) * 256
RMS_EPS = 1e-6


def rms_norm(x, g):
    xf = x.astype(jnp.float32)
    y = xf * lax.rsqrt(jnp.mean(xf * xf, axis=-1, keepdims=True) + RMS_EPS)
    return (y * g).astype(x.dtype)

def token_shift(p):
    return jnp.pad(p, ((0, 0), (1, 0), (0, 0)))[:, :-1]

def stick_breaking_attention(q, k, v):
    B, S, H, Dh = q.shape
    scale = Dh ** -0.5
    outs = []
    for i in range(S // Q_BLOCK):
        q0 = i * Q_BLOCK
        kv_len = q0 + Q_BLOCK
        qb = q[:, q0:kv_len]
        kb = k[:, :kv_len]
        vb = v[:, :kv_len]
        z = jnp.einsum('bqhd,bkhd->bhqk', qb, kb).astype(jnp.float32) * scale
        t_idx = q0 + jnp.arange(Q_BLOCK)[:, None]
        s_idx = jnp.arange(kv_len)[None, :]
        strict = s_idx < t_idx
        log_fail = jnp.where(strict, jax.nn.log_sigmoid(-z), 0.0)
        after = lax.cumsum(log_fail, axis=3, reverse=True) - log_fail
        w = jnp.where(strict, jnp.exp(jax.nn.log_sigmoid(z) + after), 0.0)
        outs.append(jnp.einsum('bhqk,bkhd->bqhd', w.astype(vb.dtype), vb))
    return jnp.concatenate(outs, axis=1)

def wkv7_scan(r, decay, k, v, kk, a):
    B, S, H, N = r.shape

    def to_chunks(t):
        return t.astype(jnp.float32).transpose(1, 0, 2, 3).reshape(S // CHUNK, CHUNK, B, H, N)

    def step(state, inp):
        r_t, w_t, k_t, v_t, kk_t, a_t = inp
        sa = jnp.einsum('bhvk,bhk->bhv', state, -kk_t)
        state = (state * w_t[:, :, None, :]
                 + sa[..., None] * (kk_t * a_t)[:, :, None, :]
                 + v_t[..., None] * k_t[:, :, None, :])
        return state, jnp.einsum('bhvk,bhk->bhv', state, r_t)

    def chunk_step(state, chunk_inp):
        return lax.scan(step, state, chunk_inp)

    state0 = jnp.zeros((B, H, N, N), jnp.float32)
    _, y = lax.scan(chunk_step, state0, tuple(to_chunks(t) for t in (r, decay, k, v, kk, a)))
    return y.reshape(S, B, H, N).transpose(1, 0, 2, 3)

def rwkv7_time_mix(p, mu, w0, w_up, a0, a_up, g_up, k_k, k_a, r_k, lnx_w, lnx_b):
    B, S, _ = p.shape
    H, N = RW_HEADS, RW_HEAD_DIM
    p = p + (token_shift(p) - p) * mu
    o1, o2, o3 = RW_WIDTH, 2 * RW_WIDTH, 3 * RW_WIDTH
    r, k, v = p[..., :o1], p[..., o1:o2], p[..., o2:o3]
    xw = p[..., o3:o3 + W_LORA]
    xa = p[..., o3 + W_LORA:o3 + W_LORA + A_LORA]
    xg = p[..., o3 + W_LORA + A_LORA:]
    w_raw = (w0 + jnp.tanh(xw) @ w_up).astype(jnp.float32)
    decay = jnp.exp(-jnp.exp(-jax.nn.softplus(-w_raw) - 0.5))
    a = jax.nn.sigmoid((a0 + xa @ a_up).astype(jnp.float32))
    g = jax.nn.sigmoid(xg) @ g_up
    kk = (k * k_k).astype(jnp.float32).reshape(B, S, H, N)
    kk = kk / jnp.maximum(jnp.linalg.norm(kk, axis=-1, keepdims=True), 1e-12)
    k = k.astype(jnp.float32) * (1.0 + (a - 1.0) * k_a)
    heads = lambda t: t.astype(jnp.float32).reshape(B, S, H, N)
    r_h, k_h, v_h = heads(r), heads(k), heads(v)
    y = wkv7_scan(r_h, heads(decay), k_h, v_h, kk, heads(a))
    mean = jnp.mean(y, axis=-1, keepdims=True)
    var = jnp.mean(jnp.square(y - mean), axis=-1, keepdims=True)
    y = ((y - mean) * lax.rsqrt(var + GN_EPS)).reshape(B, S, RW_WIDTH) * lnx_w + lnx_b
    bonus = (jnp.sum(r_h * k_h * r_k, axis=-1, keepdims=True) * v_h).reshape(B, S, RW_WIDTH)
    return ((y + bonus) * g).astype(p.dtype)

def first_inputs(seed: int = 0) -> dict:
    key = jax.random.key(seed)
    ks = jax.random.split(key, 24)
    L, D = DEPTH, D_MODEL
    nrm = lambda k_, shape, s: jax.random.normal(k_, shape, jnp.float32) * s
    return {
        "x": nrm(ks[0], (BATCH, SEQ, D), 1.0),
        "norm_mix_pre": 1.0 + nrm(ks[1], (L, D), 0.1),
        "w_in": nrm(ks[2], (L, D, IN_COLS), D ** -0.5),
        "b_gate": nrm(ks[3], (L, GATE_COLS), 0.1),
        "mu_rw": jax.random.uniform(ks[4], (L, RW_COLS), jnp.float32),
        "w0": jax.random.uniform(ks[5], (L, RW_WIDTH), jnp.float32, -6.0, 0.0),
        "w_up": nrm(ks[6], (L, W_LORA, RW_WIDTH), 0.1),
        "a0": nrm(ks[7], (L, RW_WIDTH), 0.1),
        "a_up": nrm(ks[8], (L, A_LORA, RW_WIDTH), 0.5 * A_LORA ** -0.5),
        "g_up": nrm(ks[9], (L, G_LORA, RW_WIDTH), G_LORA ** -0.5),
        "k_k": 0.85 + nrm(ks[10], (L, RW_WIDTH), 0.05),
        "k_a": 1.0 + nrm(ks[11], (L, RW_WIDTH), 0.05),
        "r_k": nrm(ks[12], (L, RW_HEADS, RW_HEAD_DIM), 0.1),
        "lnx_w": 1.0 + nrm(ks[13], (L, RW_WIDTH), 0.1),
        "lnx_b": nrm(ks[14], (L, RW_WIDTH), 0.02),
        "w_sb_out": nrm(ks[15], (L, SB_WIDTH, D), SB_WIDTH ** -0.5),
        "w_rw_out": nrm(ks[16], (L, RW_WIDTH, D), RW_WIDTH ** -0.5),
        "w_o": nrm(ks[17], (L, D, D), D ** -0.5),
        "norm_mix_post": 1.0 + nrm(ks[18], (L, D), 0.1),
        "norm_ffn_pre": 1.0 + nrm(ks[19], (L, D), 0.1),
        "w_ffn_gate": nrm(ks[20], (L, D, D_FF), D ** -0.5),
        "w_ffn_up": nrm(ks[21], (L, D, D_FF), D ** -0.5),
        "w_ffn_down": nrm(ks[22], (L, D_FF, D), D_FF ** -0.5),
        "norm_ffn_post": 1.0 + nrm(ks[23], (L, D), 0.1),
    }

def first_block(x, norm_mix_pre, w_in, b_gate, mu_rw, w0, w_up, a0, a_up, g_up, k_k, k_a, r_k,
              lnx_w, lnx_b, w_sb_out, w_rw_out, w_o, norm_mix_post, norm_ffn_pre,
              w_ffn_gate, w_ffn_up, w_ffn_down, norm_ffn_post):
    B, S, D = x.shape
    for l in range(DEPTH):
        h = rms_norm(x, norm_mix_pre[l])
        proj = h @ w_in[l]
        p_sb = proj[..., :SB_COLS]
        p_rw = proj[..., SB_COLS:SB_COLS + RW_COLS]
        gates = jax.nn.sigmoid(proj[..., SB_COLS + RW_COLS:] + b_gate[l])
        q = p_sb[..., :SB_WIDTH].reshape(B, S, SB_HEADS, SB_HEAD_DIM)
        k = p_sb[..., SB_WIDTH:2 * SB_WIDTH].reshape(B, S, SB_HEADS, SB_HEAD_DIM)
        v = p_sb[..., 2 * SB_WIDTH:].reshape(B, S, SB_HEADS, SB_HEAD_DIM)
        o_sb = stick_breaking_attention(q, k, v).reshape(B, S, SB_WIDTH)
        o_rw = rwkv7_time_mix(p_rw, mu_rw[l], w0[l], w_up[l], a0[l], a_up[l], g_up[l],
                              k_k[l], k_a[l], r_k[l], lnx_w[l], lnx_b[l])
        merged = (gates[..., :D] * (o_sb @ w_sb_out[l])
                  + gates[..., D:] * (o_rw @ w_rw_out[l]))
        x = x + rms_norm(merged @ w_o[l], norm_mix_post[l])
        h = rms_norm(x, norm_ffn_pre[l])
        f = (jax.nn.silu(h @ w_ffn_gate[l]) * (h @ w_ffn_up[l])) @ w_ffn_down[l]
        x = x + rms_norm(f, norm_ffn_post[l])
    return x


D_MIX = D_MODEL
POOL_WIDTH = D_MIX // 4
POOL_WINDOWS = (2, 4, 8, 16)
N_POOL_GROUPS = len(POOL_WINDOWS)
POOL_GROUP_DIM = POOL_WIDTH // N_POOL_GROUPS
SSD_WIDTH = D_MIX - POOL_WIDTH
SSD_HEAD_DIM = 64
SSD_HEADS = SSD_WIDTH // SSD_HEAD_DIM
SSD_GROUPS = 4
SSD_HEADS_PER_GROUP = SSD_HEADS // SSD_GROUPS
SSD_STATE = 128
SSD_CONV = 4
SSD_CHUNK = 128
SSD_CONV_DIM = SSD_WIDTH + 2 * SSD_GROUPS * SSD_STATE
IN_PROJ_DIM = POOL_WIDTH + SSD_WIDTH + SSD_CONV_DIM + SSD_HEADS
N_EXPERT_GROUPS = 4
EXPERTS_PER_GROUP = 8
N_EXPERTS = N_EXPERT_GROUPS * EXPERTS_PER_GROUP
TOP_K = 2
EXPERT_FF = 512
MOE_BLOCK = 128
NORM_EPS = 1e-6


def rms_norm_2(x, eps=NORM_EPS):
    xf = x.astype(jnp.float32)
    y = xf * lax.rsqrt(jnp.mean(xf * xf, axis=-1, keepdims=True) + eps)
    return y.astype(x.dtype)

def modulate(x, shift, scale):
    return rms_norm_2(x) * (1 + scale[:, None, :]) + shift[:, None, :]

def pool_mixer(u, w_pool, pool_scale):
    b, s, _ = u.shape
    ug = u.reshape(b, s, N_POOL_GROUPS, POOL_GROUP_DIM)
    cs = jnp.cumsum(ug.astype(jnp.float32), axis=1)
    pos = jnp.arange(1, s + 1, dtype=jnp.float32)
    means = []
    for g, w in enumerate(POOL_WINDOWS):
        csg = cs[:, :, g]
        lagged = jnp.pad(csg, ((0, 0), (w, 0), (0, 0)))[:, :s]
        cnt = jnp.minimum(pos, float(w))
        means.append((csg - lagged) / cnt[None, :, None])
    mean = jnp.stack(means, axis=2).astype(u.dtype)
    y = jnp.einsum('bsgc,gcd->bsgd', mean - ug, w_pool)
    return y.reshape(b, s, POOL_WIDTH) * pool_scale

def causal_depthwise_conv(x, w, bias):
    ch = x.shape[-1]
    y = lax.conv_general_dilated(
        x, w[:, None, :].astype(x.dtype), window_strides=(1,),
        padding=((SSD_CONV - 1, 0),), dimension_numbers=('NWC', 'WIO', 'NWC'),
        feature_group_count=ch)
    return y + bias

def ssd_scan(xh, dt, a, bmat, cmat):
    b, s = xh.shape[:2]
    L = SSD_CHUNK
    nc = s // L
    G, R, P, N = SSD_GROUPS, SSD_HEADS_PER_GROUP, SSD_HEAD_DIM, SSD_STATE
    xc = (xh.astype(jnp.float32) * dt[..., None]).reshape(b, nc, L, G, R, P)
    bc = bmat.astype(jnp.float32).reshape(b, nc, L, G, N)
    cc = cmat.astype(jnp.float32).reshape(b, nc, L, G, N)
    a_cs = jnp.cumsum((dt * a).reshape(b, nc, L, G, R), axis=2)
    causal = jnp.tril(jnp.ones((L, L), dtype=bool))
    seg = a_cs[:, :, :, None] - a_cs[:, :, None, :]
    decay = jnp.exp(jnp.where(causal[None, None, :, :, None, None], seg, -jnp.inf))
    cb = jnp.einsum('bclgn,bcsgn->bclsg', cc, bc)
    y_diag = jnp.einsum('bclsgr,bcsgrp->bclgrp', cb[..., None] * decay, xc)
    decay_to_end = jnp.exp(a_cs[:, :, -1:] - a_cs)
    chunk_states = jnp.einsum('bclgn,bclgrp->bcgrpn', bc, xc * decay_to_end[..., None])
    chunk_decay = jnp.exp(a_cs[:, :, -1])

    def step(state, inp):
        st, dec = inp
        return state * dec[..., None, None] + st, state

    init = jnp.zeros((b, G, R, P, N), jnp.float32)
    _, prev = lax.scan(step, init, (jnp.moveaxis(chunk_states, 1, 0),
                                    jnp.moveaxis(chunk_decay, 1, 0)))
    prev = jnp.moveaxis(prev, 0, 1)
    y_off = jnp.einsum('bclgn,bcgrpn->bclgrp', cc, prev) * jnp.exp(a_cs)[..., None]
    return (y_diag + y_off).reshape(b, s, G, R, P)

def ssd_mixer(z, xbc, dt_raw, conv_w, conv_b, dt_bias, a_log, d_skip, norm_w):
    b, s, _ = z.shape
    G, R, P, N = SSD_GROUPS, SSD_HEADS_PER_GROUP, SSD_HEAD_DIM, SSD_STATE
    xbc = jax.nn.silu(causal_depthwise_conv(xbc, conv_w, conv_b))
    xs, bm, cm = jnp.split(xbc, [SSD_WIDTH, SSD_WIDTH + G * N], axis=-1)
    xh = xs.reshape(b, s, G, R, P)
    bm = bm.reshape(b, s, G, N)
    cm = cm.reshape(b, s, G, N)
    dt = jax.nn.softplus(dt_raw.astype(jnp.float32) + dt_bias.astype(jnp.float32)).reshape(b, s, G, R)
    a = -jnp.exp(a_log.astype(jnp.float32)).reshape(G, R)
    y = ssd_scan(xh, dt, a, bm, cm) + xh.astype(jnp.float32) * d_skip.astype(jnp.float32).reshape(G, R)[..., None]
    y = y.reshape(b, s, SSD_WIDTH).astype(z.dtype) * jax.nn.silu(z)
    y = rms_norm_2(y.reshape(b, s, G, SSD_WIDTH // G)).reshape(b, s, SSD_WIDTH)
    return y * norm_w

def hier_moe(h, w_group, b_group, w_router, b_router, w13, w2):
    b, s, d = h.shape
    T = b * s
    hf = h.reshape(T, d)
    g_logits = (hf @ w_group + b_group).astype(jnp.float32)
    g_prob = jax.nn.softmax(g_logits, axis=-1)
    p_g, g_idx = lax.top_k(g_prob, 1)
    e_logits = (hf @ w_router + b_router).astype(jnp.float32).reshape(T, N_EXPERT_GROUPS, EXPERTS_PER_GROUP)
    within = jnp.take_along_axis(e_logits, g_idx[:, :, None], axis=1)[:, 0]
    top_v, top_i = lax.top_k(within, TOP_K)
    gate = p_g * jax.nn.softmax(top_v, axis=-1)
    expert_id = (g_idx * EXPERTS_PER_GROUP + top_i).astype(jnp.int32)
    A = T * TOP_K
    flat_e = expert_id.reshape(A)
    flat_tok = jnp.repeat(jnp.arange(T, dtype=jnp.int32), TOP_K)
    flat_w = gate.reshape(A)
    order = jnp.argsort(flat_e)
    se, stok, sw = flat_e[order], flat_tok[order], flat_w[order]
    counts = jnp.bincount(flat_e, length=N_EXPERTS)
    starts = jnp.cumsum(counts) - counts
    padded = ((counts + MOE_BLOCK - 1) // MOE_BLOCK) * MOE_BLOCK
    pends = jnp.cumsum(padded)
    pstarts = pends - padded
    dest = pstarts[se] + (jnp.arange(A, dtype=jnp.int32) - starts[se])
    R = A + N_EXPERTS * MOE_BLOCK
    n_blk = R // MOE_BLOCK
    row_tok = jnp.zeros((R,), jnp.int32).at[dest].set(stok)
    row_w = jnp.zeros((R,), h.dtype).at[dest].set(sw.astype(h.dtype))
    blk_start = jnp.arange(n_blk, dtype=jnp.int32) * MOE_BLOCK
    blk_e = jnp.clip(jnp.searchsorted(pends, blk_start, side='right'), 0, N_EXPERTS - 1)
    xs = hf[row_tok].reshape(n_blk, MOE_BLOCK, d)

    def expert_block(args):
        xb, e = args
        hu = xb @ w13[e]
        a_, b_ = jnp.split(hu, 2, axis=-1)
        return (jax.nn.silu(a_) * b_) @ w2[e]

    ys = lax.map(expert_block, (xs, blk_e)).reshape(R, d)
    out = jax.ops.segment_sum(ys * row_w[:, None], row_tok, num_segments=T)
    return out.reshape(b, s, d)

def second_inputs(seed: int = 0) -> dict:
    key = jax.random.key(seed)
    ks = jax.random.split(key, 24)
    f32 = jnp.float32
    nrm = lambda k, shape, scale: jax.random.normal(k, shape, f32) * scale
    x = jax.random.normal(ks[0], (BATCH, SEQ, D_MODEL), f32)
    c = jax.random.normal(ks[1], (BATCH, D_MODEL), f32)
    w_ada = nrm(ks[2], (DEPTH, D_MODEL, 6 * D_MODEL), D_MODEL ** -0.5)
    b_ada = nrm(ks[3], (DEPTH, 6 * D_MODEL), 0.02)
    w_in = nrm(ks[4], (DEPTH, D_MODEL, IN_PROJ_DIM), D_MODEL ** -0.5)
    w_pool = nrm(ks[5], (DEPTH, N_POOL_GROUPS, POOL_GROUP_DIM, POOL_GROUP_DIM), POOL_GROUP_DIM ** -0.5)
    pool_scale = 1.0 + nrm(ks[6], (DEPTH, POOL_WIDTH), 0.1)
    conv_w = nrm(ks[7], (DEPTH, SSD_CONV, SSD_CONV_DIM), SSD_CONV ** -0.5)
    conv_b = nrm(ks[8], (DEPTH, SSD_CONV_DIM), 0.02)
    dt0 = jnp.exp(jax.random.uniform(ks[9], (DEPTH, SSD_HEADS), f32, np.log(1e-3), np.log(1e-1)))
    dt_bias = dt0 + jnp.log(-jnp.expm1(-dt0))
    a_log = jnp.log(jax.random.uniform(ks[10], (DEPTH, SSD_HEADS), f32, 1.0, 16.0))
    d_skip = 1.0 + nrm(ks[11], (DEPTH, SSD_HEADS), 0.1)
    ssd_norm_w = 1.0 + nrm(ks[12], (DEPTH, SSD_WIDTH), 0.1)
    w_out = nrm(ks[13], (DEPTH, D_MIX, D_MODEL), D_MIX ** -0.5)
    w_group = nrm(ks[14], (DEPTH, D_MODEL, N_EXPERT_GROUPS), D_MODEL ** -0.5)
    b_group = nrm(ks[15], (DEPTH, N_EXPERT_GROUPS), 0.01)
    w_router = nrm(ks[16], (DEPTH, D_MODEL, N_EXPERTS), D_MODEL ** -0.5)
    b_router = nrm(ks[17], (DEPTH, N_EXPERTS), 0.01)
    w13 = nrm(ks[18], (DEPTH, N_EXPERTS, D_MODEL, 2 * EXPERT_FF), D_MODEL ** -0.5)
    w2 = nrm(ks[19], (DEPTH, N_EXPERTS, EXPERT_FF, D_MODEL), EXPERT_FF ** -0.5)
    final_norm_w = 1.0 + nrm(ks[20], (D_MODEL,), 0.1)
    return {"x": x, "c": c, "w_ada": w_ada, "b_ada": b_ada, "w_in": w_in,
            "w_pool": w_pool, "pool_scale": pool_scale, "conv_w": conv_w, "conv_b": conv_b,
            "dt_bias": dt_bias, "a_log": a_log, "d_skip": d_skip, "ssd_norm_w": ssd_norm_w,
            "w_out": w_out, "w_group": w_group, "b_group": b_group, "w_router": w_router,
            "b_router": b_router, "w13": w13, "w2": w2, "final_norm_w": final_norm_w}

def second_block(x, c, w_ada, b_ada, w_in, w_pool, pool_scale, conv_w, conv_b, dt_bias, a_log,
              d_skip, ssd_norm_w, w_out, w_group, b_group, w_router, b_router, w13, w2,
              final_norm_w):
    split_at = [POOL_WIDTH, POOL_WIDTH + SSD_WIDTH, POOL_WIDTH + SSD_WIDTH + SSD_CONV_DIM]
    for layer in range(DEPTH):
        mod = jax.nn.silu(c) @ w_ada[layer] + b_ada[layer]
        sh1, sc1, g1, sh2, sc2, g2 = jnp.split(mod, 6, axis=-1)
        h = modulate(x, sh1, sc1)
        proj = h @ w_in[layer]
        u, z, xbc, dt_raw = jnp.split(proj, split_at, axis=-1)
        y_pool = pool_mixer(u, w_pool[layer], pool_scale[layer])
        y_ssd = ssd_mixer(z, xbc, dt_raw, conv_w[layer], conv_b[layer], dt_bias[layer],
                          a_log[layer], d_skip[layer], ssd_norm_w[layer])
        mix = jnp.concatenate([y_pool, y_ssd], axis=-1) @ w_out[layer]
        x = x + g1[:, None, :] * mix
        h = modulate(x, sh2, sc2)
        x = x + g2[:, None, :] * hier_moe(h, w_group[layer], b_group[layer], w_router[layer],
                                           b_router[layer], w13[layer], w2[layer])
    return rms_norm_2(x) * final_norm_w


def setup_inputs(seed=0):
    out = dict(first_inputs(seed))
    for name, value in second_inputs(seed + 1).items():
        if name != "x":
            out[name + "_2"] = value
    return out


def reference(
    x, norm_mix_pre, w_in, b_gate, mu_rw, w0, w_up, a0, a_up, g_up, k_k, k_a, r_k, lnx_w, lnx_b,
    w_sb_out, w_rw_out, w_o, norm_mix_post, norm_ffn_pre, w_ffn_gate, w_ffn_up, w_ffn_down,
    norm_ffn_post, c_2, w_ada_2, b_ada_2, w_in_2, w_pool_2, pool_scale_2, conv_w_2, conv_b_2,
    dt_bias_2, a_log_2, d_skip_2, ssd_norm_w_2, w_out_2, w_group_2, b_group_2, w_router_2,
    b_router_2, w13_2, w2_2, final_norm_w_2,
):
    x = first_block(
        x, norm_mix_pre, w_in, b_gate, mu_rw, w0, w_up, a0, a_up, g_up, k_k, k_a, r_k, lnx_w,
        lnx_b, w_sb_out, w_rw_out, w_o, norm_mix_post, norm_ffn_pre, w_ffn_gate, w_ffn_up,
        w_ffn_down, norm_ffn_post,
    )
    return second_block(
        x, c_2, w_ada_2, b_ada_2, w_in_2, w_pool_2, pool_scale_2, conv_w_2, conv_b_2, dt_bias_2,
        a_log_2, d_skip_2, ssd_norm_w_2, w_out_2, w_group_2, b_group_2, w_router_2, b_router_2,
        w13_2, w2_2, final_norm_w_2,
    )


_drawn_inputs = setup_inputs


def setup_inputs(seed=0):
    import zlib

    import numpy as np

    out = dict(_drawn_inputs(seed))
    spreads = {}
    factors = {'lnx_b': 3.911, 'conv_b_2': 3.17, 'b_group_2': 8.0, 'b_router_2': 4.998, 'd_skip_2': 3.068}
    for name, (base, spread) in spreads.items():
        noise = np.random.default_rng([zlib.crc32(name.encode()), seed]).standard_normal(out[name].shape)
        drawn = base * np.exp(spread * noise) if base else spread * noise
        out[name] = __import__('jax').numpy.asarray(drawn.astype(out[name].dtype))
    for name, factor in factors.items():
        out[name] = (out[name] * factor).astype(out[name].dtype)
    return out
```

```python
import numpy as np
import concourse.bass as bass
from concourse import mybir
from contextlib import ExitStack

F32 = mybir.dt.float32
U8 = mybir.dt.uint8
ALU = mybir.AluOpType
ACT = mybir.ActivationFunctionType
AX = mybir.AxisListType

P = 128
SEQ = 256
NT = SEQ // P
D = 1024
KD = D // P
HEADS = 8
DH = 64
WID = HEADS * DH
PAIRS = HEADS // 2
CH = 64
SB_COLS = 3 * WID
RW_COLS = 3 * WID + 256
FF = 2816
KF = FF // P
GN_EPS = DH * 1e-5
EPS = 1e-6
DECAY = -float(np.exp(-0.5))
GRP = 4
SH = 12
SR = SH // GRP
POOL = 256
SSD = 768
XBC = SSD + 2 * GRP * P
MX = XBC // P
WINDOWS = (2, 4, 8, 16)
EXPERTS = 32
EG = 4
EPG = EXPERTS // EG
EF = 512
KE = EF // P
BIG = 1e30

SLOT = 4096
RING = 3
LEVELS = 6
NPAR = 3


def const_layout():
    names = [("ident", P), ("ones", P), ("neg_suffix", P), ("neg_ones", P), ("strict", P), ("gram_mask", 4 * P),
             ("head_block", P), ("head_mean", P), ("scan_reset", SEQ), ("head_sum", PAIRS * HEADS),
             ("head_spread", PAIRS * P), ("causal", P), ("after", P), ("thirty_second", P),
             ("rev_group", NT * EG), ("rev_expert", NT * EXPERTS)]
    at, out = 0, {}
    for n, w in names:
        out[n] = (at, at + w)
        at += w
    return out, at


CONST, NCONST = const_layout()


def host_constants():
    c = np.zeros((P, NCONST), np.float32)
    i, j = np.arange(P)[:, None], np.arange(P)[None, :]
    same = (i // CH) == (j // CH)

    def put(name, v):
        a, b = CONST[name]
        c[:, a:b] = v

    put("ident", i == j)
    put("ones", 1.0)
    put("neg_suffix", -1.0 * (i >= j))
    put("neg_ones", -1.0)
    put("strict", i < j)
    put("gram_mask", np.concatenate([same & (i < j), same & (i <= j)] * 2, axis=1))
    put("head_block", same)
    put("head_mean", same / DH)
    put("scan_reset", (np.arange(SEQ) % CH != 0)[None, :])
    a, b = CONST["head_sum"]
    s = np.zeros((P, PAIRS, HEADS), np.float32)
    t = np.zeros((P, PAIRS, P), np.float32)
    for p in range(PAIRS):
        for h in range(2):
            s[h * DH:(h + 1) * DH, p, 2 * p + h] = 1
            t[2 * p + h, p, h * DH:(h + 1) * DH] = 1
    c[:, a:b] = s.reshape(P, -1)
    a, b = CONST["head_spread"]
    c[:, a:b] = t.reshape(P, -1)
    put("causal", i <= j)
    put("after", i > j)
    put("thirty_second", 1.0 / 32)
    put("rev_group", np.tile(EG - np.arange(EG), NT)[None, :])
    put("rev_expert", np.tile(EXPERTS - np.arange(EXPERTS), NT)[None, :])
    return c


def host_level_masks():
    i, j = np.arange(P)[:, None], np.arange(P)[None, :]
    m = np.zeros((P, 2, LEVELS, P), np.float32)
    for n in range(LEVELS):
        s = 1 << n
        low = (i // (2 * s) == j // (2 * s)) & ((i // s) % 2 == 1) & ((j // s) % 2 == 0)
        m[:, 0, n] = low
        m[:, 1, n] = low.T
    return m.reshape(P, -1)


def host_bands():
    t, s = np.arange(SEQ)[None, :], np.arange(SEQ)[:, None]
    out = np.zeros((P, GRP, SEQ + P), np.float32)
    for g, w in enumerate(WINDOWS):
        band = ((s <= t) & (s > t - w)) / np.minimum(t + 1, w) - (s == t)
        out[:, g, :SEQ] = band[:P]
        out[:, g, SEQ:] = band[P:, P:]
    return out.reshape(P, -1)


PAR = [
    [("norm_mix_pre", 8), ("mu_rw", 14), ("w0", 4), ("a0", 4), ("k_k", 4), ("k_a", 4), ("r_k", 4), ("lnx_w", 4),
     ("lnx_b", 4), ("b_gate", 16), ("norm_ffn_pre", 8), ("c_2", 8)],
    [("pool_scale_2", 2), ("conv_w_2", 4 * MX), ("conv_b_2", MX), ("ssd_norm_w_2", 6)],
    [("b_ada_2", 48)],
]


def par_columns():
    out = {}
    for n, rows in enumerate(PAR):
        at = 0
        for name, r in rows:
            out[name] = (n, at, r)
            at += r
    return out


PARCOL = par_columns()


def ada_banks(c):
    return ([("as", c - 1)] if c else []) + [("ad", c)]


def plan_banks():
    o = [("par", n) for n in range(NPAR)]
    o += [("hT", 0, kk) for kk in range(4)]
    o += [("rw", mm) for mm in RW_ORDER]
    o += [(n, mm) for n in ("lw", "la", "lg") for mm in range(2)]
    o += [("qk", mm) for mm in range(4)] + [("v", i) for i in range(NT)]
    o += [("kn",)] + [("kb", mm) for mm in range(2)]
    o += [("z", h) for h in range(HEADS)]
    o += [("bn", mm) for mm in range(2)]
    o += [("l", h) for h in range(HEADS)]
    o += [("o", p) for p in range(PAIRS)]
    o += [("tok", i, a) for i in range(NT) for a in range(4)]
    ada = 0
    for i in range(NT):
        o += [("g", i, h) for h in range(HEADS)]
        o += [("n", i, q) for q in range(2)]
        for lv in range(1, LEVELS):
            o += [("x", i, lv, q) for q in range(2)]
            o += ada_banks(ada)
            ada += 1
            for q in range(2):
                o += ([("d", i, lv, q)] if lv < LEVELS - 1 else []) + [("dt", i, lv, q)]
        o += [("w1", i, q) for q in range(2)]
        o += ada_banks(ada)
        ada += 1
        o += [("u", i, q) for q in range(2)]
        if i == 0:
            o += [("ry", 0), ("psi", 0), ("psi", 1), ("phi", 1), ("y", 0), ("s", 1)]
        else:
            o += [("ry", 1), ("psi", 2), ("phi", 2), ("s", 2), ("y", 1)]
    o += [("as", 11)]
    o += [("ga", mm) for mm in range(0, 2)] + [("m", mm) for mm in range(2)]
    o += [("ga", mm) for mm in range(2, 5)] + [("vn",)]
    o += [("ga", mm) for mm in range(5, 8)] + [("vb", mm) for mm in range(2)]
    o += [("mg", dm) for dm in range(KD)]
    o += [("mo", i, n) for n in range(2) for i in range(NT)]
    o += [("hT", 1, kk) for kk in range(4)]
    o += [("ff", m) for m in range(KF)]
    o += [("dn", i, n) for n in range(2) for i in range(NT)]
    o += [("hT", 2, kk) for kk in range(4)]
    o += [("uz", i, n) for n in range(2) for i in range(NT)]
    o += [("xb", mm) for mm in range(7)]
    o += [("dt2",), ("pl",), ("cs",), ("pm",)]
    o += [("rb", i, q) for i in range(NT) for q in range(3)]
    o += [("cb", i) for i in range(NT)]
    o += [("xt", i, a) for i in range(NT) for a in range(2)] + [("bt",)]
    o += [("yd", 0, a) for a in range(2)] + [("cst", a) for a in range(2)]
    o += [("yd", 1, a) for a in range(2)] + [("yo", a) for a in range(2)]
    o += [("mt", i, a) for i in range(NT) for a in range(2)]
    o += [("mx", i, n) for n in range(2) for i in range(NT)]
    o += [("hT", 3, kk) for kk in range(4)]
    o += [("rt",)]
    assert len(set(o)) == len(o)
    return {k: (n % 8, n // 8) for n, k in enumerate(o)}


RW_ORDER = (6, 2, 3, 0, 1, 4, 5)
COLUMN_CHUNKS = (0, 1, 2, 3, 6, 7, 8, 9)
QTOK = 4 * SEQ

NORM1, PROJ, PREP, TOKENS, WKV, GATES, MERGE, POST1, FFN, DOWN, PROJ2, CONV, SCAN, MIXED, MOE = range(15)
BUFFERS = [
    ("junk", D, NORM1, MOE), ("parrow", NPAR * P, NORM1, NORM1), ("g1", D, NORM1, MIXED), ("g2", D, NORM1, MOE),
    ("wua", WID, NORM1, PROJ), ("gup", WID, NORM1, PROJ), ("cb", KD * 32, NORM1, WKV), ("npost", D, MERGE, POST1),
    ("xn0", NT * D, NORM1, NORM1), ("lvlf", 2 * LEVELS * P, NORM1, NORM1),
    ("osb", QTOK, PREP, MERGE), ("gT", QTOK, PROJ, GATES), ("bon", QTOK, PREP, GATES),
    ("tmp", QTOK, PREP, GATES), ("nmr", SEQ, PREP, GATES),
    ("kr", 2 * QTOK, PREP, WKV), ("bh", QTOK, PREP, WKV), ("kh", QTOK, PREP, WKV),
    ("kT", QTOK, PROJ, TOKENS), ("vT", QTOK, PROJ, TOKENS), ("b", QTOK, PREP, TOKENS),
    ("rT", QTOK, PROJ, PREP), ("lora", 2 * SEQ, PROJ, PREP), ("a", QTOK, PROJ, PREP), ("lw", QTOK, PROJ, PREP),
    ("kk", QTOK, PREP, PREP), ("cum", QTOK, PREP, PREP), ("qk", 2 * QTOK, PROJ, PREP), ("v", NT * WID, PROJ, PREP),
    ("az", HEADS * 384, PREP, PREP), ("rz", HEADS * 384, PREP, PREP),
    ("vp", NT * HEADS * P, TOKENS, WKV), ("btok", NT * WID, TOKENS, WKV), ("ktok", NT * WID, TOKENS, WKV),
    ("zb", NT * HEADS * P, TOKENS, WKV),
    ("modp", 2 * 512, WKV, GATES), ("gm", HEADS * 4 * P, WKV, WKV), ("dd", HEADS * P, WKV, WKV),
    ("ddT", HEADS * P, WKV, WKV), ("xx", HEADS * P, WKV, WKV), ("up", HEADS * DH, WKV, WKV),
    ("tk", HEADS * DH, WKV, WKV), ("phi", 2 * PAIRS * P, WKV, WKV), ("psi", 3 * PAIRS * P, WKV, WKV),
    ("ry", QTOK, WKV, WKV), ("y", QTOK, WKV, GATES),
    ("orw", QTOK, GATES, MERGE), ("gates", 16 * SEQ, GATES, POST1),
    ("mo", NT * D, POST1, POST1), ("xn1", NT * D, POST1, FFN), ("fpost", D, FFN, DOWN),
    ("fT", KF * SEQ, FFN, DOWN), ("sil", 2 * SEQ, FFN, FFN), ("dno", NT * D, DOWN, DOWN),
    ("xn2", NT * D, DOWN, PROJ2),
    ("u", NT * POOL, PROJ2, SCAN), ("sz", NT * SSD, PROJ2, MIXED), ("xraw", MX * SEQ, PROJ2, CONV),
    ("xs", MX * SEQ, PROJ2, SCAN), ("band", GRP * (SEQ + P), PROJ2, CONV), ("wp", P, PROJ2, SCAN),
    ("dif", 2 * SEQ, CONV, SCAN), ("dt", 32, CONV, SCAN), ("dtmp", 32, CONV, SCAN), ("da", 32, CONV, SCAN),
    ("acs", 48, CONV, SCAN), ("ea", 32, CONV, SCAN),
    ("dec", NT * SH * P, SCAN, SCAN), ("cbm", NT * GRP * P, SCAN, SCAN), ("xtok", NT * SSD, SCAN, SCAN),
    ("btk", GRP * P, SCAN, SCAN), ("xc", NT * SSD, SCAN, SCAN), ("xde", SSD, SCAN, SCAN), ("st", SSD, SCAN, SCAN),
    ("yo", SSD, SCAN, SCAN), ("ys", NT * SSD, SCAN, MIXED), ("ysq", NT * SSD, SCAN, MIXED),
    ("mixT", KD * SEQ, CONV, MIXED), ("gtmp", 512, MIXED, MOE),
    ("xn3", NT * D, MIXED, MOE), ("ew", 3 * SLOT, MOE, MOE), ("sa", 2 * EF, MOE, MOE), ("ac", 2 * EF, MOE, MOE),
    ("acT", 2 * EF, MOE, MOE), ("lg", NT * 36, MOE, MOE), ("rt", 8 * 64, MOE, MOE), ("gate", 64, MOE, MOE),
    ("rs", 64, MOE, MOE), ("fin", D, MOE, MOE),
]


def place(limit):
    at = {}
    spans = []
    for name, w, first, last in sorted(BUFFERS, key=lambda b: (b[2] - b[3], -b[1])):
        near = sorted((a, a + x) for a, x, f, l in spans if f <= last and first <= l)
        pos = 0
        for a, b in near:
            if pos + w <= a:
                break
            pos = max(pos, b)
        assert pos + w <= limit, (name, pos + w, limit)
        spans.append((pos, w, first, last))
        at[name] = (pos, pos + w)
    return at


def build(nc, A, out):
    BANK = plan_banks()
    ctx = ExitStack()
    with ctx:
        sems = {}

        def S(name):
            if name not in sems:
                sems[name] = ctx.enter_context(nc.semaphore(name))
            return sems[name]

        def sb(name, shape, dt=F32):
            return ctx.enter_context(nc.sbuf_tensor(name, shape, dt))

        con = sb("con", [P, NCONST])
        lvl = sb("lvl", [P, 2 * LEVELS * P], U8)
        parcol = sb("parcol", [P, NPAR, P])
        xres = sb("xres", [P, NT, D])
        hT = sb("hT", [P, KD, SEQ])
        small = sb("small", [P, 600])
        ring = sb("ring", [P, RING, SLOT])
        words = nc.sbuf_bytes_remaining // 4 - 64
        arena = sb("arena", [P, words])
        where = place(words)
        bank = [ctx.enter_context(nc.psum_tensor(f"bank{b}", [P, 512], F32)) for b in range(8)]
        bank_full = [S(f"bank_full{b}") for b in range(8)]
        bank_free = [S(f"bank_free{b}") for b in range(8)]

        def K(name):
            a, b = CONST[name]
            return con[:, a:b]

        def par(name, n=0, w=1):
            t, at, _ = PARCOL[name]
            return parcol[:, t, at + n:at + n + w]

        def lmask(lv, turned):
            m = lvl[:, (turned * LEVELS + lv) * P:(turned * LEVELS + lv + 1) * P]
            return m.unsqueeze(1).to_broadcast([P, 4, P])

        at = [0]

        def tiny(w):
            at[0] += w
            assert at[0] <= 600
            return small[:, at[0] - w:at[0]]

        ss, ms, sd, rstd = ([tiny(4) for _ in range(7)] for _ in range(4))
        omu, total, pc, modc = tiny(14), tiny(16), tiny(16), tiny(48)
        wgr = tiny(KD * 36).rearrange("p (k e) -> p k e", k=KD)
        rbias, dtb, alog, dsk, csil = tiny(36), tiny(SH), tiny(SH), tiny(SH), tiny(KD)
        gss, gms = tiny(8), tiny(8)

        def B(name, *dims):
            a, b = where[name]
            ap = arena[:, a:b]
            if len(dims) == 1:
                return ap.rearrange("p (a b) -> p a b", a=dims[0])
            if len(dims) == 2:
                return ap.rearrange("p (a b c) -> p a b c", a=dims[0], b=dims[1])
            if len(dims) == 3:
                return ap.rearrange("p (a b c d) -> p a b c d", a=dims[0], b=dims[1], c=dims[2])
            return ap

        junk, parrow, cb = B("junk"), B("parrow", NPAR), B("cb", KD)
        g1, g2, wua, gup, npost, fpost, fin = (B(n) for n in ("g1", "g2", "wua", "gup", "npost", "fpost", "fin"))
        xn = [B(f"xn{n}", NT) for n in range(4)]
        osb, gT, bon, tmp, bh, kh, kT, vT, bT = (B(n, 4) for n in ("osb", "gT", "bon", "tmp", "bh", "kh", "kT", "vT", "b"))
        rT, lora, aT, lw, kkT, cum, qk, vtok = (B(n, d) for n, d in (
            ("rT", 4), ("lora", 2), ("a", 4), ("lw", 4), ("kk", 4), ("cum", 4), ("qk", 8), ("v", NT)))
        nmr = B("nmr")
        kr = B("kr", PAIRS, NT, 2)
        az, rz = B("az", HEADS), B("rz", HEADS)
        vp, zb = B("vp", NT, HEADS), B("zb", NT, HEADS)
        btok, ktok, modp = B("btok", NT), B("ktok", NT), B("modp", 2)
        gm, dd, ddT, xx, up, tk = (B(n, HEADS) for n in ("gm", "dd", "ddT", "xx", "up", "tk"))
        phi, psi = B("phi", 2, PAIRS), B("psi", 3, PAIRS)
        ryT, yT, orw, gates = B("ry", PAIRS), B("y", PAIRS), B("orw", PAIRS), B("gates", 16)
        mo, dno, fT, sil = B("mo", NT), B("dno", NT), B("fT", KF), B("sil", 2)
        u, sz, xraw, xs, band = B("u", NT), B("sz", NT), B("xraw", MX), B("xs", MX), B("band", GRP)
        wp, dif = B("wp", 2), B("dif", 2)
        dtr, dtmp, da = (B(n, NT)[:, :, 0:SH] for n in ("dt", "dtmp", "da"))
        acs, ea = B("acs", 3), B("ea", 2)
        dec, cbm = B("dec", NT, SH), B("cbm", NT, GRP)
        xtok, btk, xc, xde, st, yo = B("xtok", NT), B("btk"), B("xc", NT), B("xde"), B("st"), B("yo")
        ys, ysq, mixT, gtmp = B("ys", NT), B("ysq", NT), B("mixT", KD), B("gtmp")
        ew = B("ew", 3)
        sa, ac, acT = B("sa", NT), B("ac", NT), B("acT", NT, KE)
        lg, gate, rs = B("lg", NT), B("gate", NT), B("rs")
        rtb = [B("rt", 8)[:, n] for n in range(8)]

        def write(pe, key):
            b, turn = BANK[key]
            if turn:
                pe.wait_ge(bank_free[b], turn)
            return bank[b]

        def full(key):
            return bank_full[BANK[key][0]], 1

        def filled(eng, key):
            b, turn = BANK[key]
            eng.wait_ge(bank_full[b], turn + 1)
            return bank[b]

        def free(key):
            return bank_free[BANK[key][0]], 1

        def drained(eng, key):
            b, turn = BANK[key]
            eng.wait_ge(bank_free[b], turn + 1)

        def cols(w, c0, c1):
            return w[:, c0:c1].rearrange("(k p) c -> p k c", p=P)

        w_in, w_in2 = A["w_in"][0], A["w_in_2"][0]
        W = []

        def stream(key, parts, last):
            W.append((key, parts, last))

        for c in (3, 1, 0, 2):
            a, b = SB_COLS + c * 512, min(SB_COLS + c * 512 + 512, SB_COLS + RW_COLS)
            stream(("rw", c), [(0, cols(w_in, a, b))], ("rw", min(2 * c + 1, 6)))
        for c, last in enumerate((("qk", 1), ("qk", 3), ("v", 1))):
            stream(("sb", c), [(0, cols(w_in, c * 512, c * 512 + 512))], last)
        for c in range(12):
            stream(("ada", c), [(0, cols(A["w_ada_2"][0], c * 512, c * 512 + 512))], ("ad", c))
        for c in range(4):
            a = SB_COLS + RW_COLS + c * 512
            stream(("gate", c), [(0, cols(w_in, a, a + 512))], ("ga", 2 * c + 1))
        stream("sb_out", [(0, cols(A["w_sb_out"][0], 0, D))], ("mg", KD - 1))
        stream("rw_out", [(0, cols(A["w_rw_out"][0], 0, D))], ("mg", KD - 1))
        for n in range(2):
            stream(("wo", n), [(0, cols(A["w_o"][0], n * 512, n * 512 + 512))], ("mo", 1, n))
        for c in range(KF // 2):
            stream(("ff", c), [(0, cols(A["w_ffn_gate"][0], c * 256, c * 256 + 256)),
                               (2048, cols(A["w_ffn_up"][0], c * 256, c * 256 + 256))], ("ff", 2 * c + 1))
        n_down = -(-KF // 4)
        for c in range(n_down):
            r0, r1 = c * 512, min(c * 512 + 512, FF)
            stream(("down", c), [(0, cols(A["w_ffn_down"][0][r0:r1, :], 0, D))],
                   ("dn", 1, 1) if c == n_down - 1 else ("sem", "down_used", c + 1))
        for c in range(6):
            stream(("in2", c), [(0, cols(w_in2, c * 512, min(c * 512 + 512, w_in2.shape[1])))],
                   ("uz", 1, c) if c < 2 else ("xb", 2 * c - 3) if c < 5 else ("dt2",))
        for n in range(2):
            stream(("out2", n), [(0, cols(A["w_out_2"][0], n * 512, n * 512 + 512))], ("mx", 1, n))
        slot_full = [S(f"slot_full{r}") for r in range(RING)]
        SLOTS, loads = {}, [0] * RING
        for n, (key, parts, last) in enumerate(W):
            loads[n % RING] += 16 * len(parts)
            SLOTS[key] = (n % RING, loads[n % RING])

        def slot_view(key, k):
            r = SLOTS[key][0]
            parts = [p for q, p, _ in W if q == key][0]
            w = parts[0][1].shape[2]
            return ring[:, r, 0:k * w].rearrange("p (k c) -> p k c", k=k)

        def arrived(eng, key):
            r, count = SLOTS[key]
            eng.wait_ge(slot_full[r], count)

        GD, GE = EXPERTS // 2, 2
        w13_full = [S(f"w13_full{s}") for s in range(2)]
        w2_full = [S(f"w2_full{s}") for s in range(2)]
        base = ring[:, :, :].rearrange("p r w -> p (r w)")
        other = ew.rearrange("p r w -> p (r w)")
        w13s = [x[:, 0:2 * SLOT].rearrange("p (k c) -> p k c", k=KD) for x in (base, other)]
        w2s = [x[:, 2 * SLOT:3 * SLOT].rearrange("p (k c) -> p k c", k=KE) for x in (base, other)]
        w13_d = A["w13_2"][0].rearrange("e (k p) c -> p e k c", p=P)
        w2_d = A["w2_2"][0].rearrange("e (k p) c -> p e k c", p=P)
        x_tok = A["x"][0].rearrange("(i p) d -> p i d", p=P)
        out_tok = out[0].rearrange("(i p) d -> p i d", p=P)

        block = ctx.enter_context(nc.Block())

        @block.sync
        def _(sp):
            sp.dma_start(xres[:, :, :], x_tok).then_inc(S("x_in"), 16)
            sp.dma_start(con[:, :], A["consts"]).then_inc(S("con_in"), 16)
            for t, rows in enumerate(PAR):
                a = 0
                for name, r in rows:
                    src = A[name].rearrange("x y z -> (x y z)") if len(A[name].shape) == 3 else \
                        A[name].rearrange("x y -> (x y)")
                    sp.dma_start(parrow[a:a + r, t, :], src.rearrange("(r c) -> r c", c=P)).then_inc(S("par_in"), 16)
                    a += r
            freed_by = {}
            for n, (key, parts, last) in enumerate(W):
                r = n % RING
                if r in freed_by:
                    was = freed_by[r]
                    if was[0] == "sem":
                        sp.wait_ge(S(was[1]), was[2])
                    else:
                        filled(sp, was)
                for c0, src in parts:
                    k, w = src.shape[1], src.shape[2]
                    dst = ring[:, r, c0:c0 + k * w].rearrange("p (k c) -> p k c", k=k)
                    sp.dma_start(dst, src).then_inc(slot_full[r], 16)
                freed_by[r] = last

            def expert(s, e, e1):
                for h in range(2):
                    sp.dma_start(w13s[s][:, 4 * h:4 * h + 4, :], w13_d[:, e:e1, 4 * h:4 * h + 4, :]
                                 if isinstance(e, int) else
                                 w13_d[:, bass.ds(e, 1), 4 * h:4 * h + 4, :].rearrange("p e k c -> p (e k) c")
                                 ).then_inc(w13_full[s], 16)
                sp.dma_start(w2s[s], w2_d[:, bass.ds(e, 1), :, :].rearrange("p e k c -> p (e k) c")
                             ).then_inc(w2_full[s], 16)

            for r in range(RING):
                was = freed_by[r]
                filled(sp, was)

            def load(s, e):
                for h in range(2):
                    sp.dma_start(w13s[s][:, 4 * h:4 * h + 4, :],
                                 w13_d[:, bass.ds(e, 1), 4 * h:4 * h + 4, :].rearrange("p e k c -> p (e k) c")
                                 ).then_inc(w13_full[s], 16)
                sp.dma_start(w2s[s], w2_d[:, bass.ds(e, 1), :, :].rearrange("p e k c -> p (e k) c")
                             ).then_inc(w2_full[s], 16)

            sp.wait_ge(S("x_new"), 6)
            for s in range(2):
                load(s, s)
            with sp.Fori(0, EXPERTS // 2 - 1) as it:
                for s in range(2):
                    sp.wait_ge(S(f"expert_done{s}"), it + 1)
                    load(s, it * 2 + (2 + s))
            sp.wait_ge(S("y_out"), NT)
            sp.dma_start(out_tok, xres[:, :, :]).then_inc(S("stored"), 16)
            sp.wait_ge(S("stored"), 16)

        @block.tensor
        def _(pe):
            mm = nc.tensor.matmul
            ident = K("ident")

            def norm_transposes(s):
                for kk in range(4):
                    ps = write(pe, ("hT", s, kk))
                    for k2 in range(2):
                        for i in range(NT):
                            if kk == 0 and k2 == 0:
                                pe.wait_ge(S("xn"), 2 * s + i + 1)
                            k = 2 * kk + k2
                            last = nc.tensor.transpose(ps[:, (k2 * NT + i) * P:(k2 * NT + i + 1) * P],
                                                       xn[s][:, i, k * P:(k + 1) * P], ident)
                    last.then_inc(*full(("hT", s, kk)))

            def normed(s):
                for kk in range(4):
                    drained(pe, ("hT", s, kk))

            def feature_major(key, wkey, m0, m_in_slot):
                ps = write(pe, key)
                w = slot_view(wkey, KD)
                for j in range(2):
                    for k in range(KD):
                        c = (m_in_slot + j) * P
                        last = mm(ps[:, j * SEQ:(j + 1) * SEQ], w[:, k, c:c + P], hT[:, k, :],
                                  start=(k == 0), stop=(k == KD - 1))
                last.then_inc(*full(key))

            def token_major(key, wkey, i, lhs, nk=KD):
                ps = write(pe, key)
                w = slot_view(wkey, nk)
                for k in range(nk):
                    last = mm(ps[:, 0:512], lhs[:, k, i * P:(i + 1) * P], w[:, k, 0:512],
                              start=(k == 0), stop=(k == nk - 1))
                last.then_inc(*full(key))

            pe.wait_ge(S("con_in"), 16)
            pe.wait_ge(S("par_in"), 16 * sum(len(x) for x in PAR))
            for t, rows in enumerate(PAR):
                n = sum(r for _, r in rows)
                ps = write(pe, ("par", t))
                nc.tensor.transpose(ps[:, 0:n], parrow[0:n, t, :], ident[0:n, 0:n]).then_inc(*full(("par", t)))

            norm_transposes(0)
            normed(0)
            for j in RW_ORDER:
                c = j // 2
                arrived(pe, ("rw", c))
                feature_major(("rw", j), ("rw", c), 2 * j, 2 * (j % 2) if c < 3 else 0)
            pe.wait_ge(S("small_in"), 16 * 3)
            for key, lo, hi, part, wt in (("lw", 0, 64, 0, wua), ("la", 64, 128, 0, wua), ("lg", 0, 128, 1, gup)):
                if key == "la":
                    drained(pe, ("rw", 6))
                else:
                    pe.wait_ge(S("lora"), 1 + part)
                for j in range(2):
                    ps = write(pe, (key, j))
                    for h in range(2):
                        mt = 2 * j + h
                        last = mm(ps[:, h * SEQ:(h + 1) * SEQ], wt[lo:hi, mt * P:(mt + 1) * P], lora[lo:hi, part, :],
                                  start=True, stop=True)
                    last.then_inc(*full((key, j)))
            for j in range(4):
                arrived(pe, ("sb", j // 2))
                feature_major(("qk", j), ("sb", j // 2), 2 * j, 2 * (j % 2))
            arrived(pe, ("sb", 2))
            for i in range(NT):
                token_major(("v", i), ("sb", 2), i, hT)
            pe.wait_ge(S("kk_sq"), 1)
            ps = write(pe, ("kn",))
            for p in range(PAIRS):
                last = mm(ps[0:HEADS, 0:SEQ], K("head_sum")[:, p * HEADS:(p + 1) * HEADS], tmp[:, p, :],
                          start=(p == 0), stop=(p == PAIRS - 1))
            last.then_inc(*full(("kn",)))

            def spread(name, sem):
                pe.wait_ge(S(sem), 1)
                for j in range(2):
                    ps = write(pe, (name, j))
                    for h in range(2):
                        p = 2 * j + h
                        last = mm(ps[:, h * SEQ:(h + 1) * SEQ], K("head_spread")[0:HEADS, p * P:(p + 1) * P],
                                  nmr[0:HEADS, :], start=True, stop=True)
                    last.then_inc(*full((name, j)))

            spread("kb", "kk_inv")

            def scores(ps, h, alone):
                o = DH * (h % 2)
                q, k = qk[o:o + DH, h // 2, :], qk[o:o + DH, PAIRS + h // 2, :]
                mm(ps[:, 0:SEQ], k[:, 0:P], q, start=True, stop=alone, skip_group_check=True)
                return mm(ps[:, SEQ:SEQ + P], k[:, P:SEQ], q[:, P:SEQ], start=alone, stop=alone, skip_group_check=True)

            for j in range(4):
                drained(pe, ("qk", j))
            for h in range(HEADS):
                ps = write(pe, ("z", h))
                scores(ps, h, True).then_inc(*full(("z", h)))
            pe.wait_ge(S("bon_raw"), 1)
            for j in range(2):
                ps = write(pe, ("bn", j))
                for h in range(2):
                    last = mm(ps[:, h * SEQ:(h + 1) * SEQ], K("head_block"), bon[:, 2 * j + h, :], start=True, stop=True)
                last.then_inc(*full(("bn", j)))
            for h in range(HEADS):
                pe.wait_ge(S("att_sp"), h // 4 + 1)
                ps = write(pe, ("l", h))
                scores(ps, h, False)
                mm(ps[:, 0:SEQ], K("neg_suffix"), rz[:, h, 0:SEQ], start=False, stop=False, skip_group_check=True)
                mm(ps[:, P:SEQ], K("neg_ones"), rz[:, h, SEQ:SEQ + P], start=False, stop=False, skip_group_check=True)
                mm(ps[:, SEQ:SEQ + P], K("neg_suffix"), rz[:, h, SEQ:SEQ + P], start=False, stop=True,
                   skip_group_check=True).then_inc(*full(("l", h)))
            for i in range(NT):
                drained(pe, ("v", i))
            for p in range(PAIRS):
                pe.wait_ge(S("att_w"), p // 2 + 1)
                ps = write(pe, ("o", p))
                for h in range(2):
                    d = DH * h
                    n = 2 * p + h
                    mm(ps[d:d + DH, 0:SEQ], vtok[:, 0, n * DH:(n + 1) * DH], az[:, n, 0:SEQ], start=True, stop=False,
                       skip_group_check=True)
                    last = mm(ps[d:d + DH, P:SEQ], vtok[:, 1, n * DH:(n + 1) * DH], az[:, n, SEQ:SEQ + P],
                              start=False, stop=True, skip_group_check=True)
                last.then_inc(*full(("o", p)))

            pe.wait_ge(S("kr_k"), 1)
            pe.wait_ge(S("bk_bar"), 1)
            for i in range(NT):
                for a in range(4):
                    ps = write(pe, ("tok", i, a))
                    for p in range(PAIRS):
                        t = slice(i * P, (i + 1) * P)
                        src = (kr[:, p, i, 0, :], bT[:, p, t], kT[:, p, t], vT[:, p, t])[a]
                        last = nc.tensor.transpose(ps[:, p * P:(p + 1) * P], src, ident)
                    last.then_inc(*full(("tok", i, a)))

            def ada_sum(c):
                drained(pe, ("ad", c))
                ps = write(pe, ("as", c))
                if c in COLUMN_CHUNKS:
                    for j in range(4):
                        last = mm(ps[:, j:j + 1], modp[:, c % 2, j * P:(j + 1) * P], K("thirty_second")[:, 0:1],
                                  start=True, stop=True)
                else:
                    last = mm(ps[:, 0:512], K("thirty_second"), modp[:, c % 2, :], start=True, stop=True)
                last.then_inc(*full(("as", c)))

            def ada(c):
                if c:
                    ada_sum(c - 1)
                arrived(pe, ("ada", c))
                pe.wait_ge(S("cb"), 1)
                ps = write(pe, ("ad", c))
                w = slot_view(("ada", c), KD)
                for kk in range(2):
                    for j in range(4):
                        k = 2 * j + kk
                        last = mm(ps[32 * j:32 * j + 32, 0:512], cb[:, k, :], w[:, k, :], start=(kk == 0),
                                  stop=(kk == 1))
                last.then_inc(*full(("ad", c)))

            pe.wait_ge(S("bk_hat"), 1)
            pe.wait_ge(S("kr_r"), 1)
            chunk = 0
            for i in range(NT):
                for h in range(HEADS):
                    o, p = DH * (h % 2), h // 2
                    ps = write(pe, ("g", i, h))
                    right = kr[o:o + DH, p, i, :, :].rearrange("p s t -> p (s t)")
                    mm(ps[:, 0:2 * P], bh[o:o + DH, p, i * P:(i + 1) * P], right, start=True, stop=True)
                    mm(ps[:, 2 * P:4 * P], kh[o:o + DH, p, i * P:(i + 1) * P], right, start=True,
                       stop=True).then_inc(*full(("g", i, h)))

                def group(key, q, left, right):
                    ps = write(pe, key)
                    for j in range(4):
                        last = mm(ps[:, j * P:(j + 1) * P], left(4 * q + j), right(4 * q + j), start=True, stop=True)
                    last.then_inc(*full(key))

                for q in range(2):
                    for h in range(4):
                        drained(pe, ("g", i, 4 * q + h))
                    group(("n", i, q), q, lambda h: gm[:, h, 0:P], lambda h: ident)
                for lv in range(1, LEVELS):
                    for q in range(2):
                        if lv == 1:
                            drained(pe, ("n", i, q))
                            pe.wait_ge(S("dt_first"), 2 * i + q + 1)
                        else:
                            drained(pe, ("d", i, lv - 1, q))
                            drained(pe, ("dt", i, lv - 1, q))
                        group(("x", i, lv, q), q, lambda h: gm[:, h, 0:P], lambda h: dd[:, h, :])
                    ada(chunk)
                    chunk += 1
                    for q in range(2):
                        drained(pe, ("x", i, lv, q))
                        if lv < LEVELS - 1:
                            group(("d", i, lv, q), q, lambda h: ddT[:, h, :], lambda h: xx[:, h, :])
                        group(("dt", i, lv, q), q, lambda h: xx[:, h, :], lambda h: ddT[:, h, :])
                for a in range(4):
                    drained(pe, ("tok", i, a))
                for q in range(2):
                    group(("w1", i, q), q, lambda h: gm[:, h, 2 * P:3 * P], lambda h: vp[:, i, h, :])
                ada(chunk)
                chunk += 1
                for q in range(2):
                    drained(pe, ("w1", i, q))
                    drained(pe, ("dt", i, LEVELS - 1, q))
                    group(("u", i, q), q, lambda h: ddT[:, h, :], lambda h: zb[:, i, h, :])
                for q in range(2):
                    drained(pe, ("u", i, q))
                ps = write(pe, ("ry", i))
                for h in range(HEADS):
                    o, p = DH * (h % 2), h // 2
                    last = mm(ps[o:o + DH, p * P:(p + 1) * P], tk[:, h, :], gm[:, h, P:2 * P], start=True, stop=True)
                last.then_inc(*full(("ry", i)))

                def psi_of(c):
                    r = slice(CH * (c % 2), CH * (c % 2) + CH)
                    ps = write(pe, ("psi", c))
                    for p in range(PAIRS):
                        f = slice(p * P, (p + 1) * P)
                        mm(ps[:, f], btok[r, i, f], up[r, 2 * p:2 * p + 2, :].rearrange("p h d -> p (h d)"),
                           start=True, stop=False)
                        last = mm(ps[:, f], ktok[r, i, f], vp[r, i, 2 * p:2 * p + 2, 0:DH], start=False, stop=True)
                    last.then_inc(*full(("psi", c)))

                def phi_of(c):
                    r = slice(CH * (c % 2), CH * (c % 2) + CH)
                    ps = write(pe, ("phi", c))
                    for p in range(PAIRS):
                        f = slice(p * P, (p + 1) * P)
                        last = mm(ps[:, f], tk[r, 2 * p:2 * p + 2, :].rearrange("p h d -> p (h d)"), btok[r, i, f],
                                  start=True, stop=True)
                    last.then_inc(*full(("phi", c)))

                def state(c):
                    drained(pe, ("s", c - 1) if c > 1 else ("psi", 0))
                    drained(pe, ("psi", c))
                    pe.wait_ge(S("phi"), c)
                    ps = write(pe, ("s", c))
                    for p in range(PAIRS):
                        last = mm(ps[:, p * P:(p + 1) * P], phi[:, c - 1, p, :], psi[:, c - 1, p, :], start=True, stop=True)
                    last.then_inc(*full(("s", c)))

                def y_of():
                    ps = write(pe, ("y", i))
                    for h in range(HEADS):
                        o, p = DH * (h % 2), h // 2
                        dst = ps[o:o + DH, p * P:(p + 1) * P]
                        mm(dst, up[:, h, :], gm[:, h, P:2 * P], start=(p == 0), stop=False, skip_group_check=True)
                        mm(dst, vp[:, i, h, 0:DH], gm[:, h, 3 * P:4 * P], start=False, stop=False, skip_group_check=True)
                    drained(pe, ("ry", i))
                    for c in (2 * i, 2 * i + 1):
                        if c == 0:
                            continue
                        drained(pe, ("psi", 0) if c == 1 else ("s", c - 1))
                        for p in range(PAIRS):
                            t = slice(p * P + CH * (c % 2), p * P + CH * (c % 2) + CH)
                            last = mm(ps[:, t], psi[:, c - 1, p, :], ryT[:, p, c * CH:(c + 1) * CH], start=False,
                                      stop=True, skip_group_check=True)
                    last.then_inc(*full(("y", i)))

                if i == 0:
                    psi_of(0)
                    psi_of(1)
                    phi_of(1)
                    y_of()
                    state(1)
                else:
                    psi_of(2)
                    phi_of(2)
                    state(2)
                    y_of()
            ada_sum(11)

            def gates_of(j):
                arrived(pe, ("gate", j // 2))
                feature_major(("ga", j), ("gate", j // 2), 2 * j, 2 * (j % 2))

            gates_of(0)
            gates_of(1)
            for i in range(NT):
                drained(pe, ("y", i))
            for j in range(2):
                ps = write(pe, ("m", j))
                for h in range(2):
                    last = mm(ps[:, h * SEQ:(h + 1) * SEQ], K("head_mean"), yT[:, 2 * j + h, :], start=True, stop=True)
                last.then_inc(*full(("m", j)))
            for j in range(2, 5):
                gates_of(j)
            pe.wait_ge(S("y_sq"), 1)
            ps = write(pe, ("vn",))
            for p in range(PAIRS):
                last = mm(ps[0:HEADS, 0:SEQ], K("head_sum")[:, p * HEADS:(p + 1) * HEADS], tmp[:, p, :],
                          start=(p == 0), stop=(p == PAIRS - 1))
            last.then_inc(*full(("vn",)))
            for j in range(5, 8):
                gates_of(j)
            spread("vb", "y_inv")
            arrived(pe, "sb_out")
            arrived(pe, "rw_out")
            for p in range(PAIRS):
                drained(pe, ("o", p))
            pe.wait_ge(S("orw"), 1)
            for dm in range(KD):
                ps = write(pe, ("mg", dm))
                for half, wkey, src in ((0, "sb_out", osb), (1, "rw_out", orw)):
                    w = slot_view(wkey, PAIRS)
                    for k in range(PAIRS):
                        last = mm(ps[:, half * SEQ:(half + 1) * SEQ], w[:, k, dm * P:(dm + 1) * P], src[:, k, :],
                                  start=(k == 0), stop=(k == PAIRS - 1))
                last.then_inc(*full(("mg", dm)))
            pe.wait_ge(S("merged"), KD)
            for n in range(2):
                arrived(pe, ("wo", n))
                for i in range(NT):
                    token_major(("mo", i, n), ("wo", n), i, gates)
            norm_transposes(1)
            normed(1)
            for f in range(KF):
                c = f // 2
                arrived(pe, ("ff", c))
                ps = write(pe, ("ff", f))
                w = ring[:, SLOTS[("ff", c)][0], :].rearrange("p (g k c) -> p g k c", g=2, k=KD)
                for gu in range(2):
                    for k in range(KD):
                        last = mm(ps[:, gu * SEQ:(gu + 1) * SEQ], w[:, gu, k, (f % 2) * P:(f % 2 + 1) * P], hT[:, k, :],
                                  start=(k == 0), stop=(k == KD - 1))
                last.then_inc(*full(("ff", f)))
            ps = {}
            for n in range(2):
                for i in range(NT):
                    ps[i, n] = write(pe, ("dn", i, n))
            for c in range(n_down):
                arrived(pe, ("down", c))
                nk = min(4, KF - 4 * c)
                w = slot_view(("down", c), nk)
                for kk in range(nk):
                    k = 4 * c + kk
                    drained(pe, ("ff", k))
                    for n in range(2):
                        for i in range(NT):
                            last = mm(ps[i, n][:, 0:512], fT[:, k, i * P:(i + 1) * P], w[:, kk, n * 512:(n + 1) * 512],
                                      start=(k == 0), stop=(k == KF - 1))
                            if k == KF - 1:
                                last.then_inc(*full(("dn", i, n)))
                if c < n_down - 1:
                    last.then_inc(S("down_used"), 1)

            norm_transposes(2)
            normed(2)
            for n in range(2):
                arrived(pe, ("in2", n))
                for i in range(NT):
                    token_major(("uz", i, n), ("in2", n), i, hT)
            for j in range(7):
                c = 2 + j // 2
                arrived(pe, ("in2", c))
                feature_major(("xb", j), ("in2", c), 2 * j, 2 * (j % 2))
            w = slot_view(("in2", 5), KD)
            ps = write(pe, ("dt2",))
            for i in range(NT):
                for k in range(KD):
                    last = mm(ps[:, i * 16:i * 16 + SH], hT[:, k, i * P:(i + 1) * P], w[:, k, 256:256 + SH],
                              start=(k == 0), stop=(k == KD - 1))
            last.then_inc(*full(("dt2",)))
            pe.wait_ge(S("pool_in"), 16 * 5)
            for i in range(NT):
                drained(pe, ("uz", i, 0))
            ps = write(pe, ("pl",))
            for g in range(GRP):
                o, c0 = 64 * (g % 2), SEQ * (g // 2)
                mm(ps[o:o + 64, c0:c0 + SEQ], u[:, 0, g * 64:(g + 1) * 64], band[:, g, 0:SEQ], start=(g < 2), stop=False,
                   skip_group_check=True)
                last = mm(ps[o:o + 64, c0 + P:c0 + SEQ], u[:, 1, g * 64:(g + 1) * 64], band[:, g, SEQ:SEQ + P],
                          start=False, stop=True, skip_group_check=True)
            last.then_inc(*full(("pl",)))
            pe.wait_ge(S("da"), 1)
            ps = write(pe, ("cs",))
            for i in range(NT):
                mm(ps[:, i * 16:i * 16 + SH], K("causal"), da[:, i, :], start=True, stop=True)
            mm(ps[:, 32:32 + SH], K("after"), da[:, 0, :], start=True, stop=True).then_inc(*full(("cs",)))
            drained(pe, ("pl",))
            ps = write(pe, ("pm",))
            for g in range(GRP):
                o, c0 = 64 * (g % 2), SEQ * (g // 2)
                last = mm(ps[o:o + 64, c0:c0 + SEQ], wp[o:o + 64, g // 2, :], dif[o:o + 64, g // 2, :], start=True,
                          stop=True)
            last.then_inc(*full(("pm",)))
            for i in range(NT):
                for q in range(3):
                    ps = write(pe, ("rb", i, q))
                    for j in range(4):
                        last = mm(ps[:, j * P:(j + 1) * P], da[:, i, 4 * q + j:4 * q + j + 1].to_broadcast([P, P]),
                                  K("causal"), start=True, stop=True)
                    last.then_inc(*full(("rb", i, q)))
            pe.wait_ge(S("xs"), 7)
            for i in range(NT):
                ps = write(pe, ("cb", i))
                for g in range(GRP):
                    t = slice(i * P, (i + 1) * P)
                    last = mm(ps[:, g * P:(g + 1) * P], xs[:, 6 + g, t], xs[:, 10 + g, t], start=True, stop=True)
                last.then_inc(*full(("cb", i)))

            def transposes(key, pairs):
                ps = write(pe, key)
                for c, src in pairs:
                    last = nc.tensor.transpose(ps[:, c * P:(c + 1) * P], src, ident)
                last.then_inc(*full(key))

            for i in range(NT):
                for a in range(2):
                    transposes(("xt", i, a), [(c, xs[:, 4 * a + c, i * P:(i + 1) * P]) for c in range(4 if a == 0 else 2)])
            transposes(("bt",), [(g, xs[:, 6 + g, 0:P]) for g in range(GRP)])

            def y_diag(i):
                pe.wait_ge(S("dec"), i + 1)
                pe.wait_ge(S("xc"), i + 1)
                for a in range(2):
                    ps = write(pe, ("yd", i, a))
                    for h in range(8 * a, min(8 * a + 8, SH)):
                        c = (h - 8 * a) * DH
                        last = mm(ps[:, c:c + DH], dec[:, i, h, :], xc[:, i, h * DH:(h + 1) * DH], start=True, stop=True)
                    last.then_inc(*full(("yd", i, a)))

            GW = SR * DH
            y_diag(0)
            pe.wait_ge(S("xde"), 1)
            drained(pe, ("bt",))
            for a in range(2):
                ps = write(pe, ("cst", a))
                for g in range(2 * a, 2 * a + 2):
                    c = (g - 2 * a) * GW
                    last = mm(ps[:, c:c + GW], btk[:, g * P:(g + 1) * P], xde[:, g * GW:(g + 1) * GW], start=True, stop=True)
                last.then_inc(*full(("cst", a)))
            y_diag(1)
            for a in range(2):
                drained(pe, ("cst", a))
                ps = write(pe, ("yo", a))
                for g in range(2 * a, 2 * a + 2):
                    c = (g - 2 * a) * GW
                    last = mm(ps[:, c:c + GW], xs[:, 10 + g, P:SEQ], st[:, g * GW:(g + 1) * GW], start=True, stop=True)
                last.then_inc(*full(("yo", a)))
            for i in range(NT):
                pe.wait_ge(S("ys"), i + 1)
                for a in range(2):
                    transposes(("mt", i, a), [(c, ys[:, i, (4 * a + c) * P:(4 * a + c + 1) * P])
                                              for c in range(4 if a == 0 else 2)])
            drained(pe, ("pm",))
            for i in range(NT):
                for a in range(2):
                    drained(pe, ("mt", i, a))
            for n in range(2):
                arrived(pe, ("out2", n))
                for i in range(NT):
                    token_major(("mx", i, n), ("out2", n), i, mixT)
            norm_transposes(3)
            normed(3)
            pe.wait_ge(S("router_in"), 16 * 4)
            ps = write(pe, ("rt",))
            for i in range(NT):
                for k in range(KD):
                    last = mm(ps[:, i * 64:i * 64 + 36], hT[:, k, i * P:(i + 1) * P], wgr[:, k, :], start=(k == 0),
                              stop=(k == KD - 1))
            last.then_inc(*full(("rt",)))

            for b in range(8):
                uses = max(t for bb, t in BANK.values() if bb == b) + 1
                pe.wait_ge(bank_free[b], uses)
            pe.wait_ge(S("zero"), 1)
            for b in range(4):
                mm(bank[b][:, 0:512], rs[0:1, 0:1].to_broadcast([1, P]), junk[0:1, 0:512], start=True, stop=False,
                   skip_group_check=True)
            with pe.Fori(0, EXPERTS // 2) as it:
                for s in range(2):
                    pe.wait_ge(w13_full[s], it * 32 + 32)
                    for i in range(NT):
                        pe.wait_ge(S("act_out"), it * 4 + (2 * s + i))
                        if i == 0:
                            pass
                        for half in range(2):
                            b = bank[4 + 2 * i + half]
                            if half == 0:
                                pe.wait_ge(S(f"turned{i}"), it * 2 + s)
                            for k in range(KD):
                                last = mm(b[:, 0:512], hT[:, k, i * P:(i + 1) * P], w13s[s][:, k, half * EF:(half + 1) * EF],
                                          start=(k == 0), stop=(k == KD - 1))
                            last.then_inc(S("hidden"), 1)
                    for i in range(NT):
                        pe.wait_ge(S("act_out"), it * 4 + (2 * s + i + 1))
                        for f in range(KE):
                            last = nc.tensor.transpose(bank[4 + 2 * i][:, f * P:(f + 1) * P], ac[:, i, f * P:(f + 1) * P],
                                                       ident)
                        last.then_inc(S("turns"), 1)
                    pe.wait_ge(w2_full[s], it * 16 + 16)
                    for i in range(NT):
                        pe.wait_ge(S(f"turned{i}"), it * 2 + (s + 1))
                        for n in range(2):
                            for f in range(KE):
                                last = mm(bank[2 * i + n][:, 0:512], acT[:, i, f, :], w2s[s][:, f, n * 512:(n + 1) * 512],
                                          start=False, stop=False, skip_group_check=True)
                    last.then_inc(S(f"expert_done{s}"), 1)

        @block.scalar
        def _(act):
            A_ = nc.scalar.activation

            def bcast(dst, src, n):
                return act.dma_start(dst, src.partition_broadcast(P)).then_inc(S(n), 16)

            act.dma_start(B("lvlf"), A["levels"]).then_inc(S("lvl_in"), 16)
            act.dma_start(wua[0:64, :], A["w_up"][0]).then_inc(S("small_in"), 16)
            act.dma_start(wua[64:128, :], A["a_up"][0]).then_inc(S("small_in"), 16)
            act.dma_start(gup[:, :], A["g_up"][0]).then_inc(S("small_in"), 16)
            bcast(g1, A["b_ada_2"][0, 2 * D:3 * D], "gate_in")
            bcast(g2, A["b_ada_2"][0, 5 * D:6 * D], "gate_in")
            bcast(dtb, A["dt_bias_2"][0], "router_in")
            act.dma_start(wgr[:, :, 0:EG], A["w_group_2"][0].rearrange("(k p) c -> p k c", p=P)).then_inc(S("router_in"), 16)
            act.dma_start(wgr[:, :, EG:36], A["w_router_2"][0].rearrange("(k p) c -> p k c", p=P)).then_inc(S("router_in"), 16)
            bcast(rbias[:, 0:EG], A["b_group_2"][0], "router_in")
            bcast(rbias[:, EG:36], A["b_router_2"][0], "par2_in")
            bcast(alog, A["a_log_2"][0], "par2_in")
            bcast(dsk, A["d_skip_2"][0], "par2_in")

            squares = [0]

            def next_square():
                if squares[0]:
                    act.wait_ge(S("sq"), squares[0])
                squares[0] += 1

            def pre_norm(n, ready):
                for i in range(NT):
                    ready(i)
                    next_square()
                    A_(junk, xres[:, i, :], ACT.Square, accum_out=ss[n][:, i:i + 1]).then_inc(S("sq"), 1)

            def root(n):
                act.wait_ge(S("ms"), n + 1)
                A_(sd[n][:, 0:NT], ms[n][:, 0:NT], ACT.Sqrt).then_inc(S("sd"), 1)

            def transposed(s, scale, bias):
                for kk in (0, 2):
                    ps = filled(act, ("hT", s, kk))
                    for k2 in range(2):
                        k = 2 * kk + k2
                        kw = {"bias": bias(k)} if bias else {}
                        ins = A_(hT[:, k, :], ps[:, k2 * SEQ:(k2 + 1) * SEQ], ACT.Identity, scale=scale(k), **kw)
                    ins.then_inc(*free(("hT", s, kk)))

            def post_norm(n, name):
                for j in range(4):
                    half, i = j // 2, j % 2
                    ps = filled(act, (name, i, half))
                    next_square()
                    A_(junk[:, 0:512], ps[:, :], ACT.Square, accum_out=ss[n][:, 2 * i + half:2 * i + half + 1]
                       ).then_inc(S("sq"), 1)
                root(n)

            pre_norm(0, lambda i: act.wait_ge(S("x_in"), 16))
            root(0)
            drained(act, ("par", 0))
            transposed(0, lambda k: par("norm_mix_pre", k), None)
            drained(act, ("par", 1))
            act.wait_ge(S("omu"), 1)

            def shifted(m):
                if m < 4:
                    return rT[:, m, :]
                if m < 8:
                    return kT[:, m - 4, :]
                return vT[:, m - 8, :] if m < 12 else lora[:, m - 12, :]

            for j in RW_ORDER:
                ps = filled(act, ("rw", j))
                for h in range(2):
                    ins = A_(shifted(2 * j + h), ps[:, h * SEQ:(h + 1) * SEQ], ACT.Identity, scale=omu[:, 2 * j + h:2 * j + h + 1])
                ins.then_inc(S("rw_own"), 1)
            drained(act, ("rw", 6))
            A_(lora[0:64, 0, :], lora[0:64, 0, :], ACT.Tanh).then_inc(S("lora"), 1)
            A_(lora[:, 1, :], lora[:, 1, :], ACT.Sigmoid).then_inc(S("lora"), 1)
            for key, dst, bias in (("lw", lw, "w0"), ("la", aT, "a0")):
                for j in range(2):
                    ps = filled(act, (key, j))
                    for h in range(2):
                        ins = A_(dst[:, 2 * j + h, :], ps[:, h * SEQ:(h + 1) * SEQ], ACT.Sigmoid, bias=par(bias, 2 * j + h))
                    ins.then_inc(*free((key, j)))
            for j in range(2):
                ps = filled(act, ("lg", j))
                A_(gT[:, 2 * j:2 * j + 2, :].rearrange("p a b -> p (a b)"), ps[:, :], ACT.Copy).then_inc(*free(("lg", j)))
            act.wait_ge(S("kk_raw"), 1)
            A_(tmp, kkT, ACT.Square).then_inc(S("kk_sq"), 1)
            for j in range(2):
                ps = filled(act, ("qk", j))
                A_(qk[:, 2 * j:2 * j + 2, :].rearrange("p a b -> p (a b)"), ps[:, :], ACT.Copy, scale=DH ** -0.5
                   ).then_inc(*free(("qk", j)))
            ps = filled(act, ("kn",))
            A_(nmr[0:HEADS, :], ps[0:HEADS, 0:SEQ], ACT.Sqrt).then_inc(*free(("kn",)))
            A_(csil, par("c_2", 0, KD), ACT.Silu).then_inc(S("csil"), 1)
            act.wait_ge(S("ex"), 1)
            A_(aT, cum, ACT.Exp, scale=DECAY).then_inc(S("e_inc"), 1)
            A_(lw, lw, ACT.Exp, scale=DECAY).then_inc(S("e_exc"), 1)
            A_(tmp, cum, ACT.Exp, scale=-DECAY).then_inc(S("e_inv"), 1)
            A_(pc, total, ACT.Exp, scale=DECAY).then_inc(S("pc"), 1)
            for half in range(2):
                for h in range(4):
                    drained(act, ("z", 4 * half + h))
                A_(az[:, 4 * half:4 * half + 4, :], az[:, 4 * half:4 * half + 4, :], ACT.Exp).then_inc(S("att_e"), 1)
            act.wait_ge(S("to_end"), 1)
            A_(cum, cum, ACT.Exp, scale=DECAY).then_inc(S("e_suf"), 1)
            for half in range(2):
                act.wait_ge(S("att_e"), half + 1)
                A_(az[:, 4 * half:4 * half + 4, :], az[:, 4 * half:4 * half + 4, :], ACT.Ln, bias=1.0).then_inc(S("att_ln"), 1)
            for half in range(2):
                for h in range(4):
                    drained(act, ("l", 4 * half + h))
                A_(az[:, 4 * half:4 * half + 4, :], az[:, 4 * half:4 * half + 4, :], ACT.Exp).then_inc(S("att_x"), 1)
            for p in range(PAIRS):
                ps = filled(act, ("o", p))
                A_(osb[:, p, :], ps[:, 0:SEQ], ACT.Copy).then_inc(*free(("o", p)))
            for i in range(NT):
                ps = filled(act, ("tok", i, 0))
                A_(zb[:, i, :, DH:P], ps[:, :].rearrange("p (h d) -> p h d", h=HEADS), ACT.Copy).then_inc(*free(("tok", i, 0)))
                ps = filled(act, ("tok", i, 1))
                A_(btok[:, i, :], ps[:, :], ACT.Copy).then_inc(*free(("tok", i, 1)))

            def ada_rows(c):
                ps = filled(act, ("ad", c))
                A_(modp[:, c % 2, :], ps[:, :], ACT.Copy).then_inc(*free(("ad", c)))

            c = 0
            for i in range(NT):
                for lv in range(1, LEVELS):
                    for q in range(2):
                        ps = filled(act, ("x", i, lv, q))
                        A_(xx[:, 4 * q:4 * q + 4, :], ps[:, :].rearrange("p (h t) -> p h t", h=4), ACT.Copy
                           ).then_inc(*free(("x", i, lv, q)))
                    ada_rows(c)
                    c += 1
                for q in range(2):
                    ps = filled(act, ("w1", i, q))
                    A_(zb[:, i, 4 * q:4 * q + 4, 0:DH], ps[:, :].rearrange("p (h t) -> p h t", h=4)[:, :, 0:DH], ACT.Copy
                       ).then_inc(*free(("w1", i, q)))
                ada_rows(c)
                c += 1
                for q in range(2):
                    ps = filled(act, ("u", i, q))
                    v = ps[:, :].rearrange("p (h t) -> p h t", h=4)
                    A_(up[:, 4 * q:4 * q + 4, :], v[:, :, 0:DH], ACT.Copy)
                    A_(tk[:, 4 * q:4 * q + 4, :], v[:, :, DH:P], ACT.Copy).then_inc(*free(("u", i, q)))
                ps = filled(act, ("y", i))
                A_(yT[:, :, i * P:(i + 1) * P], ps[:, :].rearrange("p (h t) -> p h t", h=4), ACT.Copy).then_inc(*free(("y", i)))

            def gates_of(j):
                ps = filled(act, ("ga", j))
                for h in range(2):
                    ins = A_(gates[:, 2 * j + h, :], ps[:, h * SEQ:(h + 1) * SEQ], ACT.Sigmoid, bias=par("b_gate", 2 * j + h))
                ins.then_inc(*free(("ga", j)))

            gates_of(0)
            gates_of(1)
            for j in range(2):
                drained(act, ("m", j))
            A_(tmp, yT, ACT.Square).then_inc(S("y_sq"), 1)
            for j in range(2, 5):
                gates_of(j)
            for j in range(5, 8):
                gates_of(j)
            drained(act, ("vn",))
            A_(nmr[0:HEADS, :], nmr[0:HEADS, :], ACT.Sqrt).then_inc(S("y_sd"), 1)
            drained(act, ("mg", 0))
            bcast(npost, A["norm_mix_post"][0], "npost_in")
            post_norm(1, "mo")
            pre_norm(2, lambda i: act.wait_ge(S("x_new"), i + 1))
            root(2)
            bcast(fpost, A["norm_ffn_post"][0], "post_in")
            transposed(1, lambda k: par("norm_ffn_pre", k), None)
            for f in range(KF):
                ps = filled(act, ("ff", f))
                if f >= 2:
                    drained(act, ("ff", f - 2))
                A_(sil[:, f % 2, :], ps[:, 0:SEQ], ACT.Silu).then_inc(S("sil"), 1)
            post_norm(3, "dn")
            pre_norm(4, lambda i: act.wait_ge(S("x_new"), 2 + i + 1))
            root(4)
            act.wait_ge(S("mod"), 1)
            act.dma_start(band, A["bands"].rearrange("p (g t) -> p g t", g=GRP)).then_inc(S("pool_in"), 16)
            for g in range(GRP):
                act.dma_start(wp[64 * (g % 2):64 * (g % 2) + 64, g // 2, :], A["w_pool_2"][0, g]).then_inc(S("pool_in"), 16)
            transposed(2, lambda k: modc[:, 8 + k:9 + k], lambda k: modc[:, k:k + 1])
            for n in range(2):
                for i in range(NT):
                    ps = filled(act, ("uz", i, n))
                    if n == 0:
                        A_(u[:, i, :], ps[:, 0:POOL], ACT.Copy)
                        A_(sz[:, i, 0:256], ps[:, POOL:512], ACT.Silu).then_inc(*free(("uz", i, 0)))
                    else:
                        A_(sz[:, i, 256:SSD], ps[:, :], ACT.Silu).then_inc(*free(("uz", i, 1)))
            for j in range(7):
                ps = filled(act, ("xb", j))
                A_(xraw[:, 2 * j:2 * j + 2, :], ps[:, :].rearrange("p (m t) -> p m t", m=2), ACT.Copy)
                for h in range(2):
                    m = 2 * j + h
                    ins = A_(xs[:, m, :], ps[:, h * SEQ:(h + 1) * SEQ], ACT.Identity, scale=par("conv_w_2", 3 * MX + m),
                             bias=par("conv_b_2", m))
                ins.then_inc(*free(("xb", j)))
                if j >= 1:
                    act.wait_ge(S("conv"), j)
                    A_(xs[:, 2 * j - 2:2 * j, :], xs[:, 2 * j - 2:2 * j, :], ACT.Silu).then_inc(S("xs"), 1)
            act.wait_ge(S("conv"), 7)
            A_(xs[:, 12:14, :], xs[:, 12:14, :], ACT.Silu).then_inc(S("xs"), 1)
            act.wait_ge(S("par2_in"), 16 * 3)
            act.wait_ge(S("dt_abs"), 1)
            A_(alog, alog, ACT.Exp).then_inc(S("alog"), 1)
            A_(dtmp, dtmp, ACT.Exp, scale=-1.0).then_inc(S("dt_e"), 1)
            act.wait_ge(S("dt_e"), 1)
            A_(dtmp, dtmp, ACT.Ln, bias=1.0).then_inc(S("dt_ln"), 1)
            drained(act, ("cs",))
            A_(ea[:, 0, 0:SH], acs[:, 1, 0:SH], ACT.Exp)
            A_(ea[:, 1, 0:SH], acs[:, 2, 0:SH], ACT.Exp).then_inc(S("ea"), 1)
            ps = filled(act, ("pm",))
            for h in range(2):
                ins = A_(mixT[:, h, :], ps[:, h * SEQ:(h + 1) * SEQ], ACT.Copy, scale=par("pool_scale_2", h))
            ins.then_inc(*free(("pm",)))
            for i in range(NT):
                for q in range(3):
                    drained(act, ("rb", i, q))
                A_(dec[:, i], dec[:, i], ACT.Exp).then_inc(S("dec_e"), 1)
            for i in range(NT):
                for a in range(2):
                    ps = filled(act, ("xt", i, a))
                    w = 512 if a == 0 else 256
                    A_(xtok[:, i, 512 * a:512 * a + w], ps[:, 0:w], ACT.Copy).then_inc(*free(("xt", i, a)))
            ps = filled(act, ("bt",))
            A_(btk, ps[:, :], ACT.Copy).then_inc(*free(("bt",)))
            for a in range(2):
                ps = filled(act, ("cst", a))
                A_(st[:, 384 * a:384 * a + 384], ps[:, 0:384], ACT.Copy).then_inc(*free(("cst", a)))
            act.wait_ge(S("gms"), 1)
            A_(gms, gms, ACT.Sqrt).then_inc(S("gsd"), 1)
            for i in range(NT):
                for a in range(2):
                    ps = filled(act, ("mt", i, a))
                    for c in range(4 if a == 0 else 2):
                        m = 4 * a + c
                        ins = A_(mixT[:, 2 + m, i * P:(i + 1) * P], ps[:, c * P:(c + 1) * P], ACT.Copy,
                                 scale=par("ssd_norm_w_2", m))
                    ins.then_inc(*free(("mt", i, a)))
            pre_norm(5, lambda i: act.wait_ge(S("x_new"), 4 + i + 1))
            root(5)
            transposed(3, lambda k: modc[:, 32 + k:33 + k], lambda k: modc[:, 24 + k:25 + k])
            act.wait_ge(S("xn"), 8)
            bcast(fin, A["final_norm_w"], "fin_in")
            act.wait_ge(S("g_shift"), 1)
            A_(rtb[0][:, 0:NT * EG], rtb[0][:, 0:NT * EG], ACT.Exp).then_inc(S("g_exp"), 1)
            act.wait_ge(S("v_gap"), 1)
            A_(rtb[1][:, 0:NT], rtb[1][:, 0:NT], ACT.Exp).then_inc(S("v_exp"), 1)
            with act.Fori(0, EXPERTS // 2) as it:
                for s in range(2):
                    for i in range(NT):
                        act.wait_ge(S("hidden"), it * 8 + (4 * s + 2 * i + 2))
                        act.wait_ge(S("act_out"), it * 4 + (2 * s + i))
                        A_(sa[:, i, :], bank[4 + 2 * i][:, :], ACT.Silu).then_inc(S("sa"), 1)
                    for i in range(NT):
                        act.wait_ge(S("turns"), it * 4 + (2 * s + i + 1))
                        A_(acT[:, i, :, :], bank[4 + 2 * i][:, :].rearrange("p (f t) -> p f t", f=KE), ACT.Copy
                           ).then_inc(S(f"turned{i}"), 1)
            pre_norm(6, lambda i: act.wait_ge(S("x_new"), 6 + i + 1))
            root(6)

        @block.gpsimd
        def _(pool):
            pool.wait_ge(S("csil"), 1)
            nc.gpsimd.tensor_copy(cb, csil.unsqueeze(2).to_broadcast([P, KD, 32])).then_inc(S("cb"), 1)
            strict = K("strict").unsqueeze(1).unsqueeze(1).to_broadcast([P, 4, 2, P])

            def diagonal(buf, half):
                return buf[:, 4 * half:4 * half + 4, :].rearrange("p h (b t) -> p h b t", b=3)[:, :, 0:3:2, :]

            pool.wait_ge(S("con_in"), 16)
            for half in range(2):
                pool.wait_ge(S("att_ln"), half + 1)
                hs = slice(4 * half, 4 * half + 4)
                nc.gpsimd.tensor_tensor(rz[:, hs, :], rz[:, hs, :], az[:, hs, :], ALU.add).then_inc(S("att_sum"), 1)
                pool.wait_ge(S("att_sum"), half + 1)
                nc.gpsimd.tensor_tensor(diagonal(rz, half), diagonal(rz, half), strict, ALU.mult).then_inc(S("att_sp"), 1)
            for half in range(2):
                pool.wait_ge(S("att_x"), half + 1)
                nc.gpsimd.tensor_tensor(diagonal(az, half), diagonal(az, half), strict, ALU.mult).then_inc(S("att_w"), 1)
            eye = K("ident").unsqueeze(1).to_broadcast([P, HEADS, P])
            for i in range(NT):
                drained(pool, ("tok", NT - 1, 3) if i == 0 else ("y", 0))
                nc.gpsimd.tensor_copy(dd, eye).then_inc(S("eye"), 1)
                nc.gpsimd.tensor_copy(ddT, eye).then_inc(S("eye"), 1)
            for dm in range(KD):
                drained(pool, ("mg", dm))
                nc.gpsimd.tensor_tensor(gates[:, dm, :], gates[:, dm, :], gates[:, KD + dm, :], ALU.add).then_inc(S("merged"), 1)

        @block.vector
        def _(dve):
            V = nc.vector
            steps = [0]

            def link(ins):
                steps[0] += 1
                ins.then_inc(S("dve_step"), 1)
                dve.wait_ge(S("dve_step"), steps[0])

            def cast(ap, *shape):
                return ap.to_broadcast(list(shape))

            sq_seen = [0]

            def inverse_root(n, halves):
                sq_seen[0] += NT * halves
                dve.wait_ge(S("sq"), sq_seen[0])
                src = ss[n][:, 0:NT]
                if halves == 2:
                    v = ss[n].rearrange("p (i h) -> p i h", h=2)
                    link(V.tensor_tensor(ms[n][:, 0:NT], v[:, :, 0], v[:, :, 1], ALU.add))
                    src = ms[n][:, 0:NT]
                V.tensor_scalar(ms[n][:, 0:NT], src, 1.0 / D, EPS, ALU.mult, ALU.add).then_inc(S("ms"), 1)
                dve.wait_ge(S("sd"), n + 1)
                link(V.reciprocal(rstd[n][:, 0:NT], sd[n][:, 0:NT]))

            def pre_norm(n, s):
                inverse_root(n, 1)
                for i in range(NT):
                    V.tensor_scalar(xn[s][:, i, :], xres[:, i, :], rstd[n][:, i:i + 1], None, ALU.mult).then_inc(S("xn"), 1)

            def transposed(s, scale, bias):
                for kk in (1, 3):
                    ps = filled(dve, ("hT", s, kk))
                    for k2 in range(2):
                        k = 2 * kk + k2
                        ins = V.tensor_scalar(hT[:, k, :], ps[:, k2 * SEQ:(k2 + 1) * SEQ], scale(k), bias(k) if bias else None,
                                              ALU.mult, ALU.add if bias else ALU.bypass)
                    ins.then_inc(*free(("hT", s, kk)))

            sq_out = [2, 8]

            def post_norm(n, name, buf, weight, first):
                for j in range(4):
                    half, i = j // 2, j % 2
                    ps = filled(dve, (name, i, half))
                    dve.wait_ge(S("sq"), sq_seen[0] + j + 1)
                    V.tensor_copy(buf[:, i, 512 * half:512 * half + 512], ps[:, :]).then_inc(*free((name, i, half)))
                inverse_root(n, 2)
                for j in range(4):
                    drained(dve, (name, j % 2, j // 2))
                for i in range(NT):
                    link(V.scalar_tensor_tensor(buf[:, i, :], buf[:, i, :], rstd[n][:, i:i + 1], weight, ALU.mult, ALU.mult))
                    V.tensor_tensor(xres[:, i, :], xres[:, i, :], buf[:, i, :], ALU.add).then_inc(S("x_new"), 1)

            for t, rows in enumerate(PAR):
                n = sum(r for _, r in rows)
                ps = filled(dve, ("par", t))
                V.tensor_copy(parcol[:, t, 0:n], ps[:, 0:n]).then_inc(*free(("par", t)))
            for t in range(NPAR):
                drained(dve, ("par", t))
            V.tensor_scalar(omu, par("mu_rw", 0, 14), -1.0, 1.0, ALU.mult, ALU.add).then_inc(S("omu"), 1)
            dve.wait_ge(S("x_in"), 16)
            pre_norm(0, 0)
            dve.wait_ge(S("lvl_in"), 16)
            link(V.tensor_copy(lvl[:, :], B("lvlf")))
            transposed(0, lambda k: par("norm_mix_pre", k), None)

            def shifted(m):
                if m < 4:
                    return rT[:, m, :]
                if m < 8:
                    return kT[:, m - 4, :]
                return vT[:, m - 8, :] if m < 12 else lora[:, m - 12, :]

            for n, j in enumerate(RW_ORDER):
                ps = filled(dve, ("rw", j))
                dve.wait_ge(S("rw_own"), n + 1)
                for h in range(2):
                    m = 2 * j + h
                    dst = shifted(m)[:, 1:SEQ]
                    ins = V.scalar_tensor_tensor(dst, ps[:, h * SEQ:(h + 1) * SEQ - 1], par("mu_rw", m), dst, ALU.mult, ALU.add)
                ins.then_inc(*free(("rw", j)))
                if j == 3:
                    drained(dve, ("rw", 2))
                    drained(dve, ("rw", 3))
                    for m in range(4):
                        ins = V.tensor_scalar(kkT[:, m, :], kT[:, m, :], par("k_k", m), None, ALU.mult)
                    ins.then_inc(S("kk_raw"), 1)
            dve.wait_ge(S("con_in"), 16)
            for j in range(2):
                drained(dve, ("lw", j))
                for h in range(2):
                    m = 2 * j + h
                    ins = V.tensor_tensor_scan(cum[:, m, :], K("scan_reset"), lw[:, m, :], 0.0, ALU.mult, ALU.add)
            link(ins)
            ch = cum.rearrange("p m (c t) -> p m c t", t=CH)
            tot = total.rearrange("p (m c) -> p m c", c=4)
            V.tensor_copy(tot.unsqueeze(3), ch[:, :, :, CH - 1:CH])
            for j in range(2):
                drained(dve, ("la", j))
            drained(dve, ("kn",))
            for m in range(4):
                ins = V.tensor_scalar(tmp[:, m, :], aT[:, m, :], -1.0, par("k_a", m), ALU.add, ALU.mult)
            link(ins)
            link(V.scalar_tensor_tensor(kT, tmp, 1.0, kT, ALU.add, ALU.mult))
            link(V.tensor_scalar(nmr[0:HEADS, :], nmr[0:HEADS, :], 1e-12, None, ALU.max))
            V.reciprocal(nmr[0:HEADS, :], nmr[0:HEADS, :]).then_inc(S("kk_inv"), 1)
            for m in range(4):
                ins = V.scalar_tensor_tensor(bon[:, m, :], rT[:, m, :], par("r_k", m), kT[:, m, :], ALU.mult, ALU.mult)
            ins.then_inc(S("bon_raw"), 1)
            for j in range(2, 4):
                ps = filled(dve, ("qk", j))
                V.tensor_copy(qk[:, 2 * j:2 * j + 2, :].rearrange("p a b -> p (a b)"), ps[:, :]).then_inc(*free(("qk", j)))
            for i in range(NT):
                ps = filled(dve, ("v", i))
                V.tensor_copy(vtok[:, i, :], ps[:, :]).then_inc(*free(("v", i)))
            for j in range(2):
                ps = filled(dve, ("kb", j))
                V.tensor_tensor(kkT[:, 2 * j:2 * j + 2, :], kkT[:, 2 * j:2 * j + 2, :],
                                ps[:, :].rearrange("p (a b) -> p a b", a=2), ALU.mult).then_inc(*free(("kb", j)))
            for j in range(2):
                drained(dve, ("kb", j))
            V.tensor_tensor(bT, kkT, aT, ALU.mult)
            V.tensor_tensor(lw, cum, lw, ALU.subtract).then_inc(S("ex"), 1)
            for h in range(HEADS):
                ps = filled(dve, ("z", h))
                link(V.tensor_scalar(rz[:, h, :], ps[:, 0:384], 0.0, None, ALU.max))
                V.scalar_tensor_tensor(az[:, h, :], rz[:, h, :], -2.0, ps[:, 0:384], ALU.mult, ALU.add).then_inc(*free(("z", h)))

            def by_tile(x):
                return x.rearrange("p a (i t) -> p a i t", i=NT)

            dve.wait_ge(S("e_inc"), 1)
            V.tensor_tensor(kr[:, :, :, 1, :], by_tile(rT), by_tile(aT), ALU.mult).then_inc(S("kr_r"), 1)
            dve.wait_ge(S("e_exc"), 1)
            V.scalar_tensor_tensor(kr[:, :, :, 0, :], by_tile(kkT), -1.0, by_tile(lw), ALU.mult, ALU.mult).then_inc(S("kr_k"), 1)
            dve.wait_ge(S("e_inv"), 1)
            V.tensor_tensor(bh, bT, tmp, ALU.mult)
            V.tensor_tensor(kh, kT, tmp, ALU.mult).then_inc(S("bk_hat"), 1)
            V.tensor_tensor(ch, cast(tot.unsqueeze(3), P, 4, 4, CH), ch, ALU.subtract).then_inc(S("to_end"), 1)
            for j in range(2):
                ps = filled(dve, ("bn", j))
                V.tensor_tensor(bon[:, 2 * j:2 * j + 2, :], ps[:, :].rearrange("p (a b) -> p a b", a=2),
                                vT[:, 2 * j:2 * j + 2, :], ALU.mult).then_inc(*free(("bn", j)))
            dve.wait_ge(S("e_suf"), 1)
            V.tensor_tensor(bT, bT, cum, ALU.mult)
            V.tensor_tensor(kT, kT, cum, ALU.mult).then_inc(S("bk_bar"), 1)
            for h in range(HEADS):
                ps = filled(dve, ("l", h))
                V.tensor_scalar(az[:, h, :], ps[:, 0:384], 0.0, None, ALU.min).then_inc(*free(("l", h)))
            for i in range(NT):
                ps = filled(dve, ("tok", i, 2))
                V.tensor_copy(ktok[:, i, :], ps[:, :]).then_inc(*free(("tok", i, 2)))
                ps = filled(dve, ("tok", i, 3))
                V.memset(vp[:, i, :, DH:P], 0.0)
                V.tensor_copy(vp[:, i, :, 0:DH], ps[:, :].rearrange("p (h d) -> p h d", h=HEADS)).then_inc(*free(("tok", i, 3)))

            def heads4(ps):
                return ps[:, :].rearrange("p (h t) -> p h t", h=4)

            blocks = cast(K("head_block").unsqueeze(1), P, PAIRS, P)

            def ada_sum(c):
                ps = filled(dve, ("as", c))
                if c in COLUMN_CHUNKS:
                    V.tensor_tensor(modc[:, 4 * c:4 * c + 4], ps[:, 0:4], par("b_ada_2", 4 * c, 4), ALU.add).then_inc(*free(("as", c)))
                else:
                    g = (g1 if c < 6 else g2)[:, 512 * (c % 2):512 * (c % 2) + 512]
                    V.tensor_tensor(g, g, ps[:, :], ALU.add).then_inc(*free(("as", c)))

            dve.wait_ge(S("gate_in"), 32)
            dve.wait_ge(S("pc"), 1)
            c = 0
            for i in range(NT):
                for h in range(HEADS):
                    ps = filled(dve, ("g", i, h))
                    V.tensor_tensor(gm[:, h, :], ps[:, :], K("gram_mask"), ALU.mult).then_inc(*free(("g", i, h)))
                dve.wait_ge(S("eye"), 2 * i + 2)
                for q in range(2):
                    hs = slice(4 * q, 4 * q + 4)
                    ps = filled(dve, ("n", i, q))
                    V.copy_predicated(dd[:, hs, :], lmask(0, 0), heads4(ps)).then_inc(*free(("n", i, q)))
                    drained(dve, ("g", i, 4 * q + 3))
                    V.copy_predicated(ddT[:, hs, :], lmask(0, 1), gm[:, hs, 0:P]).then_inc(S("dt_first"), 1)
                for lv in range(1, LEVELS):
                    if c:
                        ada_sum(c - 1)
                    c += 1
                    for q in range(2):
                        hs = slice(4 * q, 4 * q + 4)
                        if lv < LEVELS - 1:
                            ps = filled(dve, ("d", i, lv, q))
                            V.copy_predicated(dd[:, hs, :], lmask(lv, 0), heads4(ps)).then_inc(*free(("d", i, lv, q)))
                        ps = filled(dve, ("dt", i, lv, q))
                        V.copy_predicated(ddT[:, hs, :], lmask(lv, 1), heads4(ps)).then_inc(*free(("dt", i, lv, q)))
                ada_sum(c - 1)
                c += 1
                ps = filled(dve, ("ry", i))
                V.tensor_tensor(ryT[:, :, i * P:(i + 1) * P], heads4(ps), kr[:, :, i, 1, :], ALU.add).then_inc(*free(("ry", i)))
                for k in (2 * i, 2 * i + 1):
                    if k == 3:
                        continue
                    ps = filled(dve, ("psi", k))
                    V.tensor_tensor(psi[:, k], heads4(ps), blocks, ALU.mult).then_inc(*free(("psi", k)))
                k = i + 1
                ps = filled(dve, ("phi", k))
                V.tensor_tensor(phi[:, k - 1], heads4(ps), blocks, ALU.mult).then_inc(*free(("phi", k)))
                drained(dve, ("phi", k))
                for p in range(PAIRS):
                    ins = V.scalar_tensor_tensor(phi[:, k - 1, p, :], K("ident"), pc[:, 4 * p + k:4 * p + k + 1],
                                                 phi[:, k - 1, p, :], ALU.mult, ALU.add)
                ins.then_inc(S("phi"), 1)
                ps = filled(dve, ("s", k))
                drained(dve, ("psi", k))
                V.tensor_tensor(psi[:, k], psi[:, k], heads4(ps), ALU.add).then_inc(*free(("s", k)))
            ada_sum(11)
            for c in COLUMN_CHUNKS:
                drained(dve, ("as", c))
            link(V.tensor_scalar(modc[:, 8:16], modc[:, 8:16], 1.0, None, ALU.add))
            V.tensor_scalar(modc[:, 32:40], modc[:, 32:40], 1.0, None, ALU.add).then_inc(S("mod"), 1)
            for i in range(NT):
                drained(dve, ("y", i))
            for j in range(2):
                ps = filled(dve, ("m", j))
                V.tensor_tensor(yT[:, 2 * j:2 * j + 2, :], yT[:, 2 * j:2 * j + 2, :],
                                ps[:, :].rearrange("p (a b) -> p a b", a=2), ALU.subtract).then_inc(*free(("m", j)))
            ps = filled(dve, ("vn",))
            V.tensor_scalar(nmr[0:HEADS, :], ps[0:HEADS, 0:SEQ], 1.0 / DH, GN_EPS, ALU.mult, ALU.add).then_inc(*free(("vn",)))
            dve.wait_ge(S("y_sd"), 1)
            V.reciprocal(nmr[0:HEADS, :], nmr[0:HEADS, :]).then_inc(S("y_inv"), 1)
            for j in range(2):
                drained(dve, ("m", j))
                ps = filled(dve, ("vb", j))
                V.tensor_tensor(yT[:, 2 * j:2 * j + 2, :], yT[:, 2 * j:2 * j + 2, :],
                                ps[:, :].rearrange("p (a b) -> p a b", a=2), ALU.mult).then_inc(*free(("vb", j)))
            for j in range(2):
                drained(dve, ("vb", j))
            for m in range(4):
                ins = V.tensor_scalar(yT[:, m, :], yT[:, m, :], par("lnx_w", m), par("lnx_b", m), ALU.mult, ALU.add)
            link(ins)
            for j in range(2):
                drained(dve, ("bn", j))
            link(V.tensor_tensor(yT, yT, bon, ALU.add))
            V.tensor_tensor(orw, yT, gT, ALU.mult).then_inc(S("orw"), 1)
            for j in range(8):
                drained(dve, ("ga", j))
            for dm in range(KD):
                ps = filled(dve, ("mg", dm))
                V.tensor_tensor(gates[:, dm, :], gates[:, dm, :], ps[:, 0:SEQ], ALU.mult)
                V.tensor_tensor(gates[:, KD + dm, :], gates[:, KD + dm, :], ps[:, SEQ:2 * SEQ], ALU.mult).then_inc(*free(("mg", dm)))
            dve.wait_ge(S("npost_in"), 16)
            post_norm(1, "mo", mo, npost, 0)
            for i in range(NT):
                dve.wait_ge(S("x_new"), i + 1)
            pre_norm(2, 1)
            transposed(1, lambda k: par("norm_ffn_pre", k), None)
            for f in range(KF):
                ps = filled(dve, ("ff", f))
                dve.wait_ge(S("sil"), f + 1)
                V.tensor_tensor(fT[:, f, :], sil[:, f % 2, :], ps[:, SEQ:2 * SEQ], ALU.mult).then_inc(*free(("ff", f)))
            dve.wait_ge(S("post_in"), 16)
            post_norm(3, "dn", dno, fpost, 0)
            dve.wait_ge(S("x_new"), 4)
            pre_norm(4, 2)
            dve.wait_ge(S("mod"), 1)
            transposed(2, lambda k: modc[:, 8 + k:9 + k], lambda k: modc[:, k:k + 1])
            for j in range(7):
                drained(dve, ("xb", j))
                for d in range(1, 4):
                    for h in range(2):
                        m = 2 * j + h
                        ins = V.scalar_tensor_tensor(xs[:, m, d:SEQ], xraw[:, m, 0:SEQ - d], par("conv_w_2", (3 - d) * MX + m),
                                                     xs[:, m, d:SEQ], ALU.mult, ALU.add)
                    if d < 3:
                        link(ins)
                    else:
                        ins.then_inc(S("conv"), 1)
            dve.wait_ge(S("router_in"), 64)
            ps = filled(dve, ("dt2",))
            V.tensor_tensor(dtr, ps[:, 0:32].rearrange("p (i c) -> p i c", i=NT)[:, :, 0:SH], cast(dtb.unsqueeze(1), P, NT, SH),
                            ALU.add).then_inc(*free(("dt2",)))
            drained(dve, ("dt2",))
            V.scalar_tensor_tensor(dtmp, dtr, -1.0, dtr, ALU.mult, ALU.max).then_inc(S("dt_abs"), 1)
            ps = filled(dve, ("pl",))
            V.tensor_copy(dif.rearrange("p a b -> p (a b)"), ps[:, :]).then_inc(*free(("pl",)))
            dve.wait_ge(S("dt_ln"), 1)
            link(V.scalar_tensor_tensor(dtr, dtr, 0.0, dtmp, ALU.max, ALU.add))
            dve.wait_ge(S("alog"), 1)
            V.scalar_tensor_tensor(da, dtr, -1.0, cast(alog.unsqueeze(1), P, NT, SH), ALU.mult, ALU.mult).then_inc(S("da"), 1)
            ps = filled(dve, ("cs",))
            V.tensor_copy(acs[:, :, 0:SH], ps[:, 0:48].rearrange("p (i c) -> p i c", i=3)[:, :, 0:SH]).then_inc(*free(("cs",)))
            drained(dve, ("cs",))
            for i in range(NT):
                for q in range(3):
                    ps = filled(dve, ("rb", i, q))
                    for j in range(4):
                        h = 4 * q + j
                        ins = V.tensor_scalar(dec[:, i, h, :], ps[:, j * P:(j + 1) * P], acs[:, i, h:h + 1], 0.0, ALU.subtract, ALU.min)
                    ins.then_inc(*free(("rb", i, q)))
            for i in range(NT):
                ps = filled(dve, ("cb", i))
                V.tensor_tensor(cbm[:, i], heads4(ps), cast(K("causal").unsqueeze(1), P, GRP, P), ALU.mult).then_inc(*free(("cb", i)))
                dve.wait_ge(S("dec_e"), i + 1)
                drained(dve, ("cb", i))
                d4 = dec[:, i].rearrange("p (g r) t -> p g r t", g=GRP)
                V.tensor_tensor(d4, d4, cast(cbm[:, i].unsqueeze(2), P, GRP, SR, P), ALU.mult).then_inc(S("dec"), 1)

            def by_head(x):
                return x.rearrange("p (h d) -> p h d", h=SH)

            dve.wait_ge(S("ea"), 1)
            for i in range(NT):
                for a in range(2):
                    drained(dve, ("xt", i, a))
                V.tensor_tensor(by_head(xc[:, i]), by_head(xtok[:, i]), cast(dtr[:, i, :].unsqueeze(2), P, SH, DH), ALU.mult
                                ).then_inc(S("xc"), 1)
                if i == 0:
                    dve.wait_ge(S("xc"), 1)
                    V.tensor_tensor(by_head(xde), by_head(xc[:, 0]), cast(ea[:, 1, 0:SH].unsqueeze(2), P, SH, DH), ALU.mult
                                    ).then_inc(S("xde"), 1)
            dve.wait_ge(S("par2_in"), 48)
            for i in range(NT):
                link(V.tensor_tensor(by_head(ys[:, i]), by_head(xtok[:, i]), cast(dsk.unsqueeze(2), P, SH, DH), ALU.mult))
                for a in range(2):
                    w = 512 if a == 0 else 256
                    f = slice(512 * a, 512 * a + w)
                    ps = filled(dve, ("yd", i, a))
                    V.tensor_tensor(ys[:, i, f], ys[:, i, f], ps[:, 0:w], ALU.add).then_inc(*free(("yd", i, a)))
            for a in range(2):
                ps = filled(dve, ("yo", a))
                f = slice(384 * a, 384 * a + 384)
                V.tensor_tensor(yo[:, f].rearrange("p (h d) -> p h d", d=DH), ps[:, 0:384].rearrange("p (h d) -> p h d", d=DH),
                                cast(ea[:, 0, 6 * a:6 * a + 6].unsqueeze(2), P, 6, DH), ALU.mult).then_inc(*free(("yo", a)))
            for a in range(2):
                drained(dve, ("yo", a))
                drained(dve, ("yd", 1, a))
            link(V.tensor_tensor(ys[:, 1], ys[:, 1], yo, ALU.add))
            for a in range(2):
                drained(dve, ("yd", 0, a))
            link(V.tensor_tensor(ys, ys, sz, ALU.mult))
            link(V.tensor_tensor(ysq, ys, ys, ALU.mult))
            GW = SR * DH
            grp = ysq.rearrange("p i (g d) -> p (i g) d", g=GRP)
            link(V.tensor_reduce(gss, grp, AX.X, ALU.add))
            V.tensor_scalar(gms, gss, 1.0 / GW, EPS, ALU.mult, ALU.add).then_inc(S("gms"), 1)
            dve.wait_ge(S("gsd"), 1)
            link(V.reciprocal(gss, gms))
            for i in range(NT):
                yg = ys[:, i].rearrange("p (g d) -> p g d", g=GRP)
                V.tensor_tensor(yg, yg, cast(gss[:, GRP * i:GRP * i + GRP].unsqueeze(2), P, GRP, GW), ALU.mult).then_inc(S("ys"), 1)
            for c in (4, 5, 10, 11):
                drained(dve, ("as", c))
            for n in range(2):
                f = slice(512 * n, 512 * n + 512)
                for i in range(NT):
                    ps = filled(dve, ("mx", i, n))
                    V.tensor_tensor(gtmp, ps[:, :], g1[:, f], ALU.mult).then_inc(*free(("mx", i, n)))
                    drained(dve, ("mx", i, n))
                    ins = V.tensor_tensor(xres[:, i, f], xres[:, i, f], gtmp, ALU.add)
                    if n == 1:
                        ins.then_inc(S("x_new"), 1)
                        dve.wait_ge(S("x_new"), 5 + i)
                    else:
                        link(ins)
            dve.wait_ge(S("x_new"), 6)
            pre_norm(5, 3)
            transposed(3, lambda k: modc[:, 32 + k:33 + k], lambda k: modc[:, 24 + k:25 + k])
            V.memset(junk[0:1, 0:512], 0.0)
            V.memset(rs[0:1, 0:1], 0.0).then_inc(S("zero"), 1)
            ps = filled(dve, ("rt",))
            V.tensor_tensor(lg, ps[:, 0:NT * 64].rearrange("p (i c) -> p i c", i=NT)[:, :, 0:36], cast(rbias.unsqueeze(1), P, NT, 36),
                            ALU.add).then_inc(*free(("rt",)))
            drained(dve, ("rt",))

            def first_max(hot, vals, best, rev, n, keep):
                flag, top = keep
                link(V.tensor_reduce(best, vals, AX.X, ALU.max))
                link(V.tensor_tensor(flag, vals, cast(best.unsqueeze(2), P, NT, n), ALU.is_ge))
                link(V.tensor_tensor(flag, flag, rev, ALU.mult))
                link(V.tensor_reduce(top, flag, AX.X, ALU.max))
                link(V.tensor_tensor(hot, flag, cast(top.unsqueeze(2), P, NT, n), ALU.is_equal))

            def wide(buf, n):
                return buf[:, 0:NT * n].rearrange("p (i c) -> p i c", i=NT)

            best_g, v1, v2, top, gsum = (rtb[7][:, 2 * n:2 * n + 2] for n in range(5))
            hot_g = wide(rtb[2], EG)
            flag = wide(rtb[3], EG)
            first_max(hot_g, lg[:, :, 0:EG], best_g, wide(K("rev_group"), EG), EG, (flag, top))
            ex_g = wide(rtb[0], EG)
            V.tensor_tensor(ex_g, lg[:, :, 0:EG], cast(best_g.unsqueeze(2), P, NT, EG), ALU.subtract).then_inc(S("g_shift"), 1)
            link(V.tensor_scalar(hot_g, hot_g, 1.0, BIG, ALU.subtract, ALU.mult))
            inside = wide(rtb[4], EXPERTS)
            link(V.tensor_tensor(inside.rearrange("p i (g e) -> p i g e", g=EG),
                                 lg[:, :, EG:36].rearrange("p i (g e) -> p i g e", g=EG),
                                 cast(hot_g.unsqueeze(3), P, NT, EG, EPG), ALU.add))
            hot1, hot2, flag = wide(rtb[5], EXPERTS), wide(rtb[6], EXPERTS), wide(rtb[3], EXPERTS)
            rev = wide(K("rev_expert"), EXPERTS)
            first_max(hot1, inside, v1, rev, EXPERTS, (flag, top))
            link(V.scalar_tensor_tensor(inside, hot1, -3.0 * BIG, inside, ALU.mult, ALU.add))
            first_max(hot2, inside, v2, rev, EXPERTS, (flag, top))
            V.tensor_tensor(rtb[1][:, 0:NT], v2, v1, ALU.subtract).then_inc(S("v_gap"), 1)
            dve.wait_ge(S("g_exp"), 1)
            link(V.tensor_reduce(gsum, ex_g, AX.X, ALU.add))
            dve.wait_ge(S("v_exp"), 1)
            link(V.scalar_tensor_tensor(top, rtb[1][:, 0:NT], 1.0, gsum, ALU.add, ALU.mult))
            link(V.reciprocal(top, top))
            link(V.tensor_tensor(hot2, hot2, cast(rtb[1][:, 0:NT].unsqueeze(2), P, NT, EXPERTS), ALU.mult))
            link(V.tensor_tensor(hot1, hot1, hot2, ALU.add))
            V.tensor_tensor(gate, hot1, cast(top.unsqueeze(2), P, NT, EXPERTS), ALU.mult).then_inc(S("gate"), 1)
            dve.wait_ge(S("gate"), 1)
            with dve.Fori(0, EXPERTS // 2) as it:
                for s in range(2):
                    for i in range(NT):
                        dve.wait_ge(S("sa"), it * 4 + (2 * s + i + 1))
                        dve.wait_ge(S("turns"), it * 4 + (2 * s))
                        V.scalar_tensor_tensor(ac[:, i, :], sa[:, i, :], gate[:, i, bass.ds(it * 2 + s, 1)], bank[5 + 2 * i][:, :],
                                               ALU.mult, ALU.mult).then_inc(S("act_out"), 1)
            dve.wait_ge(S("expert_done1"), EXPERTS // 2)
            for i in range(NT):
                for n in range(2):
                    f = slice(512 * n, 512 * n + 512)
                    link(V.tensor_tensor(gtmp, bank[2 * i + n][:, :], g2[:, f], ALU.mult))
                    ins = V.tensor_tensor(xres[:, i, f], xres[:, i, f], gtmp, ALU.add)
                    if n == 1:
                        ins.then_inc(S("x_new"), 1)
                        dve.wait_ge(S("x_new"), 7 + i)
                    else:
                        link(ins)
            dve.wait_ge(S("x_new"), 8)
            inverse_root(6, 1)
            dve.wait_ge(S("fin_in"), 16)
            for i in range(NT):
                V.scalar_tensor_tensor(xres[:, i, :], xres[:, i, :], rstd[6][:, i:i + 1], fin, ALU.mult, ALU.mult).then_inc(S("y_out"), 1)


_INS = ['x', 'norm_mix_pre', 'w_in', 'b_gate', 'mu_rw', 'w0', 'w_up', 'a0', 'a_up', 'g_up', 'k_k', 'k_a', 'r_k',
        'lnx_w', 'lnx_b', 'w_sb_out', 'w_rw_out', 'w_o', 'norm_mix_post', 'norm_ffn_pre', 'w_ffn_gate', 'w_ffn_up',
        'w_ffn_down', 'norm_ffn_post', 'c_2', 'w_ada_2', 'b_ada_2', 'w_in_2', 'w_pool_2', 'pool_scale_2', 'conv_w_2',
        'conv_b_2', 'dt_bias_2', 'a_log_2', 'd_skip_2', 'ssd_norm_w_2', 'w_out_2', 'w_group_2', 'b_group_2',
        'w_router_2', 'b_router_2', 'w13_2', 'w2_2', 'final_norm_w_2']


def kernel(**inputs):
    import numpy as _np
    import concourse.bacc as _bacc
    from concourse import mybir as _mybir
    from concourse.bass_utils import run_bass_kernel_spmd as _run

    nc = _bacc.Bacc("TRN2", target_bir_lowering=False, num_devices=1)
    arrays, args = {}, {}
    for name in _INS:
        a = _np.ascontiguousarray(inputs[name])
        arrays[f"in_{name}"] = a
        args[name] = nc.dram_tensor(f"in_{name}", a.shape, _mybir.dt.from_np(a.dtype), kind="ExternalInput").ap()
    for name, a in (("consts", host_constants()), ("levels", host_level_masks()), ("bands", host_bands())):
        arrays[name] = a
        args[name] = nc.dram_tensor(name, a.shape, _mybir.dt.from_np(a.dtype), kind="ExternalInput").ap()
    args["final_norm_w"] = args["final_norm_w_2"]
    out = nc.dram_tensor("out", (1, SEQ, D), _mybir.dt.from_np(_np.dtype("float32")), kind="ExternalOutput").ap()
    build(nc, args, out)
    r = _run(nc, [arrays], core_ids=[0])
    return r.results[0]["out"]
```

```python
import numpy as np
import concourse.bass as bass
from concourse import mybir
from contextlib import ExitStack

F32 = mybir.dt.float32
F32R = mybir.dt.float32r
U8 = mybir.dt.uint8
I32 = mybir.dt.int32
ALU = mybir.AluOpType
ACT = mybir.ActivationFunctionType
AX = mybir.AxisListType

P = 128
SEQ = 256
NT = SEQ // P
D = 1024
KD = D // P
HEADS = 8
DH = 64
WID = HEADS * DH
PAIRS = HEADS // 2
CH = 64
SB_COLS = 3 * WID
RW_COLS = 3 * WID + 256
FF = 2816
KF = FF // P
GN_EPS = DH * 1e-5
EPS = 1e-6
DECAY = -float(np.exp(-0.5))
GRP = 4
SH = 12
SR = SH // GRP
POOL = 256
SSD = 768
XBC = SSD + 2 * GRP * P
MX = XBC // P
WINDOWS = (2, 4, 8, 16)
EXPERTS = 32
EG = 4
EPG = EXPERTS // EG
EF = 512
KE = EF // P
BIG = 1e30

SLOT = 4096
CAP = 64
RING = 3
LEVELS = 6
NPAR = 3


def const_layout():
    names = [("ident", P), ("ones", P), ("neg_suffix", P), ("neg_ones", P), ("strict", P), ("gram_mask", 4 * P),
             ("head_block", P), ("head_mean", P), ("scan_reset", SEQ), ("head_sum", PAIRS * HEADS),
             ("head_spread", PAIRS * P), ("causal", P), ("after", P), ("thirty_second", P),
             ("rev_group", NT * EG), ("rev_expert", NT * EXPERTS), ("slot", CAP)]
    at, out = 0, {}
    for n, w in names:
        out[n] = (at, at + w)
        at += w
    return out, at


CONST, NCONST = const_layout()


def host_constants():
    c = np.zeros((P, NCONST), np.float32)
    i, j = np.arange(P)[:, None], np.arange(P)[None, :]
    same = (i // CH) == (j // CH)

    def put(name, v):
        a, b = CONST[name]
        c[:, a:b] = v

    put("ident", i == j)
    put("ones", 1.0)
    put("neg_suffix", -1.0 * (i >= j))
    put("neg_ones", -1.0)
    put("strict", i < j)
    put("gram_mask", np.concatenate([same & (i < j), same & (i <= j)] * 2, axis=1))
    put("head_block", same)
    put("head_mean", same / DH)
    put("scan_reset", (np.arange(SEQ) % CH != 0)[None, :])
    a, b = CONST["head_sum"]
    s = np.zeros((P, PAIRS, HEADS), np.float32)
    t = np.zeros((P, PAIRS, P), np.float32)
    for p in range(PAIRS):
        for h in range(2):
            s[h * DH:(h + 1) * DH, p, 2 * p + h] = 1
            t[2 * p + h, p, h * DH:(h + 1) * DH] = 1
    c[:, a:b] = s.reshape(P, -1)
    a, b = CONST["head_spread"]
    c[:, a:b] = t.reshape(P, -1)
    put("causal", i <= j)
    put("after", i > j)
    put("thirty_second", 1.0 / 32)
    put("rev_group", np.tile(EG - np.arange(EG), NT)[None, :])
    put("rev_expert", np.tile(EXPERTS - np.arange(EXPERTS), NT)[None, :])
    put("slot", 1.0 + np.arange(CAP)[None, :])
    return c


def host_level_masks():
    i, j = np.arange(P)[:, None], np.arange(P)[None, :]
    m = np.zeros((P, 2, LEVELS, P), np.float32)
    for n in range(LEVELS):
        s = 1 << n
        low = (i // (2 * s) == j // (2 * s)) & ((i // s) % 2 == 1) & ((j // s) % 2 == 0)
        m[:, 0, n] = low
        m[:, 1, n] = low.T
    return m.reshape(P, -1)


def host_bands():
    t, s = np.arange(SEQ)[None, :], np.arange(SEQ)[:, None]
    out = np.zeros((P, GRP, SEQ + P), np.float32)
    for g, w in enumerate(WINDOWS):
        band = ((s <= t) & (s > t - w)) / np.minimum(t + 1, w) - (s == t)
        out[:, g, :SEQ] = band[:P]
        out[:, g, SEQ:] = band[P:, P:]
    return out.reshape(P, -1)


PAR = [
    [("norm_mix_pre", 8), ("mu_rw", 14), ("w0", 4), ("a0", 4), ("k_k", 4), ("k_a", 4), ("r_k", 4), ("lnx_w", 4),
     ("lnx_b", 4), ("b_gate", 16), ("norm_ffn_pre", 8), ("c_2", 8)],
    [("pool_scale_2", 2), ("conv_w_2", 4 * MX), ("conv_b_2", MX), ("ssd_norm_w_2", 6)],
    [("b_ada_2", 48)],
]


def par_columns():
    out = {}
    for n, rows in enumerate(PAR):
        at = 0
        for name, r in rows:
            out[name] = (n, at, r)
            at += r
    return out


PARCOL = par_columns()


def ada_banks(c):
    return ([("as", c - 1)] if c else []) + [("ad", c)]


def plan_banks():
    o = [("par", n) for n in range(NPAR)]
    o += [("hT", 0, kk) for kk in range(4)]
    o += [("rw", mm) for mm in RW_ORDER]
    o += [(n, mm) for n in ("lw", "la", "lg") for mm in range(2)]
    o += [("qk", mm) for mm in range(4)] + [("v", i) for i in range(NT)]
    o += [("kn",)] + [("kb", mm) for mm in range(2)]
    o += [("z", h) for h in range(HEADS)]
    o += [("bn", mm) for mm in range(2)]
    o += [("l", h) for h in range(HEADS)]
    o += [("o", p) for p in range(PAIRS)]
    o += [("tok", i, a) for i in range(NT) for a in range(4)]
    ada = 0
    for i in range(NT):
        o += [("g", i, h) for h in range(HEADS)]
        o += [("n", i, q) for q in range(2)]
        for lv in range(1, LEVELS):
            o += [("x", i, lv, q) for q in range(2)]
            o += ada_banks(ada)
            ada += 1
            for q in range(2):
                o += ([("d", i, lv, q)] if lv < LEVELS - 1 else []) + [("dt", i, lv, q)]
        o += [("w1", i, q) for q in range(2)]
        o += ada_banks(ada)
        ada += 1
        o += [("u", i, q) for q in range(2)]
        if i == 0:
            o += [("ry", 0), ("psi", 0), ("psi", 1), ("phi", 1), ("y", 0), ("s", 1)]
        else:
            o += [("ry", 1), ("psi", 2), ("phi", 2), ("s", 2), ("y", 1)]
    o += [("as", 11)]
    o += [("ga", mm) for mm in range(0, 2)] + [("m", mm) for mm in range(2)]
    o += [("ga", mm) for mm in range(2, 5)] + [("vn",)]
    o += [("ga", mm) for mm in range(5, 8)] + [("vb", mm) for mm in range(2)]
    o += [("mg", dm) for dm in range(KD)]
    o += [("mo", i, n) for n in range(2) for i in range(NT)]
    o += [("hT", 1, kk) for kk in range(4)]
    o += [("ff", m) for m in range(KF)]
    o += [("dn", i, n) for n in range(2) for i in range(NT)]
    o += [("hT", 2, kk) for kk in range(4)]
    o += [("uz", i, n) for n in range(2) for i in range(NT)]
    o += [("xb", mm) for mm in range(7)]
    o += [("dt2",), ("pl",), ("cs",), ("pm",)]
    o += [("rb", i, q) for i in range(NT) for q in range(3)]
    o += [("cb", i) for i in range(NT)]
    o += [("xt", i, a) for i in range(NT) for a in range(2)] + [("bt",)]
    o += [("yd", 0, a) for a in range(2)] + [("cst", a) for a in range(2)]
    o += [("yd", 1, a) for a in range(2)] + [("yo", a) for a in range(2)]
    o += [("mt", i, a) for i in range(NT) for a in range(2)]
    o += [("mx", i, n) for n in range(2) for i in range(NT)]
    o += [("hT", 3, kk) for kk in range(4)]
    o += [("rt",), ("rk",)]
    assert len(set(o)) == len(o)
    return {k: (n % 8, n // 8) for n, k in enumerate(o)}


RW_ORDER = (6, 2, 3, 0, 1, 4, 5)
COLUMN_CHUNKS = (0, 1, 2, 3, 6, 7, 8, 9)
QTOK = 4 * SEQ

NORM1, PROJ, PREP, TOKENS, WKV, GATES, MERGE, POST1, FFN, DOWN, PROJ2, CONV, SCAN, MIXED, MOE = range(15)
BUFFERS = [
    ("junk", D, NORM1, MOE), ("parrow", NPAR * P, NORM1, NORM1), ("g1", D, NORM1, MIXED), ("g2", D, NORM1, MOE),
    ("wua", WID, NORM1, PROJ), ("gup", WID, NORM1, PROJ), ("cb", KD * 32, NORM1, WKV), ("npost", D, MERGE, POST1),
    ("xn0", NT * D, NORM1, NORM1), ("lvlf", 2 * LEVELS * P, NORM1, NORM1),
    ("osb", QTOK, PREP, MERGE), ("gT", QTOK, PROJ, GATES), ("bon", QTOK, PREP, GATES),
    ("tmp", QTOK, PREP, GATES), ("nmr", SEQ, PREP, GATES),
    ("kr", 2 * QTOK, PREP, WKV), ("bh", QTOK, PREP, WKV), ("kh", QTOK, PREP, WKV),
    ("kT", QTOK, PROJ, TOKENS), ("vT", QTOK, PROJ, TOKENS), ("b", QTOK, PREP, TOKENS),
    ("rT", QTOK, PROJ, PREP), ("lora", 2 * SEQ, PROJ, PREP), ("a", QTOK, PROJ, PREP), ("lw", QTOK, PROJ, PREP),
    ("kk", QTOK, PREP, PREP), ("cum", QTOK, PREP, PREP), ("qk", 2 * QTOK, PROJ, PREP), ("v", NT * WID, PROJ, PREP),
    ("az", HEADS * 384, PREP, PREP), ("rz", HEADS * 384, PREP, PREP),
    ("vp", NT * HEADS * P, TOKENS, WKV), ("btok", NT * WID, TOKENS, WKV), ("ktok", NT * WID, TOKENS, WKV),
    ("zb", NT * HEADS * P, TOKENS, WKV),
    ("modp", 2 * 512, WKV, GATES), ("gm", HEADS * 4 * P, WKV, WKV), ("dd", HEADS * P, WKV, WKV),
    ("ddT", HEADS * P, WKV, WKV), ("xx", HEADS * P, WKV, WKV), ("up", HEADS * DH, WKV, WKV),
    ("tk", HEADS * DH, WKV, WKV), ("phi", 2 * PAIRS * P, WKV, WKV), ("psi", 3 * PAIRS * P, WKV, WKV),
    ("ry", QTOK, WKV, WKV), ("y", QTOK, WKV, GATES),
    ("orw", QTOK, GATES, MERGE), ("gates", 16 * SEQ, GATES, POST1),
    ("mo", NT * D, POST1, POST1), ("xn1", NT * D, POST1, FFN), ("fpost", D, FFN, DOWN),
    ("fT", KF * SEQ, FFN, DOWN), ("fh", KF * SEQ, FFN, DOWN), ("hi", 3 * SLOT, POST1, PROJ2), ("hh1", KD * SEQ, FFN, FFN),
    ("hh2", KD * SEQ, PROJ2, PROJ2),
    ("sil", 2 * SEQ, FFN, FFN), ("dno", NT * D, DOWN, DOWN),
    ("xn2", NT * D, DOWN, PROJ2),
    ("u", NT * POOL, PROJ2, SCAN), ("sz", NT * SSD, PROJ2, MIXED), ("xraw", MX * SEQ, PROJ2, CONV),
    ("xs", MX * SEQ, PROJ2, SCAN), ("band", GRP * (SEQ + P), PROJ2, CONV), ("wp", P, PROJ2, SCAN),
    ("dif", 2 * SEQ, CONV, SCAN), ("dt", 32, CONV, SCAN), ("dtmp", 32, CONV, SCAN), ("da", 32, CONV, SCAN),
    ("acs", 48, CONV, SCAN), ("ea", 32, CONV, SCAN),
    ("dec", NT * SH * P, SCAN, SCAN), ("cbm", NT * GRP * P, SCAN, SCAN), ("xtok", NT * SSD, SCAN, SCAN),
    ("btk", GRP * P, SCAN, SCAN), ("xc", NT * SSD, SCAN, SCAN), ("xde", SSD, SCAN, SCAN), ("st", SSD, SCAN, SCAN),
    ("yo", SSD, SCAN, SCAN), ("ys", NT * SSD, SCAN, MIXED), ("ysq", NT * SSD, SCAN, MIXED),
    ("mixT", KD * SEQ, CONV, MIXED), ("gtmp", 512, MIXED, MOE),
    ("xn3", NT * D, MIXED, MOE), ("ew", 3 * SLOT, MIXED, MOE), ("sa", 2 * EF, MOE, MOE), ("ac", 2 * EF, MOE, MOE),
    ("acT", 2 * EF, MOE, MOE), ("lg", NT * 36, MOE, MOE), ("rt", 8 * 64, MOE, MOE), ("gate", 64, MOE, MOE),
    ("rs", 64, MOE, MOE), ("fin", D, MOE, MOE), ("posq", 64, MOE, MOE), ("gateq", 64, MOE, MOE),
    ("hg", KD * P, MOE, MOE), ("one", 2 * P, MOE, MOE), ("onew", 2 * P, MOE, MOE), ("onewT", SEQ, MOE, MOE),
    ("yslot", D, MOE, MOE),
]


def place(limit):
    at = {}
    spans = []
    for name, w, first, last in sorted(BUFFERS, key=lambda b: (b[2] - b[3], -b[1])):
        near = sorted((a, a + x) for a, x, f, l in spans if f <= last and first <= l)
        pos = 0
        for a, b in near:
            if pos + w <= a:
                break
            pos = max(pos, b)
        assert pos + w <= limit, (name, pos + w, limit)
        spans.append((pos, w, first, last))
        at[name] = (pos, pos + w)
    return at


def build(nc, A, out):
    BANK = plan_banks()
    ctx = ExitStack()
    with ctx:
        sems = {}

        def S(name):
            if name not in sems:
                sems[name] = ctx.enter_context(nc.semaphore(name))
            return sems[name]

        start = {}

        def sb(name, shape, dt=F32):
            start[name] = -(-nc.sbuf_base // 32) * 32
            return ctx.enter_context(nc.sbuf_tensor(name, shape, dt))

        def rounded(name, shape, buffer, words=0):
            return nc.alloc_sbuf_tensor_at(name, [P] + shape, F32R, offset=start[buffer] + 4 * words)

        con = sb("con", [P, NCONST])
        lvl = sb("lvl", [P, 2 * LEVELS * P], U8)
        parcol = sb("parcol", [P, NPAR, P])
        xres = sb("xres", [P, NT, D])
        hT = sb("hT", [P, KD, SEQ])
        small = sb("small", [P, 600])
        crowded = sb("crowded", [P, 1], I32)
        ring = sb("ring", [P, RING, SLOT])
        words = nc.sbuf_bytes_remaining // 4 - 64
        arena = sb("arena", [P, words])
        where = place(words)
        bank = [ctx.enter_context(nc.psum_tensor(f"bank{b}", [P, 512], F32)) for b in range(8)]
        bank_full = [S(f"bank_full{b}") for b in range(8)]
        bank_free = [S(f"bank_free{b}") for b in range(8)]

        def K(name):
            a, b = CONST[name]
            return con[:, a:b]

        def par(name, n=0, w=1):
            t, at, _ = PARCOL[name]
            return parcol[:, t, at + n:at + n + w]

        def lmask(lv, turned):
            m = lvl[:, (turned * LEVELS + lv) * P:(turned * LEVELS + lv + 1) * P]
            return m.unsqueeze(1).to_broadcast([P, 4, P])

        at = [0]

        def tiny(w):
            at[0] += w
            assert at[0] <= 600
            return small[:, at[0] - w:at[0]]

        ss, ms, sd, rstd = ([tiny(4) for _ in range(7)] for _ in range(4))
        omu, total, pc, modc = tiny(14), tiny(16), tiny(16), tiny(48)
        wgr = tiny(KD * 36).rearrange("p (k e) -> p k e", k=KD)
        rbias, dtb, alog, dsk, csil = tiny(36), tiny(SH), tiny(SH), tiny(SH), tiny(KD)
        gss, gms = tiny(8), tiny(8)

        def B(name, *dims):
            a, b = where[name]
            ap = arena[:, a:b]
            if len(dims) == 1:
                return ap.rearrange("p (a b) -> p a b", a=dims[0])
            if len(dims) == 2:
                return ap.rearrange("p (a b c) -> p a b c", a=dims[0], b=dims[1])
            if len(dims) == 3:
                return ap.rearrange("p (a b c d) -> p a b c d", a=dims[0], b=dims[1], c=dims[2])
            return ap

        junk, parrow, cb = B("junk"), B("parrow", NPAR), B("cb", KD)
        g1, g2, wua, gup, npost, fpost, fin = (B(n) for n in ("g1", "g2", "wua", "gup", "npost", "fpost", "fin"))
        xn = [B(f"xn{n}", NT) for n in range(4)]
        osb, gT, bon, tmp, bh, kh, kT, vT, bT = (B(n, 4) for n in ("osb", "gT", "bon", "tmp", "bh", "kh", "kT", "vT", "b"))
        rT, lora, aT, lw, kkT, cum, qk, vtok = (B(n, d) for n, d in (
            ("rT", 4), ("lora", 2), ("a", 4), ("lw", 4), ("kk", 4), ("cum", 4), ("qk", 8), ("v", NT)))
        nmr = B("nmr")
        kr = B("kr", PAIRS, NT, 2)
        az, rz = B("az", HEADS), B("rz", HEADS)
        vp, zb = B("vp", NT, HEADS), B("zb", NT, HEADS)
        btok, ktok, modp = B("btok", NT), B("ktok", NT), B("modp", 2)
        gm, dd, ddT, xx, up, tk = (B(n, HEADS) for n in ("gm", "dd", "ddT", "xx", "up", "tk"))
        phi, psi = B("phi", 2, PAIRS), B("psi", 3, PAIRS)
        ryT, yT, orw, gates = B("ry", PAIRS), B("y", PAIRS), B("orw", PAIRS), B("gates", 16)
        mo, dno, fT, sil = B("mo", NT), B("dno", NT), B("fT", KF), B("sil", 2)
        hi, fh, fT_lo = (rounded(n, sh, "arena", where[b][0]) for n, b, sh in (
            ("high", "hi", [3, SLOT]), ("f_high", "fh", [KF, SEQ]), ("f_low", "fT", [KF, SEQ])))
        hT_hi = {n: rounded(f"h{n}_high", [KD, SEQ], "arena", where[f"hh{n}"][0]) for n in (1, 2)}
        hT_lo, ring_lo = rounded("h_low", [KD, SEQ], "hT"), rounded("ring_low", [RING, SLOT], "ring")
        u, sz, xraw, xs, band = B("u", NT), B("sz", NT), B("xraw", MX), B("xs", MX), B("band", GRP)
        wp, dif = B("wp", 2), B("dif", 2)
        dtr, dtmp, da = (B(n, NT)[:, :, 0:SH] for n in ("dt", "dtmp", "da"))
        acs, ea = B("acs", 3), B("ea", 2)
        dec, cbm = B("dec", NT, SH), B("cbm", NT, GRP)
        xtok, btk, xc, xde, st, yo = B("xtok", NT), B("btk"), B("xc", NT), B("xde"), B("st"), B("yo")
        ys, ysq, mixT, gtmp = B("ys", NT), B("ysq", NT), B("mixT", KD), B("gtmp")
        ew = B("ew", 3)
        sa, ac, acT = B("sa", NT), B("ac", NT), B("acT", NT, KE)
        lg, gate, rs = B("lg", NT), B("gate", NT), B("rs")
        posq, gateq, hg, yslot = B("posq"), B("gateq"), B("hg", KD), B("yslot")
        one, onew, onewT = B("one", 2 * NT), B("onew", 2 * NT), B("onewT")
        rtb = [B("rt", 8)[:, n] for n in range(8)]

        def write(pe, key):
            b, turn = BANK[key]
            if turn:
                pe.wait_ge(bank_free[b], turn)
            return bank[b]

        def full(key):
            return bank_full[BANK[key][0]], 1

        def filled(eng, key):
            b, turn = BANK[key]
            eng.wait_ge(bank_full[b], turn + 1)
            return bank[b]

        def free(key):
            return bank_free[BANK[key][0]], 1

        def drained(eng, key):
            b, turn = BANK[key]
            eng.wait_ge(bank_free[b], turn + 1)

        def cols(w, c0, c1):
            return w[:, c0:c1].rearrange("(k p) c -> p k c", p=P)

        w_in, w_in2 = A["w_in"][0], A["w_in_2"][0]
        W = []

        def stream(key, parts, last):
            W.append((key, parts, last))

        for c in (3, 1, 0, 2):
            a, b = SB_COLS + c * 512, min(SB_COLS + c * 512 + 512, SB_COLS + RW_COLS)
            stream(("rw", c), [(0, cols(w_in, a, b))], ("rw", min(2 * c + 1, 6)))
        for c, last in enumerate((("qk", 1), ("qk", 3), ("v", 1))):
            stream(("sb", c), [(0, cols(w_in, c * 512, c * 512 + 512))], last)
        for c in range(12):
            stream(("ada", c), [(0, cols(A["w_ada_2"][0], c * 512, c * 512 + 512))], ("ad", c))
        for c in range(4):
            a = SB_COLS + RW_COLS + c * 512
            stream(("gate", c), [(0, cols(w_in, a, a + 512))], ("ga", 2 * c + 1))
        stream("sb_out", [(0, cols(A["w_sb_out"][0], 0, D))], ("mg", KD - 1))
        stream("rw_out", [(0, cols(A["w_rw_out"][0], 0, D))], ("mg", KD - 1))
        for n in range(2):
            stream(("wo", n), [(0, cols(A["w_o"][0], n * 512, n * 512 + 512))], ("mo", 1, n))
        for c in range(KF // 2):
            stream(("ff", c), [(0, cols(A["w_ffn_gate"][0], c * 256, c * 256 + 256)),
                               (2048, cols(A["w_ffn_up"][0], c * 256, c * 256 + 256))], ("ff", 2 * c + 1))
        n_down = -(-KF // 4)
        for c in range(n_down):
            r0, r1 = c * 512, min(c * 512 + 512, FF)
            stream(("down", c), [(0, cols(A["w_ffn_down"][0][r0:r1, :], 0, D))],
                   ("dn", 1, 1) if c == n_down - 1 else ("sem", "down_used", c + 1))
        for c in range(6):
            stream(("in2", c), [(0, cols(w_in2, c * 512, min(c * 512 + 512, w_in2.shape[1])))],
                   ("uz", 1, c) if c < 2 else ("xb", 2 * c - 3) if c < 5 else ("dt2",))
        for n in range(2):
            stream(("out2", n), [(0, cols(A["w_out_2"][0], n * 512, n * 512 + 512))], ("mx", 1, n))
        slot_full = [S(f"slot_full{r}") for r in range(RING)]
        SLOTS, loads = {}, [0] * RING
        for n, (key, parts, last) in enumerate(W):
            loads[n % RING] += 16 * len(parts)
            SLOTS[key] = (n % RING, loads[n % RING])

        def slot_view(key, k):
            r = SLOTS[key][0]
            parts = [p for q, p, _ in W if q == key][0]
            w = parts[0][1].shape[2]
            return ring[:, r, 0:k * w].rearrange("p (k c) -> p k c", k=k)

        def arrived(eng, key):
            r, count = SLOTS[key]
            eng.wait_ge(slot_full[r], count)

        SPLIT = [(key, last) for key, _, last in W if key[0] in ("ff", "down", "in2")]
        split_at = {key: n for n, (key, _) in enumerate(SPLIT)}
        BY_TWO = sum(key[0] != "in2" for key, _ in SPLIT)

        def split_words(n):
            key = SPLIT[n][0]
            parts = [p for q, p, _ in W if q == key][0]
            return SLOTS[key][0], sum(src.shape[1] * src.shape[2] for _, src in parts)

        def parts_view(key, pattern, **dims):
            n = split_at[key]
            r, words = split_words(n)
            return [x.rearrange(pattern, **dims) for x in (hi[:, n % 3, 0:words], ring_lo[:, r, 0:words])]

        def low_part(eng, n, c0, c1):
            r, _ = split_words(n)
            return eng.tensor_tensor(ring_lo[:, r, c0:c1], ring[:, r, c0:c1], hi[:, n % 3, c0:c1].bitcast(F32), ALU.subtract)

        def consumed(eng, last):
            if last[0] == "sem":
                eng.wait_ge(S(last[1]), last[2])
            else:
                filled(eng, last)

        EP = EXPERTS // 2
        w13_full = [S(f"w13_full{c}") for c in range(KD // 2)]
        w2_full = [S(f"w2_full{c}") for c in range(KE // 2)]
        base = ring[:, :, :].rearrange("p r w -> p (r w)")
        other = ew.rearrange("p r w -> p (r w)")
        w13s = [x[:, 0:2 * SLOT].rearrange("p (k c) -> p k c", k=KD) for x in (base, other)]
        w2s = [x[:, 2 * SLOT:3 * SLOT].rearrange("p (k c) -> p k c", k=KE) for x in (base, other)]
        w13_d = A["w13_2"][0].rearrange("e (k p) c -> p e k c", p=P)
        w2_d = A["w2_2"][0].rearrange("e (k p) c -> p e k c", p=P)
        x_tok = A["x"][0].rearrange("(i p) d -> p i d", p=P)
        out_tok = out[0].rearrange("(i p) d -> p i d", p=P)

        block = ctx.enter_context(nc.Block())

        @block.sync
        def _(sp):
            sp.dma_start(xres[:, :, :], x_tok).then_inc(S("x_in"), 16)
            sp.dma_start(con[:, :], A["consts"]).then_inc(S("con_in"), 16)
            for t, rows in enumerate(PAR):
                a = 0
                for name, r in rows:
                    src = A[name].rearrange("x y z -> (x y z)") if len(A[name].shape) == 3 else \
                        A[name].rearrange("x y -> (x y)")
                    sp.dma_start(parrow[a:a + r, t, :], src.rearrange("(r c) -> r c", c=P)).then_inc(S("par_in"), 16)
                    a += r
            freed_by = {}
            for n, (key, parts, last) in enumerate(W):
                r = n % RING
                if r in freed_by:
                    consumed(sp, freed_by[r])
                for c0, src in parts:
                    k, w = src.shape[1], src.shape[2]
                    dst = ring[:, r, c0:c0 + k * w].rearrange("p (k c) -> p k c", k=k)
                    sp.dma_start(dst, src).then_inc(slot_full[r], 16)
                freed_by[r] = last

            def load_w13(p, c, x):
                e = p * 2 + x
                sp.dma_start(w13s[x][:, 2 * c:2 * c + 2, :],
                             w13_d[:, bass.ds(e, 1), 2 * c:2 * c + 2, :].rearrange("p e k c -> p (e k) c")
                             ).then_inc(w13_full[c], 16)

            def load_w2(p, c, x):
                e = p * 2 + x
                sp.dma_start(w2s[x][:, 2 * c:2 * c + 2, :],
                             w2_d[:, bass.ds(e, 1), 2 * c:2 * c + 2, :].rearrange("p e k c -> p (e k) c")
                             ).then_inc(w2_full[c], 16)

            sp.wait_ge(S("gms"), 1)
            drained(sp, ("pm",))
            for x in (1, 0):
                if x == 0:
                    for r in range(RING):
                        filled(sp, freed_by[r])
                for c in range(KD // 2):
                    load_w13(0, c, x)
                for c in range(KE // 2):
                    load_w2(0, c, x)
            with sp.Fori(0, EP - 1) as it:
                for c in range(KD // 2):
                    sp.wait_ge(S("w13_used"), it * 4 + (c + 1))
                    for x in range(2):
                        load_w13(it + 1, c, x)
                for c in range(KE // 2):
                    sp.wait_ge(S("w2_used"), it * 2 + (c + 1))
                    for x in range(2):
                        load_w2(it + 1, c, x)
            sp.wait_ge(S("y_out"), NT)
            sp.dma_start(out_tok, xres[:, :, :]).then_inc(S("stored"), 16)
            sp.wait_ge(S("stored"), 16)

        @block.tensor
        def _(pe):
            mm = nc.tensor.matmul
            ident = K("ident")

            def norm_transposes(s):
                for kk in range(4):
                    ps = write(pe, ("hT", s, kk))
                    for k2 in range(2):
                        for i in range(NT):
                            if kk == 0 and k2 == 0:
                                pe.wait_ge(S("xn"), 2 * s + i + 1)
                            k = 2 * kk + k2
                            last = nc.tensor.transpose(ps[:, (k2 * NT + i) * P:(k2 * NT + i + 1) * P],
                                                       xn[s][:, i, k * P:(k + 1) * P], ident)
                    last.then_inc(*full(("hT", s, kk)))

            def normed(s):
                for kk in range(4):
                    drained(pe, ("hT", s, kk))

            def feature_major(key, wkey, m0, m_in_slot):
                ps = write(pe, key)
                w = slot_view(wkey, KD)
                for j in range(2):
                    for k in range(KD):
                        c = (m_in_slot + j) * P
                        last = mm(ps[:, j * SEQ:(j + 1) * SEQ], w[:, k, c:c + P], hT[:, k, :],
                                  start=(k == 0), stop=(k == KD - 1))
                last.then_inc(*full(key))

            def token_major(key, wkey, i, lhs, nk=KD):
                ps = write(pe, key)
                w = slot_view(wkey, nk)
                for k in range(nk):
                    last = mm(ps[:, 0:512], lhs[:, k, i * P:(i + 1) * P], w[:, k, 0:512],
                              start=(k == 0), stop=(k == nk - 1))
                last.then_inc(*full(key))

            def halved(key):
                n = split_at[key]
                pe.wait_ge(S("low"), n + 1)
                if n < BY_TWO:
                    pe.wait_ge(S("low2"), n + 1)

            def by_parts(ps, a, b, start, stop):
                mm(ps, a[0], b[0], start=start, stop=False)
                mm(ps, a[0], b[1], start=False, stop=False)
                return mm(ps, a[1], b[0], start=False, stop=stop)

            pe.wait_ge(S("con_in"), 16)
            pe.wait_ge(S("par_in"), 16 * sum(len(x) for x in PAR))
            for t, rows in enumerate(PAR):
                n = sum(r for _, r in rows)
                ps = write(pe, ("par", t))
                nc.tensor.transpose(ps[:, 0:n], parrow[0:n, t, :], ident[0:n, 0:n]).then_inc(*full(("par", t)))

            norm_transposes(0)
            normed(0)
            for j in RW_ORDER:
                c = j // 2
                arrived(pe, ("rw", c))
                feature_major(("rw", j), ("rw", c), 2 * j, 2 * (j % 2) if c < 3 else 0)
            pe.wait_ge(S("small_in"), 16 * 3)
            for key, lo, hi, part, wt in (("lw", 0, 64, 0, wua), ("la", 64, 128, 0, wua), ("lg", 0, 128, 1, gup)):
                if key == "la":
                    drained(pe, ("rw", 6))
                else:
                    pe.wait_ge(S("lora"), 1 + part)
                for j in range(2):
                    ps = write(pe, (key, j))
                    for h in range(2):
                        mt = 2 * j + h
                        last = mm(ps[:, h * SEQ:(h + 1) * SEQ], wt[lo:hi, mt * P:(mt + 1) * P], lora[lo:hi, part, :],
                                  start=True, stop=True)
                    last.then_inc(*full((key, j)))
            for j in range(4):
                arrived(pe, ("sb", j // 2))
                feature_major(("qk", j), ("sb", j // 2), 2 * j, 2 * (j % 2))
            arrived(pe, ("sb", 2))
            for i in range(NT):
                token_major(("v", i), ("sb", 2), i, hT)
            pe.wait_ge(S("kk_sq"), 1)
            ps = write(pe, ("kn",))
            for p in range(PAIRS):
                last = mm(ps[0:HEADS, 0:SEQ], K("head_sum")[:, p * HEADS:(p + 1) * HEADS], tmp[:, p, :],
                          start=(p == 0), stop=(p == PAIRS - 1))
            last.then_inc(*full(("kn",)))

            def spread(name, sem):
                pe.wait_ge(S(sem), 1)
                for j in range(2):
                    ps = write(pe, (name, j))
                    for h in range(2):
                        p = 2 * j + h
                        last = mm(ps[:, h * SEQ:(h + 1) * SEQ], K("head_spread")[0:HEADS, p * P:(p + 1) * P],
                                  nmr[0:HEADS, :], start=True, stop=True)
                    last.then_inc(*full((name, j)))

            spread("kb", "kk_inv")

            def scores(ps, h, alone):
                o = DH * (h % 2)
                q, k = qk[o:o + DH, h // 2, :], qk[o:o + DH, PAIRS + h // 2, :]
                mm(ps[:, 0:SEQ], k[:, 0:P], q, start=True, stop=alone, skip_group_check=True)
                return mm(ps[:, SEQ:SEQ + P], k[:, P:SEQ], q[:, P:SEQ], start=alone, stop=alone, skip_group_check=True)

            for j in range(4):
                drained(pe, ("qk", j))
            for h in range(HEADS):
                ps = write(pe, ("z", h))
                scores(ps, h, True).then_inc(*full(("z", h)))
            pe.wait_ge(S("bon_raw"), 1)
            for j in range(2):
                ps = write(pe, ("bn", j))
                for h in range(2):
                    last = mm(ps[:, h * SEQ:(h + 1) * SEQ], K("head_block"), bon[:, 2 * j + h, :], start=True, stop=True)
                last.then_inc(*full(("bn", j)))
            for h in range(HEADS):
                pe.wait_ge(S("att_sp"), h // 4 + 1)
                ps = write(pe, ("l", h))
                scores(ps, h, False)
                mm(ps[:, 0:SEQ], K("neg_suffix"), rz[:, h, 0:SEQ], start=False, stop=False, skip_group_check=True)
                mm(ps[:, P:SEQ], K("neg_ones"), rz[:, h, SEQ:SEQ + P], start=False, stop=False, skip_group_check=True)
                mm(ps[:, SEQ:SEQ + P], K("neg_suffix"), rz[:, h, SEQ:SEQ + P], start=False, stop=True,
                   skip_group_check=True).then_inc(*full(("l", h)))
            for i in range(NT):
                drained(pe, ("v", i))
            for p in range(PAIRS):
                pe.wait_ge(S("att_w"), p // 2 + 1)
                ps = write(pe, ("o", p))
                for h in range(2):
                    d = DH * h
                    n = 2 * p + h
                    mm(ps[d:d + DH, 0:SEQ], vtok[:, 0, n * DH:(n + 1) * DH], az[:, n, 0:SEQ], start=True, stop=False,
                       skip_group_check=True)
                    last = mm(ps[d:d + DH, P:SEQ], vtok[:, 1, n * DH:(n + 1) * DH], az[:, n, SEQ:SEQ + P],
                              start=False, stop=True, skip_group_check=True)
                last.then_inc(*full(("o", p)))

            pe.wait_ge(S("kr_k"), 1)
            pe.wait_ge(S("bk_bar"), 1)
            for i in range(NT):
                for a in range(4):
                    ps = write(pe, ("tok", i, a))
                    for p in range(PAIRS):
                        t = slice(i * P, (i + 1) * P)
                        src = (kr[:, p, i, 0, :], bT[:, p, t], kT[:, p, t], vT[:, p, t])[a]
                        last = nc.tensor.transpose(ps[:, p * P:(p + 1) * P], src, ident)
                    last.then_inc(*full(("tok", i, a)))

            def ada_sum(c):
                drained(pe, ("ad", c))
                ps = write(pe, ("as", c))
                if c in COLUMN_CHUNKS:
                    for j in range(4):
                        last = mm(ps[:, j:j + 1], modp[:, c % 2, j * P:(j + 1) * P], K("thirty_second")[:, 0:1],
                                  start=True, stop=True)
                else:
                    last = mm(ps[:, 0:512], K("thirty_second"), modp[:, c % 2, :], start=True, stop=True)
                last.then_inc(*full(("as", c)))

            def ada(c):
                if c:
                    ada_sum(c - 1)
                arrived(pe, ("ada", c))
                pe.wait_ge(S("cb"), 1)
                ps = write(pe, ("ad", c))
                w = slot_view(("ada", c), KD)
                for kk in range(2):
                    for j in range(4):
                        k = 2 * j + kk
                        last = mm(ps[32 * j:32 * j + 32, 0:512], cb[:, k, :], w[:, k, :], start=(kk == 0),
                                  stop=(kk == 1))
                last.then_inc(*full(("ad", c)))

            pe.wait_ge(S("bk_hat"), 1)
            pe.wait_ge(S("kr_r"), 1)
            chunk = 0
            for i in range(NT):
                for h in range(HEADS):
                    o, p = DH * (h % 2), h // 2
                    ps = write(pe, ("g", i, h))
                    right = kr[o:o + DH, p, i, :, :].rearrange("p s t -> p (s t)")
                    mm(ps[:, 0:2 * P], bh[o:o + DH, p, i * P:(i + 1) * P], right, start=True, stop=True)
                    mm(ps[:, 2 * P:4 * P], kh[o:o + DH, p, i * P:(i + 1) * P], right, start=True,
                       stop=True).then_inc(*full(("g", i, h)))

                def group(key, q, left, right):
                    ps = write(pe, key)
                    for j in range(4):
                        last = mm(ps[:, j * P:(j + 1) * P], left(4 * q + j), right(4 * q + j), start=True, stop=True)
                    last.then_inc(*full(key))

                for q in range(2):
                    for h in range(4):
                        drained(pe, ("g", i, 4 * q + h))
                    group(("n", i, q), q, lambda h: gm[:, h, 0:P], lambda h: ident)
                for lv in range(1, LEVELS):
                    for q in range(2):
                        if lv == 1:
                            drained(pe, ("n", i, q))
                            pe.wait_ge(S("dt_first"), 2 * i + q + 1)
                        else:
                            drained(pe, ("d", i, lv - 1, q))
                            drained(pe, ("dt", i, lv - 1, q))
                        group(("x", i, lv, q), q, lambda h: gm[:, h, 0:P], lambda h: dd[:, h, :])
                    ada(chunk)
                    chunk += 1
                    for q in range(2):
                        drained(pe, ("x", i, lv, q))
                        if lv < LEVELS - 1:
                            group(("d", i, lv, q), q, lambda h: ddT[:, h, :], lambda h: xx[:, h, :])
                        group(("dt", i, lv, q), q, lambda h: xx[:, h, :], lambda h: ddT[:, h, :])
                for a in range(4):
                    drained(pe, ("tok", i, a))
                for q in range(2):
                    group(("w1", i, q), q, lambda h: gm[:, h, 2 * P:3 * P], lambda h: vp[:, i, h, :])
                ada(chunk)
                chunk += 1
                for q in range(2):
                    drained(pe, ("w1", i, q))
                    drained(pe, ("dt", i, LEVELS - 1, q))
                    group(("u", i, q), q, lambda h: ddT[:, h, :], lambda h: zb[:, i, h, :])
                for q in range(2):
                    drained(pe, ("u", i, q))
                ps = write(pe, ("ry", i))
                for h in range(HEADS):
                    o, p = DH * (h % 2), h // 2
                    last = mm(ps[o:o + DH, p * P:(p + 1) * P], tk[:, h, :], gm[:, h, P:2 * P], start=True, stop=True)
                last.then_inc(*full(("ry", i)))

                def psi_of(c):
                    r = slice(CH * (c % 2), CH * (c % 2) + CH)
                    ps = write(pe, ("psi", c))
                    for p in range(PAIRS):
                        f = slice(p * P, (p + 1) * P)
                        mm(ps[:, f], btok[r, i, f], up[r, 2 * p:2 * p + 2, :].rearrange("p h d -> p (h d)"),
                           start=True, stop=False)
                        last = mm(ps[:, f], ktok[r, i, f], vp[r, i, 2 * p:2 * p + 2, 0:DH], start=False, stop=True)
                    last.then_inc(*full(("psi", c)))

                def phi_of(c):
                    r = slice(CH * (c % 2), CH * (c % 2) + CH)
                    ps = write(pe, ("phi", c))
                    for p in range(PAIRS):
                        f = slice(p * P, (p + 1) * P)
                        last = mm(ps[:, f], tk[r, 2 * p:2 * p + 2, :].rearrange("p h d -> p (h d)"), btok[r, i, f],
                                  start=True, stop=True)
                    last.then_inc(*full(("phi", c)))

                def state(c):
                    drained(pe, ("s", c - 1) if c > 1 else ("psi", 0))
                    drained(pe, ("psi", c))
                    pe.wait_ge(S("phi"), c)
                    ps = write(pe, ("s", c))
                    for p in range(PAIRS):
                        last = mm(ps[:, p * P:(p + 1) * P], phi[:, c - 1, p, :], psi[:, c - 1, p, :], start=True, stop=True)
                    last.then_inc(*full(("s", c)))

                def y_of():
                    ps = write(pe, ("y", i))
                    for h in range(HEADS):
                        o, p = DH * (h % 2), h // 2
                        dst = ps[o:o + DH, p * P:(p + 1) * P]
                        mm(dst, up[:, h, :], gm[:, h, P:2 * P], start=(p == 0), stop=False, skip_group_check=True)
                        mm(dst, vp[:, i, h, 0:DH], gm[:, h, 3 * P:4 * P], start=False, stop=False, skip_group_check=True)
                    drained(pe, ("ry", i))
                    for c in (2 * i, 2 * i + 1):
                        if c == 0:
                            continue
                        drained(pe, ("psi", 0) if c == 1 else ("s", c - 1))
                        for p in range(PAIRS):
                            t = slice(p * P + CH * (c % 2), p * P + CH * (c % 2) + CH)
                            last = mm(ps[:, t], psi[:, c - 1, p, :], ryT[:, p, c * CH:(c + 1) * CH], start=False,
                                      stop=True, skip_group_check=True)
                    last.then_inc(*full(("y", i)))

                if i == 0:
                    psi_of(0)
                    psi_of(1)
                    phi_of(1)
                    y_of()
                    state(1)
                else:
                    psi_of(2)
                    phi_of(2)
                    state(2)
                    y_of()
            ada_sum(11)

            def gates_of(j):
                arrived(pe, ("gate", j // 2))
                feature_major(("ga", j), ("gate", j // 2), 2 * j, 2 * (j % 2))

            gates_of(0)
            gates_of(1)
            for i in range(NT):
                drained(pe, ("y", i))
            for j in range(2):
                ps = write(pe, ("m", j))
                for h in range(2):
                    last = mm(ps[:, h * SEQ:(h + 1) * SEQ], K("head_mean"), yT[:, 2 * j + h, :], start=True, stop=True)
                last.then_inc(*full(("m", j)))
            for j in range(2, 5):
                gates_of(j)
            pe.wait_ge(S("y_sq"), 1)
            ps = write(pe, ("vn",))
            for p in range(PAIRS):
                last = mm(ps[0:HEADS, 0:SEQ], K("head_sum")[:, p * HEADS:(p + 1) * HEADS], tmp[:, p, :],
                          start=(p == 0), stop=(p == PAIRS - 1))
            last.then_inc(*full(("vn",)))
            for j in range(5, 8):
                gates_of(j)
            spread("vb", "y_inv")
            arrived(pe, "sb_out")
            arrived(pe, "rw_out")
            for p in range(PAIRS):
                drained(pe, ("o", p))
            pe.wait_ge(S("orw"), 1)
            for dm in range(KD):
                ps = write(pe, ("mg", dm))
                for half, wkey, src in ((0, "sb_out", osb), (1, "rw_out", orw)):
                    w = slot_view(wkey, PAIRS)
                    for k in range(PAIRS):
                        last = mm(ps[:, half * SEQ:(half + 1) * SEQ], w[:, k, dm * P:(dm + 1) * P], src[:, k, :],
                                  start=(k == 0), stop=(k == PAIRS - 1))
                last.then_inc(*full(("mg", dm)))
            pe.wait_ge(S("merged"), KD)
            for n in range(2):
                arrived(pe, ("wo", n))
                for i in range(NT):
                    token_major(("mo", i, n), ("wo", n), i, gates)
            norm_transposes(1)
            normed(1)
            for f in range(KF):
                c = f // 2
                halved(("ff", c))
                ps = write(pe, ("ff", f))
                w = parts_view(("ff", c), "p (g k c) -> p g k c", g=2, k=KD)
                for gu in range(2):
                    for k in range(KD):
                        last = by_parts(ps[:, gu * SEQ:(gu + 1) * SEQ], [x[:, gu, k, (f % 2) * P:(f % 2 + 1) * P] for x in w],
                                        (hT_hi[1][:, k, :], hT_lo[:, k, :]), k == 0, k == KD - 1)
                last.then_inc(*full(("ff", f)))
            ps = {}
            for n in range(2):
                for i in range(NT):
                    ps[i, n] = write(pe, ("dn", i, n))
            for c in range(n_down):
                halved(("down", c))
                nk = min(4, KF - 4 * c)
                w = parts_view(("down", c), "p (k c) -> p k c", k=nk)
                for kk in range(nk):
                    k = 4 * c + kk
                    pe.wait_ge(S("f_low"), k // 2 + 1)
                    for n in range(2):
                        for i in range(NT):
                            last = by_parts(ps[i, n][:, 0:512], [x[:, k, i * P:(i + 1) * P] for x in (fh, fT_lo)],
                                            [x[:, kk, n * 512:(n + 1) * 512] for x in w], k == 0, k == KF - 1)
                            if k == KF - 1:
                                last.then_inc(*full(("dn", i, n)))
                if c < n_down - 1:
                    last.then_inc(S("down_used"), 1)

            norm_transposes(2)
            normed(2)
            for n in range(2):
                halved(("in2", n))
                w = parts_view(("in2", n), "p (k c) -> p k c", k=KD)
                for i in range(NT):
                    ps = write(pe, ("uz", i, n))
                    for k in range(KD):
                        last = by_parts(ps[:, 0:512], [x[:, k, i * P:(i + 1) * P] for x in (hT_hi[2], hT_lo)],
                                        [x[:, k, :] for x in w], k == 0, k == KD - 1)
                    last.then_inc(*full(("uz", i, n)))
            for j in range(7):
                c = 2 + j // 2
                halved(("in2", c))
                w = parts_view(("in2", c), "p (k c) -> p k c", k=KD)
                ps = write(pe, ("xb", j))
                for h in range(2):
                    m = 2 * (j % 2) + h
                    for k in range(KD):
                        last = by_parts(ps[:, h * SEQ:(h + 1) * SEQ], [x[:, k, m * P:(m + 1) * P] for x in w],
                                        (hT_hi[2][:, k, :], hT_lo[:, k, :]), k == 0, k == KD - 1)
                last.then_inc(*full(("xb", j)))
            ps = write(pe, ("dt2",))
            for i in range(NT):
                for k in range(KD):
                    last = by_parts(ps[:, i * 16:i * 16 + SH], [x[:, k, i * P:(i + 1) * P] for x in (hT_hi[2], hT_lo)],
                                    [x[:, k, 256:256 + SH] for x in w], k == 0, k == KD - 1)
            last.then_inc(*full(("dt2",)))
            pe.wait_ge(S("pool_in"), 16 * 5)
            for i in range(NT):
                drained(pe, ("uz", i, 0))
            ps = write(pe, ("pl",))
            for g in range(GRP):
                o, c0 = 64 * (g % 2), SEQ * (g // 2)
                mm(ps[o:o + 64, c0:c0 + SEQ], u[:, 0, g * 64:(g + 1) * 64], band[:, g, 0:SEQ], start=(g < 2), stop=False,
                   skip_group_check=True)
                last = mm(ps[o:o + 64, c0 + P:c0 + SEQ], u[:, 1, g * 64:(g + 1) * 64], band[:, g, SEQ:SEQ + P],
                          start=False, stop=True, skip_group_check=True)
            last.then_inc(*full(("pl",)))
            pe.wait_ge(S("da"), 1)
            ps = write(pe, ("cs",))
            for i in range(NT):
                mm(ps[:, i * 16:i * 16 + SH], K("causal"), da[:, i, :], start=True, stop=True)
            mm(ps[:, 32:32 + SH], K("after"), da[:, 0, :], start=True, stop=True).then_inc(*full(("cs",)))
            drained(pe, ("pl",))
            ps = write(pe, ("pm",))
            for g in range(GRP):
                o, c0 = 64 * (g % 2), SEQ * (g // 2)
                last = mm(ps[o:o + 64, c0:c0 + SEQ], wp[o:o + 64, g // 2, :], dif[o:o + 64, g // 2, :], start=True,
                          stop=True)
            last.then_inc(*full(("pm",)))
            for i in range(NT):
                for q in range(3):
                    ps = write(pe, ("rb", i, q))
                    for j in range(4):
                        last = mm(ps[:, j * P:(j + 1) * P], da[:, i, 4 * q + j:4 * q + j + 1].to_broadcast([P, P]),
                                  K("causal"), start=True, stop=True)
                    last.then_inc(*full(("rb", i, q)))
            pe.wait_ge(S("xs"), 7)
            for i in range(NT):
                ps = write(pe, ("cb", i))
                for g in range(GRP):
                    t = slice(i * P, (i + 1) * P)
                    last = mm(ps[:, g * P:(g + 1) * P], xs[:, 6 + g, t], xs[:, 10 + g, t], start=True, stop=True)
                last.then_inc(*full(("cb", i)))

            def transposes(key, pairs):
                ps = write(pe, key)
                for c, src in pairs:
                    last = nc.tensor.transpose(ps[:, c * P:(c + 1) * P], src, ident)
                last.then_inc(*full(key))

            for i in range(NT):
                for a in range(2):
                    transposes(("xt", i, a), [(c, xs[:, 4 * a + c, i * P:(i + 1) * P]) for c in range(4 if a == 0 else 2)])
            transposes(("bt",), [(g, xs[:, 6 + g, 0:P]) for g in range(GRP)])

            def y_diag(i):
                pe.wait_ge(S("dec"), i + 1)
                pe.wait_ge(S("xc"), i + 1)
                for a in range(2):
                    ps = write(pe, ("yd", i, a))
                    for h in range(8 * a, min(8 * a + 8, SH)):
                        c = (h - 8 * a) * DH
                        last = mm(ps[:, c:c + DH], dec[:, i, h, :], xc[:, i, h * DH:(h + 1) * DH], start=True, stop=True)
                    last.then_inc(*full(("yd", i, a)))

            GW = SR * DH
            y_diag(0)
            pe.wait_ge(S("xde"), 1)
            drained(pe, ("bt",))
            for a in range(2):
                ps = write(pe, ("cst", a))
                for g in range(2 * a, 2 * a + 2):
                    c = (g - 2 * a) * GW
                    last = mm(ps[:, c:c + GW], btk[:, g * P:(g + 1) * P], xde[:, g * GW:(g + 1) * GW], start=True, stop=True)
                last.then_inc(*full(("cst", a)))
            y_diag(1)
            for a in range(2):
                drained(pe, ("cst", a))
                ps = write(pe, ("yo", a))
                for g in range(2 * a, 2 * a + 2):
                    c = (g - 2 * a) * GW
                    last = mm(ps[:, c:c + GW], xs[:, 10 + g, P:SEQ], st[:, g * GW:(g + 1) * GW], start=True, stop=True)
                last.then_inc(*full(("yo", a)))
            for i in range(NT):
                pe.wait_ge(S("ys"), i + 1)
                for a in range(2):
                    transposes(("mt", i, a), [(c, ys[:, i, (4 * a + c) * P:(4 * a + c + 1) * P])
                                              for c in range(4 if a == 0 else 2)])
            drained(pe, ("pm",))
            for i in range(NT):
                for a in range(2):
                    drained(pe, ("mt", i, a))
            for n in range(2):
                arrived(pe, ("out2", n))
                for i in range(NT):
                    token_major(("mx", i, n), ("out2", n), i, mixT)
            norm_transposes(3)
            normed(3)
            pe.wait_ge(S("router_in"), 16 * 4)
            ps = write(pe, ("rt",))
            for i in range(NT):
                for k in range(KD):
                    last = mm(ps[:, i * 64:i * 64 + 36], hT[:, k, i * P:(i + 1) * P], wgr[:, k, :], start=(k == 0),
                              stop=(k == KD - 1))
            last.then_inc(*full(("rt",)))

            pe.wait_ge(S("chosen"), 1)
            ps = write(pe, ("rk",))
            sel = rtb[4][:, 0:NT * EXPERTS].rearrange("p (i c) -> p i c", i=NT)
            for n, terms in enumerate(((("strict", 0),), (("ones", 0), ("strict", 1)), (("ones", 0), ("ones", 1)))):
                for j, (name, i) in enumerate(terms):
                    last = mm(ps[:, n * EXPERTS:(n + 1) * EXPERTS], K(name), sel[:, i, :], start=(j == 0),
                              stop=(j == len(terms) - 1))
            last.then_inc(*full(("rk",)))

            for b in range(8):
                uses = max(t for bb, t in BANK.values() if bb == b) + 1
                pe.wait_ge(bank_free[b], uses)
            pe.wait_ge(S("zero"), 1)
            for b in range(4):
                mm(bank[b][:, 0:512], rs[0:1, 0:1].to_broadcast([1, P]), junk[0:1, 0:512], start=True, stop=False,
                   skip_group_check=True)

            def gather(p):
                pe.wait_ge(S("one"), p + 1)
                if not isinstance(p, int) or p > 1:
                    pe.wait_ge(S("y_slots"), p * 2 - 2)
                for k in range(KD):
                    for i in range(NT):
                        last = mm(bank[4 + k // 4][:, (k % 4) * P:(k % 4 + 1) * P], xn[3][:, i, k * P:(k + 1) * P],
                                  one[:, 2 * i:2 * i + 2, :].rearrange("p x s -> p (x s)"), start=(i == 0), stop=(i == NT - 1))
                    if k % 4 == 3:
                        last.then_inc(S("gathered"), 1)

            def both(b, x):
                return bank[b][x * CAP:(x + 1) * CAP, 0:512]

            def hidden(p):
                pe.wait_ge(S("hg"), p * 2 + 2)
                if not isinstance(p, int) or p > 0:
                    pe.wait_ge(S("ac_turned"), p)
                    pe.wait_ge(S("w_turned"), p)
                for c in range(KD // 2):
                    pe.wait_ge(w13_full[c], p * 32 + 32)
                    for k in (2 * c, 2 * c + 1):
                        for half in range(2):
                            for x in range(2):
                                last = mm(both(6 + half, x), hg[:, k, x * CAP:(x + 1) * CAP],
                                          w13s[x][:, k, half * EF:(half + 1) * EF], start=(k == 0), stop=(k == KD - 1))
                    last.then_inc(S("w13_used"), 1)

            def turn_ac(p):
                pe.wait_ge(S("ac"), p + 1)
                for f in range(KE):
                    last = nc.tensor.transpose(bank[6][:, f * P:(f + 1) * P], ac[:, 0, f * P:(f + 1) * P], ident)
                last.then_inc(S("turns"), 1)

            def turn_weights(p):
                pe.wait_ge(S("onew"), p + 1)
                for i in range(NT):
                    last = nc.tensor.transpose(bank[7][:, i * P:(i + 1) * P],
                                               onew[:, 2 * i:2 * i + 2, :].rearrange("p x s -> p (x s)"), ident)
                last.then_inc(S("w_turns"), 1)

            def expert_out(p):
                pe.wait_ge(S("ac_turned"), p + 1)
                pe.wait_ge(S("hg"), p * 2 + 4 if not isinstance(p, int) or p < EP - 1 else 2 * EP)
                for c in range(KE // 2):
                    pe.wait_ge(w2_full[c], p * 32 + 32)
                    for f in (2 * c, 2 * c + 1):
                        for n in range(2):
                            for x in range(2):
                                last = mm(both(4 + n, x), acT[:, 0, f, x * CAP:(x + 1) * CAP],
                                          w2s[x][:, f, n * 512:(n + 1) * 512], start=(f == 0), stop=(f == KE - 1))
                    last.then_inc(S("w2_used"), 1)

            def combine(p):
                pe.wait_ge(S("y_slots"), p * 2 + 2)
                pe.wait_ge(S("w_turned"), p + 1)
                for i in range(NT):
                    for n in range(2):
                        last = mm(bank[2 * i + n][:, 0:512], onewT[:, i * P:(i + 1) * P], yslot[:, n * 512:(n + 1) * 512],
                                  start=False, stop=False, skip_group_check=True)
                last.then_inc(S("combined"), 1)

            pe.wait_ge(S("crowded"), 1)
            many = pe.value_load(crowded[0:1, 0:1])
            with pe.If(many > 0):
                with pe.Fori(0, EP) as it:
                    for c in range(KD // 2):
                        pe.wait_ge(w13_full[c], it * 32 + 32)
                    for x in range(2):
                        for i in range(NT):
                            for half in range(2):
                                for k in range(KD):
                                    last = mm(bank[4 + 2 * i + half][:, 0:512], hT[:, k, i * P:(i + 1) * P],
                                              w13s[x][:, k, half * EF:(half + 1) * EF], start=(k == 0), stop=(k == KD - 1))
                                last.then_inc(S("hidden"), 1)
                        for i in range(NT):
                            pe.wait_ge(S("act_out"), it * 4 + (2 * x + i + 1))
                            for f in range(KE):
                                last = nc.tensor.transpose(bank[4 + 2 * i][:, f * P:(f + 1) * P],
                                                           ac[:, i, f * P:(f + 1) * P], ident)
                            last.then_inc(S("turns"), 1)
                        for c in range(KE // 2):
                            pe.wait_ge(w2_full[c], it * 32 + 32)
                        for i in range(NT):
                            pe.wait_ge(S("turned"), it * 4 + (2 * x + i + 1))
                            for n in range(2):
                                for f in range(KE):
                                    last = mm(bank[2 * i + n][:, 0:512], acT[:, i, f, :], w2s[x][:, f, n * 512:(n + 1) * 512],
                                              start=False, stop=False, skip_group_check=True)
                            if x == 1:
                                last.then_inc(*((S("w13_used"), 4) if i == 0 else (S("w2_used"), 2)))
            with pe.Else():
                gather(0)
                hidden(0)
                gather(1)
                turn_ac(0)
                turn_weights(0)
                expert_out(0)
                with pe.Fori(1, EP - 1) as it:
                    hidden(it)
                    gather(it + 1)
                    turn_ac(it)
                    combine(it - 1)
                    turn_weights(it)
                    expert_out(it)
                hidden(EP - 1)
                turn_ac(EP - 1)
                combine(EP - 2)
                turn_weights(EP - 1)
                expert_out(EP - 1)
                combine(EP - 1)

        @block.scalar
        def _(act):
            A_ = nc.scalar.activation

            def bcast(dst, src, n):
                return act.dma_start(dst, src.partition_broadcast(P)).then_inc(S(n), 16)

            act.dma_start(B("lvlf"), A["levels"]).then_inc(S("lvl_in"), 16)
            act.dma_start(wua[0:64, :], A["w_up"][0]).then_inc(S("small_in"), 16)
            act.dma_start(wua[64:128, :], A["a_up"][0]).then_inc(S("small_in"), 16)
            act.dma_start(gup[:, :], A["g_up"][0]).then_inc(S("small_in"), 16)
            bcast(g1, A["b_ada_2"][0, 2 * D:3 * D], "gate_in")
            bcast(g2, A["b_ada_2"][0, 5 * D:6 * D], "gate_in")
            bcast(dtb, A["dt_bias_2"][0], "router_in")
            act.dma_start(wgr[:, :, 0:EG], A["w_group_2"][0].rearrange("(k p) c -> p k c", p=P)).then_inc(S("router_in"), 16)
            act.dma_start(wgr[:, :, EG:36], A["w_router_2"][0].rearrange("(k p) c -> p k c", p=P)).then_inc(S("router_in"), 16)
            bcast(rbias[:, 0:EG], A["b_group_2"][0], "router_in")
            bcast(rbias[:, EG:36], A["b_router_2"][0], "par2_in")
            bcast(alog, A["a_log_2"][0], "par2_in")
            bcast(dsk, A["d_skip_2"][0], "par2_in")

            squares = [0]

            def next_square():
                if squares[0]:
                    act.wait_ge(S("sq"), squares[0])
                squares[0] += 1

            def pre_norm(n, ready):
                for i in range(NT):
                    ready(i)
                    next_square()
                    A_(junk, xres[:, i, :], ACT.Square, accum_out=ss[n][:, i:i + 1]).then_inc(S("sq"), 1)

            def root(n):
                act.wait_ge(S("ms"), n + 1)
                A_(sd[n][:, 0:NT], ms[n][:, 0:NT], ACT.Sqrt).then_inc(S("sd"), 1)

            def transposed(s, scale, bias):
                for kk in (0, 2):
                    ps = filled(act, ("hT", s, kk))
                    for k2 in range(2):
                        k = 2 * kk + k2
                        kw = {"bias": bias(k)} if bias else {}
                        ins = A_(hT[:, k, :], ps[:, k2 * SEQ:(k2 + 1) * SEQ], ACT.Identity, scale=scale(k), **kw)
                    ins.then_inc(*free(("hT", s, kk)))

            def post_norm(n, name):
                for j in range(4):
                    half, i = j // 2, j % 2
                    ps = filled(act, (name, i, half))
                    next_square()
                    A_(junk[:, 0:512], ps[:, :], ACT.Square, accum_out=ss[n][:, 2 * i + half:2 * i + half + 1]
                       ).then_inc(S("sq"), 1)
                root(n)

            def high_parts(n):
                arrived(act, SPLIT[n][0])
                if n >= 3:
                    consumed(act, SPLIT[n - 3][1])
                r, words = split_words(n)
                for a in range(2):
                    f = slice(a * words // 2, (a + 1) * words // 2)
                    A_(hi[:, n % 3, f], ring[:, r, f], ACT.Copy).then_inc(S("high"), 1)

            def transposed_high(s, scale, bias):
                for kk in range(4):
                    ps = filled(act, ("hT", s, kk))
                    for k2 in range(2):
                        k = 2 * kk + k2
                        kw = {"bias": bias(k)} if bias else {}
                        ins = A_(hT_hi[s][:, k, :], ps[:, k2 * SEQ:(k2 + 1) * SEQ], ACT.Identity, scale=scale(k), **kw)
                    ins.then_inc(S("h_high"), 1)

            pre_norm(0, lambda i: act.wait_ge(S("x_in"), 16))
            root(0)
            drained(act, ("par", 0))
            transposed(0, lambda k: par("norm_mix_pre", k), None)
            drained(act, ("par", 1))
            act.wait_ge(S("omu"), 1)

            def shifted(m):
                if m < 4:
                    return rT[:, m, :]
                if m < 8:
                    return kT[:, m - 4, :]
                return vT[:, m - 8, :] if m < 12 else lora[:, m - 12, :]

            for j in RW_ORDER:
                ps = filled(act, ("rw", j))
                for h in range(2):
                    ins = A_(shifted(2 * j + h), ps[:, h * SEQ:(h + 1) * SEQ], ACT.Identity, scale=omu[:, 2 * j + h:2 * j + h + 1])
                ins.then_inc(S("rw_own"), 1)
            drained(act, ("rw", 6))
            A_(lora[0:64, 0, :], lora[0:64, 0, :], ACT.Tanh).then_inc(S("lora"), 1)
            A_(lora[:, 1, :], lora[:, 1, :], ACT.Sigmoid).then_inc(S("lora"), 1)
            for key, dst, bias in (("lw", lw, "w0"), ("la", aT, "a0")):
                for j in range(2):
                    ps = filled(act, (key, j))
                    for h in range(2):
                        ins = A_(dst[:, 2 * j + h, :], ps[:, h * SEQ:(h + 1) * SEQ], ACT.Sigmoid, bias=par(bias, 2 * j + h))
                    ins.then_inc(*free((key, j)))
            for j in range(2):
                ps = filled(act, ("lg", j))
                A_(gT[:, 2 * j:2 * j + 2, :].rearrange("p a b -> p (a b)"), ps[:, :], ACT.Copy).then_inc(*free(("lg", j)))
            act.wait_ge(S("kk_raw"), 1)
            A_(tmp, kkT, ACT.Square).then_inc(S("kk_sq"), 1)
            for j in range(2):
                ps = filled(act, ("qk", j))
                A_(qk[:, 2 * j:2 * j + 2, :].rearrange("p a b -> p (a b)"), ps[:, :], ACT.Copy, scale=DH ** -0.5
                   ).then_inc(*free(("qk", j)))
            ps = filled(act, ("kn",))
            A_(nmr[0:HEADS, :], ps[0:HEADS, 0:SEQ], ACT.Sqrt).then_inc(*free(("kn",)))
            A_(csil, par("c_2", 0, KD), ACT.Silu).then_inc(S("csil"), 1)
            act.wait_ge(S("ex"), 1)
            A_(aT, cum, ACT.Exp, scale=DECAY).then_inc(S("e_inc"), 1)
            A_(lw, lw, ACT.Exp, scale=DECAY).then_inc(S("e_exc"), 1)
            A_(tmp, cum, ACT.Exp, scale=-DECAY).then_inc(S("e_inv"), 1)
            A_(pc, total, ACT.Exp, scale=DECAY).then_inc(S("pc"), 1)
            for half in range(2):
                for h in range(4):
                    drained(act, ("z", 4 * half + h))
                A_(az[:, 4 * half:4 * half + 4, :], az[:, 4 * half:4 * half + 4, :], ACT.Exp).then_inc(S("att_e"), 1)
            act.wait_ge(S("to_end"), 1)
            A_(cum, cum, ACT.Exp, scale=DECAY).then_inc(S("e_suf"), 1)
            for half in range(2):
                act.wait_ge(S("att_e"), half + 1)
                A_(az[:, 4 * half:4 * half + 4, :], az[:, 4 * half:4 * half + 4, :], ACT.Ln, bias=1.0).then_inc(S("att_ln"), 1)
            for half in range(2):
                for h in range(4):
                    drained(act, ("l", 4 * half + h))
                A_(az[:, 4 * half:4 * half + 4, :], az[:, 4 * half:4 * half + 4, :], ACT.Exp).then_inc(S("att_x"), 1)
            for p in range(PAIRS):
                ps = filled(act, ("o", p))
                A_(osb[:, p, :], ps[:, 0:SEQ], ACT.Copy).then_inc(*free(("o", p)))
            for i in range(NT):
                ps = filled(act, ("tok", i, 0))
                A_(zb[:, i, :, DH:P], ps[:, :].rearrange("p (h d) -> p h d", h=HEADS), ACT.Copy).then_inc(*free(("tok", i, 0)))
                ps = filled(act, ("tok", i, 1))
                A_(btok[:, i, :], ps[:, :], ACT.Copy).then_inc(*free(("tok", i, 1)))

            def ada_rows(c):
                ps = filled(act, ("ad", c))
                A_(modp[:, c % 2, :], ps[:, :], ACT.Copy).then_inc(*free(("ad", c)))

            c = 0
            for i in range(NT):
                for lv in range(1, LEVELS):
                    for q in range(2):
                        ps = filled(act, ("x", i, lv, q))
                        A_(xx[:, 4 * q:4 * q + 4, :], ps[:, :].rearrange("p (h t) -> p h t", h=4), ACT.Copy
                           ).then_inc(*free(("x", i, lv, q)))
                    ada_rows(c)
                    c += 1
                for q in range(2):
                    ps = filled(act, ("w1", i, q))
                    A_(zb[:, i, 4 * q:4 * q + 4, 0:DH], ps[:, :].rearrange("p (h t) -> p h t", h=4)[:, :, 0:DH], ACT.Copy
                       ).then_inc(*free(("w1", i, q)))
                ada_rows(c)
                c += 1
                for q in range(2):
                    ps = filled(act, ("u", i, q))
                    v = ps[:, :].rearrange("p (h t) -> p h t", h=4)
                    A_(up[:, 4 * q:4 * q + 4, :], v[:, :, 0:DH], ACT.Copy)
                    A_(tk[:, 4 * q:4 * q + 4, :], v[:, :, DH:P], ACT.Copy).then_inc(*free(("u", i, q)))
                ps = filled(act, ("y", i))
                A_(yT[:, :, i * P:(i + 1) * P], ps[:, :].rearrange("p (h t) -> p h t", h=4), ACT.Copy).then_inc(*free(("y", i)))

            def gates_of(j):
                ps = filled(act, ("ga", j))
                for h in range(2):
                    ins = A_(gates[:, 2 * j + h, :], ps[:, h * SEQ:(h + 1) * SEQ], ACT.Sigmoid, bias=par("b_gate", 2 * j + h))
                ins.then_inc(*free(("ga", j)))

            gates_of(0)
            gates_of(1)
            for j in range(2):
                drained(act, ("m", j))
            A_(tmp, yT, ACT.Square).then_inc(S("y_sq"), 1)
            for j in range(2, 5):
                gates_of(j)
            for j in range(5, 8):
                gates_of(j)
            drained(act, ("vn",))
            A_(nmr[0:HEADS, :], nmr[0:HEADS, :], ACT.Sqrt).then_inc(S("y_sd"), 1)
            drained(act, ("mg", 0))
            bcast(npost, A["norm_mix_post"][0], "npost_in")
            filled(act, ("mg", KD - 1))
            high_parts(0)
            post_norm(1, "mo")
            high_parts(1)
            pre_norm(2, lambda i: act.wait_ge(S("x_new"), i + 1))
            root(2)
            bcast(fpost, A["norm_ffn_post"][0], "post_in")
            transposed_high(1, lambda k: par("norm_ffn_pre", k), None)
            high_parts(2)
            for f in range(KF):
                ps = filled(act, ("ff", f))
                if f >= 2:
                    drained(act, ("ff", f - 2))
                A_(sil[:, f % 2, :], ps[:, 0:SEQ], ACT.Silu).then_inc(S("sil"), 1)
                if f % 2:
                    drained(act, ("ff", f - 1))
                    drained(act, ("ff", f))
                    A_(fh[:, f - 1:f + 1, :], fT[:, f - 1:f + 1, :], ACT.Copy).then_inc(S("f_high"), 1)
                    high_parts(f // 2 + 3)
            for n in range(KF // 2 + 3, BY_TWO + 1):
                high_parts(n)
            post_norm(3, "dn")
            high_parts(BY_TWO + 1)
            high_parts(BY_TWO + 2)
            pre_norm(4, lambda i: act.wait_ge(S("x_new"), 2 + i + 1))
            root(4)
            act.wait_ge(S("mod"), 1)
            act.dma_start(band, A["bands"].rearrange("p (g t) -> p g t", g=GRP)).then_inc(S("pool_in"), 16)
            for g in range(GRP):
                act.dma_start(wp[64 * (g % 2):64 * (g % 2) + 64, g // 2, :], A["w_pool_2"][0, g]).then_inc(S("pool_in"), 16)
            transposed_high(2, lambda k: modc[:, 8 + k:9 + k], lambda k: modc[:, k:k + 1])
            for n in range(2):
                for i in range(NT):
                    ps = filled(act, ("uz", i, n))
                    if n == 0:
                        A_(u[:, i, :], ps[:, 0:POOL], ACT.Copy)
                        A_(sz[:, i, 0:256], ps[:, POOL:512], ACT.Silu).then_inc(*free(("uz", i, 0)))
                    else:
                        A_(sz[:, i, 256:SSD], ps[:, :], ACT.Silu).then_inc(*free(("uz", i, 1)))
                high_parts(BY_TWO + 3 + n)
            for j in range(7):
                ps = filled(act, ("xb", j))
                A_(xraw[:, 2 * j:2 * j + 2, :], ps[:, :].rearrange("p (m t) -> p m t", m=2), ACT.Copy)
                for h in range(2):
                    m = 2 * j + h
                    ins = A_(xs[:, m, :], ps[:, h * SEQ:(h + 1) * SEQ], ACT.Identity, scale=par("conv_w_2", 3 * MX + m),
                             bias=par("conv_b_2", m))
                ins.then_inc(*free(("xb", j)))
                if j == 1:
                    high_parts(BY_TWO + 5)
                if j >= 1:
                    act.wait_ge(S("conv"), j)
                    A_(xs[:, 2 * j - 2:2 * j, :], xs[:, 2 * j - 2:2 * j, :], ACT.Silu).then_inc(S("xs"), 1)
            act.wait_ge(S("conv"), 7)
            A_(xs[:, 12:14, :], xs[:, 12:14, :], ACT.Silu).then_inc(S("xs"), 1)
            act.wait_ge(S("par2_in"), 16 * 3)
            act.wait_ge(S("dt_abs"), 1)
            A_(alog, alog, ACT.Exp).then_inc(S("alog"), 1)
            A_(dtmp, dtmp, ACT.Exp, scale=-1.0).then_inc(S("dt_e"), 1)
            act.wait_ge(S("dt_e"), 1)
            A_(dtmp, dtmp, ACT.Ln, bias=1.0).then_inc(S("dt_ln"), 1)
            drained(act, ("cs",))
            A_(ea[:, 0, 0:SH], acs[:, 1, 0:SH], ACT.Exp)
            A_(ea[:, 1, 0:SH], acs[:, 2, 0:SH], ACT.Exp).then_inc(S("ea"), 1)
            ps = filled(act, ("pm",))
            for h in range(2):
                ins = A_(mixT[:, h, :], ps[:, h * SEQ:(h + 1) * SEQ], ACT.Copy, scale=par("pool_scale_2", h))
            ins.then_inc(*free(("pm",)))
            for i in range(NT):
                for q in range(3):
                    drained(act, ("rb", i, q))
                A_(dec[:, i], dec[:, i], ACT.Exp).then_inc(S("dec_e"), 1)
            for i in range(NT):
                for a in range(2):
                    ps = filled(act, ("xt", i, a))
                    w = 512 if a == 0 else 256
                    A_(xtok[:, i, 512 * a:512 * a + w], ps[:, 0:w], ACT.Copy).then_inc(*free(("xt", i, a)))
            ps = filled(act, ("bt",))
            A_(btk, ps[:, :], ACT.Copy).then_inc(*free(("bt",)))
            for a in range(2):
                ps = filled(act, ("cst", a))
                A_(st[:, 384 * a:384 * a + 384], ps[:, 0:384], ACT.Copy).then_inc(*free(("cst", a)))
            act.wait_ge(S("gms"), 1)
            A_(gms, gms, ACT.Sqrt).then_inc(S("gsd"), 1)
            for i in range(NT):
                for a in range(2):
                    ps = filled(act, ("mt", i, a))
                    for c in range(4 if a == 0 else 2):
                        m = 4 * a + c
                        ins = A_(mixT[:, 2 + m, i * P:(i + 1) * P], ps[:, c * P:(c + 1) * P], ACT.Copy,
                                 scale=par("ssd_norm_w_2", m))
                    ins.then_inc(*free(("mt", i, a)))
            pre_norm(5, lambda i: act.wait_ge(S("x_new"), 4 + i + 1))
            root(5)
            transposed(3, lambda k: modc[:, 32 + k:33 + k], lambda k: modc[:, 24 + k:25 + k])
            act.wait_ge(S("xn"), 8)
            bcast(fin, A["final_norm_w"], "fin_in")
            act.wait_ge(S("g_shift"), 1)
            A_(rtb[0][:, 0:NT * EG], rtb[0][:, 0:NT * EG], ACT.Exp).then_inc(S("g_exp"), 1)
            act.wait_ge(S("v_gap"), 1)
            A_(rtb[1][:, 0:NT], rtb[1][:, 0:NT], ACT.Exp).then_inc(S("v_exp"), 1)
            act.wait_ge(S("crowded"), 1)
            many = act.value_load(crowded[0:1, 0:1])
            with act.If(many > 0):
                with act.Fori(0, EP) as it:
                    for x in range(2):
                        for i in range(NT):
                            act.wait_ge(S("hidden"), it * 8 + (4 * x + 2 * i + 2))
                            A_(sa[:, i, :], bank[4 + 2 * i][:, :], ACT.Silu).then_inc(S("sa"), 1)
                        for i in range(NT):
                            act.wait_ge(S("turns"), it * 4 + (2 * x + i + 1))
                            A_(acT[:, i, :, :], bank[4 + 2 * i][:, :].rearrange("p (f t) -> p f t", f=KE), ACT.Copy
                               ).then_inc(S("turned"), 1)
            with act.Else():
                def gathered(p):
                    act.wait_ge(S("gathered"), p * 2 + 1)
                    for k in range(4):
                        ins = A_(hg[:, k, :], bank[4][:, k * P:(k + 1) * P], ACT.Identity, bias=modc[:, 24 + k:25 + k],
                                 scale=modc[:, 32 + k:33 + k])
                    ins.then_inc(S("hg"), 1)

                def silu(p):
                    act.wait_ge(S("w13_used"), p * 4 + 4)
                    A_(sa[:, 0, :], bank[6][:, :], ACT.Silu).then_inc(S("sa"), 1)

                def turned(p):
                    act.wait_ge(S("turns"), p + 1)
                    A_(acT[:, 0, :, :], bank[6][:, :].rearrange("p (f t) -> p f t", f=KE), ACT.Copy).then_inc(S("ac_turned"), 1)

                def slots_out(p):
                    act.wait_ge(S("w2_used"), p * 2 + 2)
                    A_(yslot[:, 0:512], bank[4][:, :], ACT.Copy).then_inc(S("y_slots"), 1)

                gathered(0)
                with act.Fori(0, EP - 1) as it:
                    silu(it)
                    gathered(it + 1)
                    turned(it)
                    slots_out(it)
                silu(EP - 1)
                turned(EP - 1)
                slots_out(EP - 1)
            pre_norm(6, lambda i: act.wait_ge(S("x_new"), 6 + i + 1))
            root(6)

        @block.gpsimd
        def _(pool):
            pool.wait_ge(S("csil"), 1)
            nc.gpsimd.tensor_copy(cb, csil.unsqueeze(2).to_broadcast([P, KD, 32])).then_inc(S("cb"), 1)
            strict = K("strict").unsqueeze(1).unsqueeze(1).to_broadcast([P, 4, 2, P])

            def diagonal(buf, half):
                return buf[:, 4 * half:4 * half + 4, :].rearrange("p h (b t) -> p h b t", b=3)[:, :, 0:3:2, :]

            pool.wait_ge(S("con_in"), 16)
            for half in range(2):
                pool.wait_ge(S("att_ln"), half + 1)
                hs = slice(4 * half, 4 * half + 4)
                nc.gpsimd.tensor_tensor(rz[:, hs, :], rz[:, hs, :], az[:, hs, :], ALU.add).then_inc(S("att_sum"), 1)
                pool.wait_ge(S("att_sum"), half + 1)
                nc.gpsimd.tensor_tensor(diagonal(rz, half), diagonal(rz, half), strict, ALU.mult).then_inc(S("att_sp"), 1)
            for half in range(2):
                pool.wait_ge(S("att_x"), half + 1)
                nc.gpsimd.tensor_tensor(diagonal(az, half), diagonal(az, half), strict, ALU.mult).then_inc(S("att_w"), 1)
            eye = K("ident").unsqueeze(1).to_broadcast([P, HEADS, P])
            for i in range(NT):
                drained(pool, ("tok", NT - 1, 3) if i == 0 else ("y", 0))
                nc.gpsimd.tensor_copy(dd, eye).then_inc(S("eye"), 1)
                nc.gpsimd.tensor_copy(ddT, eye).then_inc(S("eye"), 1)
            for dm in range(KD):
                drained(pool, ("mg", dm))
                nc.gpsimd.tensor_tensor(gates[:, dm, :], gates[:, dm, :], gates[:, KD + dm, :], ALU.add).then_inc(S("merged"), 1)
            for n in range(len(SPLIT)):
                _, words = split_words(n)
                if n < BY_TWO:
                    pool.wait_ge(S("high"), 2 * n + 1)
                    low_part(nc.gpsimd, n, 0, words // 2).then_inc(S("low"), 1)
                else:
                    pool.wait_ge(S("high"), 2 * n + 2)
                    low_part(nc.gpsimd, n, 0, words).then_inc(S("low"), 1)
                c = n - 3
                if 0 <= c < KF // 2:
                    pool.wait_ge(S("f_high"), c + 1)
                    f = slice(2 * c, 2 * c + 2)
                    nc.gpsimd.tensor_tensor(fT_lo[:, f, :], fT[:, f, :], fh[:, f, :].bitcast(F32), ALU.subtract).then_inc(S("f_low"), 1)

        @block.vector
        def _(dve):
            V = nc.vector
            steps = [0]

            def link(ins):
                steps[0] += 1
                ins.then_inc(S("dve_step"), 1)
                dve.wait_ge(S("dve_step"), steps[0])

            def cast(ap, *shape):
                return ap.to_broadcast(list(shape))

            sq_seen = [0]

            def inverse_root(n, halves):
                sq_seen[0] += NT * halves
                dve.wait_ge(S("sq"), sq_seen[0])
                src = ss[n][:, 0:NT]
                if halves == 2:
                    v = ss[n].rearrange("p (i h) -> p i h", h=2)
                    link(V.tensor_tensor(ms[n][:, 0:NT], v[:, :, 0], v[:, :, 1], ALU.add))
                    src = ms[n][:, 0:NT]
                V.tensor_scalar(ms[n][:, 0:NT], src, 1.0 / D, EPS, ALU.mult, ALU.add).then_inc(S("ms"), 1)
                dve.wait_ge(S("sd"), n + 1)
                link(V.reciprocal(rstd[n][:, 0:NT], sd[n][:, 0:NT]))

            def pre_norm(n, s):
                inverse_root(n, 1)
                for i in range(NT):
                    V.tensor_scalar(xn[s][:, i, :], xres[:, i, :], rstd[n][:, i:i + 1], None, ALU.mult).then_inc(S("xn"), 1)

            def transposed(s, scale, bias):
                for kk in (1, 3):
                    ps = filled(dve, ("hT", s, kk))
                    for k2 in range(2):
                        k = 2 * kk + k2
                        ins = V.tensor_scalar(hT[:, k, :], ps[:, k2 * SEQ:(k2 + 1) * SEQ], scale(k), bias(k) if bias else None,
                                              ALU.mult, ALU.add if bias else ALU.bypass)
                    ins.then_inc(*free(("hT", s, kk)))

            low_seen = [0]

            def transposed_low(s, scale, bias):
                for kk in range(4):
                    ps = filled(dve, ("hT", s, kk))
                    low_seen[0] += 1
                    dve.wait_ge(S("h_high"), low_seen[0])
                    two = slice(2 * kk, 2 * kk + 2)
                    for k2 in range(2):
                        k = 2 * kk + k2
                        cols = ps[:, k2 * SEQ:(k2 + 1) * SEQ]
                        if bias:
                            ins = V.tensor_scalar(hT[:, k, :], cols, scale(k), bias(k), ALU.mult, ALU.add)
                        else:
                            ins = V.scalar_tensor_tensor(hT_lo[:, k, :], cols, scale(k), hT_hi[s][:, k, :].bitcast(F32), ALU.mult, ALU.subtract)
                    if bias:
                        link(ins)
                        ins = V.tensor_tensor(hT_lo[:, two, :], hT[:, two, :], hT_hi[s][:, two, :].bitcast(F32), ALU.subtract)
                    ins.then_inc(*free(("hT", s, kk)))

            def second_low(n):
                dve.wait_ge(S("high"), 2 * n + 2)
                _, words = split_words(n)
                low_part(V, n, words // 2, words).then_inc(S("low2"), 1)

            def post_norm(n, name, buf, weight):
                for j in range(4):
                    half, i = j // 2, j % 2
                    ps = filled(dve, (name, i, half))
                    dve.wait_ge(S("sq"), sq_seen[0] + j + 1)
                    V.tensor_copy(buf[:, i, 512 * half:512 * half + 512], ps[:, :]).then_inc(*free((name, i, half)))
                inverse_root(n, 2)
                for j in range(4):
                    drained(dve, (name, j % 2, j // 2))
                for i in range(NT):
                    link(V.scalar_tensor_tensor(buf[:, i, :], buf[:, i, :], rstd[n][:, i:i + 1], weight, ALU.mult, ALU.mult))
                    V.tensor_tensor(xres[:, i, :], xres[:, i, :], buf[:, i, :], ALU.add).then_inc(S("x_new"), 1)

            for t, rows in enumerate(PAR):
                n = sum(r for _, r in rows)
                ps = filled(dve, ("par", t))
                V.tensor_copy(parcol[:, t, 0:n], ps[:, 0:n]).then_inc(*free(("par", t)))
            for t in range(NPAR):
                drained(dve, ("par", t))
            V.tensor_scalar(omu, par("mu_rw", 0, 14), -1.0, 1.0, ALU.mult, ALU.add).then_inc(S("omu"), 1)
            dve.wait_ge(S("x_in"), 16)
            pre_norm(0, 0)
            dve.wait_ge(S("lvl_in"), 16)
            link(V.tensor_copy(lvl[:, :], B("lvlf")))
            transposed(0, lambda k: par("norm_mix_pre", k), None)

            def shifted(m):
                if m < 4:
                    return rT[:, m, :]
                if m < 8:
                    return kT[:, m - 4, :]
                return vT[:, m - 8, :] if m < 12 else lora[:, m - 12, :]

            for n, j in enumerate(RW_ORDER):
                ps = filled(dve, ("rw", j))
                dve.wait_ge(S("rw_own"), n + 1)
                for h in range(2):
                    m = 2 * j + h
                    dst = shifted(m)[:, 1:SEQ]
                    ins = V.scalar_tensor_tensor(dst, ps[:, h * SEQ:(h + 1) * SEQ - 1], par("mu_rw", m), dst, ALU.mult, ALU.add)
                ins.then_inc(*free(("rw", j)))
                if j == 3:
                    drained(dve, ("rw", 2))
                    drained(dve, ("rw", 3))
                    for m in range(4):
                        ins = V.tensor_scalar(kkT[:, m, :], kT[:, m, :], par("k_k", m), None, ALU.mult)
                    ins.then_inc(S("kk_raw"), 1)
            dve.wait_ge(S("con_in"), 16)
            for j in range(2):
                drained(dve, ("lw", j))
                for h in range(2):
                    m = 2 * j + h
                    ins = V.tensor_tensor_scan(cum[:, m, :], K("scan_reset"), lw[:, m, :], 0.0, ALU.mult, ALU.add)
            link(ins)
            ch = cum.rearrange("p m (c t) -> p m c t", t=CH)
            tot = total.rearrange("p (m c) -> p m c", c=4)
            V.tensor_copy(tot.unsqueeze(3), ch[:, :, :, CH - 1:CH])
            for j in range(2):
                drained(dve, ("la", j))
            drained(dve, ("kn",))
            for m in range(4):
                ins = V.tensor_scalar(tmp[:, m, :], aT[:, m, :], -1.0, par("k_a", m), ALU.add, ALU.mult)
            link(ins)
            link(V.scalar_tensor_tensor(kT, tmp, 1.0, kT, ALU.add, ALU.mult))
            link(V.tensor_scalar(nmr[0:HEADS, :], nmr[0:HEADS, :], 1e-12, None, ALU.max))
            V.reciprocal(nmr[0:HEADS, :], nmr[0:HEADS, :]).then_inc(S("kk_inv"), 1)
            for m in range(4):
                ins = V.scalar_tensor_tensor(bon[:, m, :], rT[:, m, :], par("r_k", m), kT[:, m, :], ALU.mult, ALU.mult)
            ins.then_inc(S("bon_raw"), 1)
            for j in range(2, 4):
                ps = filled(dve, ("qk", j))
                V.tensor_copy(qk[:, 2 * j:2 * j + 2, :].rearrange("p a b -> p (a b)"), ps[:, :]).then_inc(*free(("qk", j)))
            for i in range(NT):
                ps = filled(dve, ("v", i))
                V.tensor_copy(vtok[:, i, :], ps[:, :]).then_inc(*free(("v", i)))
            for j in range(2):
                ps = filled(dve, ("kb", j))
                V.tensor_tensor(kkT[:, 2 * j:2 * j + 2, :], kkT[:, 2 * j:2 * j + 2, :],
                                ps[:, :].rearrange("p (a b) -> p a b", a=2), ALU.mult).then_inc(*free(("kb", j)))
            for j in range(2):
                drained(dve, ("kb", j))
            V.tensor_tensor(bT, kkT, aT, ALU.mult)
            V.tensor_tensor(lw, cum, lw, ALU.subtract).then_inc(S("ex"), 1)
            for h in range(HEADS):
                ps = filled(dve, ("z", h))
                link(V.tensor_scalar(rz[:, h, :], ps[:, 0:384], 0.0, None, ALU.max))
                V.scalar_tensor_tensor(az[:, h, :], rz[:, h, :], -2.0, ps[:, 0:384], ALU.mult, ALU.add).then_inc(*free(("z", h)))

            def by_tile(x):
                return x.rearrange("p a (i t) -> p a i t", i=NT)

            dve.wait_ge(S("e_inc"), 1)
            V.tensor_tensor(kr[:, :, :, 1, :], by_tile(rT), by_tile(aT), ALU.mult).then_inc(S("kr_r"), 1)
            dve.wait_ge(S("e_exc"), 1)
            V.scalar_tensor_tensor(kr[:, :, :, 0, :], by_tile(kkT), -1.0, by_tile(lw), ALU.mult, ALU.mult).then_inc(S("kr_k"), 1)
            dve.wait_ge(S("e_inv"), 1)
            V.tensor_tensor(bh, bT, tmp, ALU.mult)
            V.tensor_tensor(kh, kT, tmp, ALU.mult).then_inc(S("bk_hat"), 1)
            V.tensor_tensor(ch, cast(tot.unsqueeze(3), P, 4, 4, CH), ch, ALU.subtract).then_inc(S("to_end"), 1)
            for j in range(2):
                ps = filled(dve, ("bn", j))
                V.tensor_tensor(bon[:, 2 * j:2 * j + 2, :], ps[:, :].rearrange("p (a b) -> p a b", a=2),
                                vT[:, 2 * j:2 * j + 2, :], ALU.mult).then_inc(*free(("bn", j)))
            dve.wait_ge(S("e_suf"), 1)
            V.tensor_tensor(bT, bT, cum, ALU.mult)
            V.tensor_tensor(kT, kT, cum, ALU.mult).then_inc(S("bk_bar"), 1)
            for h in range(HEADS):
                ps = filled(dve, ("l", h))
                V.tensor_scalar(az[:, h, :], ps[:, 0:384], 0.0, None, ALU.min).then_inc(*free(("l", h)))
            for i in range(NT):
                ps = filled(dve, ("tok", i, 2))
                V.tensor_copy(ktok[:, i, :], ps[:, :]).then_inc(*free(("tok", i, 2)))
                ps = filled(dve, ("tok", i, 3))
                V.memset(vp[:, i, :, DH:P], 0.0)
                V.tensor_copy(vp[:, i, :, 0:DH], ps[:, :].rearrange("p (h d) -> p h d", h=HEADS)).then_inc(*free(("tok", i, 3)))

            def heads4(ps):
                return ps[:, :].rearrange("p (h t) -> p h t", h=4)

            blocks = cast(K("head_block").unsqueeze(1), P, PAIRS, P)

            def ada_sum(c):
                ps = filled(dve, ("as", c))
                if c in COLUMN_CHUNKS:
                    V.tensor_tensor(modc[:, 4 * c:4 * c + 4], ps[:, 0:4], par("b_ada_2", 4 * c, 4), ALU.add).then_inc(*free(("as", c)))
                else:
                    g = (g1 if c < 6 else g2)[:, 512 * (c % 2):512 * (c % 2) + 512]
                    V.tensor_tensor(g, g, ps[:, :], ALU.add).then_inc(*free(("as", c)))

            dve.wait_ge(S("gate_in"), 32)
            dve.wait_ge(S("pc"), 1)
            c = 0
            for i in range(NT):
                for h in range(HEADS):
                    ps = filled(dve, ("g", i, h))
                    V.tensor_tensor(gm[:, h, :], ps[:, :], K("gram_mask"), ALU.mult).then_inc(*free(("g", i, h)))
                dve.wait_ge(S("eye"), 2 * i + 2)
                for q in range(2):
                    hs = slice(4 * q, 4 * q + 4)
                    ps = filled(dve, ("n", i, q))
                    V.copy_predicated(dd[:, hs, :], lmask(0, 0), heads4(ps)).then_inc(*free(("n", i, q)))
                    drained(dve, ("g", i, 4 * q + 3))
                    V.copy_predicated(ddT[:, hs, :], lmask(0, 1), gm[:, hs, 0:P]).then_inc(S("dt_first"), 1)
                for lv in range(1, LEVELS):
                    if c:
                        ada_sum(c - 1)
                    c += 1
                    for q in range(2):
                        hs = slice(4 * q, 4 * q + 4)
                        if lv < LEVELS - 1:
                            ps = filled(dve, ("d", i, lv, q))
                            V.copy_predicated(dd[:, hs, :], lmask(lv, 0), heads4(ps)).then_inc(*free(("d", i, lv, q)))
                        ps = filled(dve, ("dt", i, lv, q))
                        V.copy_predicated(ddT[:, hs, :], lmask(lv, 1), heads4(ps)).then_inc(*free(("dt", i, lv, q)))
                ada_sum(c - 1)
                c += 1
                ps = filled(dve, ("ry", i))
                V.tensor_tensor(ryT[:, :, i * P:(i + 1) * P], heads4(ps), kr[:, :, i, 1, :], ALU.add).then_inc(*free(("ry", i)))
                for k in (2 * i, 2 * i + 1):
                    if k == 3:
                        continue
                    ps = filled(dve, ("psi", k))
                    V.tensor_tensor(psi[:, k], heads4(ps), blocks, ALU.mult).then_inc(*free(("psi", k)))
                k = i + 1
                ps = filled(dve, ("phi", k))
                V.tensor_tensor(phi[:, k - 1], heads4(ps), blocks, ALU.mult).then_inc(*free(("phi", k)))
                drained(dve, ("phi", k))
                for p in range(PAIRS):
                    ins = V.scalar_tensor_tensor(phi[:, k - 1, p, :], K("ident"), pc[:, 4 * p + k:4 * p + k + 1],
                                                 phi[:, k - 1, p, :], ALU.mult, ALU.add)
                ins.then_inc(S("phi"), 1)
                ps = filled(dve, ("s", k))
                drained(dve, ("psi", k))
                V.tensor_tensor(psi[:, k], psi[:, k], heads4(ps), ALU.add).then_inc(*free(("s", k)))
            ada_sum(11)
            for c in COLUMN_CHUNKS:
                drained(dve, ("as", c))
            link(V.tensor_scalar(modc[:, 8:16], modc[:, 8:16], 1.0, None, ALU.add))
            V.tensor_scalar(modc[:, 32:40], modc[:, 32:40], 1.0, None, ALU.add).then_inc(S("mod"), 1)
            for i in range(NT):
                drained(dve, ("y", i))
            for j in range(2):
                ps = filled(dve, ("m", j))
                V.tensor_tensor(yT[:, 2 * j:2 * j + 2, :], yT[:, 2 * j:2 * j + 2, :],
                                ps[:, :].rearrange("p (a b) -> p a b", a=2), ALU.subtract).then_inc(*free(("m", j)))
            ps = filled(dve, ("vn",))
            V.tensor_scalar(nmr[0:HEADS, :], ps[0:HEADS, 0:SEQ], 1.0 / DH, GN_EPS, ALU.mult, ALU.add).then_inc(*free(("vn",)))
            dve.wait_ge(S("y_sd"), 1)
            V.reciprocal(nmr[0:HEADS, :], nmr[0:HEADS, :]).then_inc(S("y_inv"), 1)
            for j in range(2):
                drained(dve, ("m", j))
                ps = filled(dve, ("vb", j))
                V.tensor_tensor(yT[:, 2 * j:2 * j + 2, :], yT[:, 2 * j:2 * j + 2, :],
                                ps[:, :].rearrange("p (a b) -> p a b", a=2), ALU.mult).then_inc(*free(("vb", j)))
            for j in range(2):
                drained(dve, ("vb", j))
            for m in range(4):
                ins = V.tensor_scalar(yT[:, m, :], yT[:, m, :], par("lnx_w", m), par("lnx_b", m), ALU.mult, ALU.add)
            link(ins)
            for j in range(2):
                drained(dve, ("bn", j))
            link(V.tensor_tensor(yT, yT, bon, ALU.add))
            V.tensor_tensor(orw, yT, gT, ALU.mult).then_inc(S("orw"), 1)
            for j in range(8):
                drained(dve, ("ga", j))
            for dm in range(KD):
                ps = filled(dve, ("mg", dm))
                V.tensor_tensor(gates[:, dm, :], gates[:, dm, :], ps[:, 0:SEQ], ALU.mult)
                V.tensor_tensor(gates[:, KD + dm, :], gates[:, KD + dm, :], ps[:, SEQ:2 * SEQ], ALU.mult).then_inc(*free(("mg", dm)))
            dve.wait_ge(S("npost_in"), 16)
            post_norm(1, "mo", mo, npost)
            for i in range(NT):
                dve.wait_ge(S("x_new"), i + 1)
            pre_norm(2, 1)
            transposed_low(1, lambda k: par("norm_ffn_pre", k), None)
            for n in range(3):
                second_low(n)
            for f in range(KF):
                ps = filled(dve, ("ff", f))
                dve.wait_ge(S("sil"), f + 1)
                V.tensor_tensor(fT[:, f, :], sil[:, f % 2, :], ps[:, SEQ:2 * SEQ], ALU.mult).then_inc(*free(("ff", f)))
                if f % 2:
                    second_low(f // 2 + 3)
            for n in range(KF // 2 + 3, BY_TWO):
                second_low(n)
            dve.wait_ge(S("post_in"), 16)
            post_norm(3, "dn", dno, fpost)
            dve.wait_ge(S("x_new"), 4)
            pre_norm(4, 2)
            dve.wait_ge(S("mod"), 1)
            transposed_low(2, lambda k: modc[:, 8 + k:9 + k], lambda k: modc[:, k:k + 1])
            for j in range(7):
                drained(dve, ("xb", j))
                for d in range(1, 4):
                    for h in range(2):
                        m = 2 * j + h
                        ins = V.scalar_tensor_tensor(xs[:, m, d:SEQ], xraw[:, m, 0:SEQ - d], par("conv_w_2", (3 - d) * MX + m),
                                                     xs[:, m, d:SEQ], ALU.mult, ALU.add)
                    if d < 3:
                        link(ins)
                    else:
                        ins.then_inc(S("conv"), 1)
            dve.wait_ge(S("router_in"), 64)
            ps = filled(dve, ("dt2",))
            V.tensor_tensor(dtr, ps[:, 0:32].rearrange("p (i c) -> p i c", i=NT)[:, :, 0:SH], cast(dtb.unsqueeze(1), P, NT, SH),
                            ALU.add).then_inc(*free(("dt2",)))
            drained(dve, ("dt2",))
            V.scalar_tensor_tensor(dtmp, dtr, -1.0, dtr, ALU.mult, ALU.max).then_inc(S("dt_abs"), 1)
            ps = filled(dve, ("pl",))
            V.tensor_copy(dif.rearrange("p a b -> p (a b)"), ps[:, :]).then_inc(*free(("pl",)))
            dve.wait_ge(S("dt_ln"), 1)
            link(V.scalar_tensor_tensor(dtr, dtr, 0.0, dtmp, ALU.max, ALU.add))
            dve.wait_ge(S("alog"), 1)
            V.scalar_tensor_tensor(da, dtr, -1.0, cast(alog.unsqueeze(1), P, NT, SH), ALU.mult, ALU.mult).then_inc(S("da"), 1)
            ps = filled(dve, ("cs",))
            V.tensor_copy(acs[:, :, 0:SH], ps[:, 0:48].rearrange("p (i c) -> p i c", i=3)[:, :, 0:SH]).then_inc(*free(("cs",)))
            drained(dve, ("cs",))
            for i in range(NT):
                for q in range(3):
                    ps = filled(dve, ("rb", i, q))
                    for j in range(4):
                        h = 4 * q + j
                        ins = V.tensor_scalar(dec[:, i, h, :], ps[:, j * P:(j + 1) * P], acs[:, i, h:h + 1], 0.0, ALU.subtract, ALU.min)
                    ins.then_inc(*free(("rb", i, q)))
            for i in range(NT):
                ps = filled(dve, ("cb", i))
                V.tensor_tensor(cbm[:, i], heads4(ps), cast(K("causal").unsqueeze(1), P, GRP, P), ALU.mult).then_inc(*free(("cb", i)))
                dve.wait_ge(S("dec_e"), i + 1)
                drained(dve, ("cb", i))
                d4 = dec[:, i].rearrange("p (g r) t -> p g r t", g=GRP)
                V.tensor_tensor(d4, d4, cast(cbm[:, i].unsqueeze(2), P, GRP, SR, P), ALU.mult).then_inc(S("dec"), 1)

            def by_head(x):
                return x.rearrange("p (h d) -> p h d", h=SH)

            dve.wait_ge(S("ea"), 1)
            for i in range(NT):
                for a in range(2):
                    drained(dve, ("xt", i, a))
                V.tensor_tensor(by_head(xc[:, i]), by_head(xtok[:, i]), cast(dtr[:, i, :].unsqueeze(2), P, SH, DH), ALU.mult
                                ).then_inc(S("xc"), 1)
                if i == 0:
                    dve.wait_ge(S("xc"), 1)
                    V.tensor_tensor(by_head(xde), by_head(xc[:, 0]), cast(ea[:, 1, 0:SH].unsqueeze(2), P, SH, DH), ALU.mult
                                    ).then_inc(S("xde"), 1)
            dve.wait_ge(S("par2_in"), 48)
            for i in range(NT):
                link(V.tensor_tensor(by_head(ys[:, i]), by_head(xtok[:, i]), cast(dsk.unsqueeze(2), P, SH, DH), ALU.mult))
                for a in range(2):
                    w = 512 if a == 0 else 256
                    f = slice(512 * a, 512 * a + w)
                    ps = filled(dve, ("yd", i, a))
                    V.tensor_tensor(ys[:, i, f], ys[:, i, f], ps[:, 0:w], ALU.add).then_inc(*free(("yd", i, a)))
            for a in range(2):
                ps = filled(dve, ("yo", a))
                f = slice(384 * a, 384 * a + 384)
                V.tensor_tensor(yo[:, f].rearrange("p (h d) -> p h d", d=DH), ps[:, 0:384].rearrange("p (h d) -> p h d", d=DH),
                                cast(ea[:, 0, 6 * a:6 * a + 6].unsqueeze(2), P, 6, DH), ALU.mult).then_inc(*free(("yo", a)))
            for a in range(2):
                drained(dve, ("yo", a))
                drained(dve, ("yd", 1, a))
            link(V.tensor_tensor(ys[:, 1], ys[:, 1], yo, ALU.add))
            for a in range(2):
                drained(dve, ("yd", 0, a))
            link(V.tensor_tensor(ys, ys, sz, ALU.mult))
            link(V.tensor_tensor(ysq, ys, ys, ALU.mult))
            GW = SR * DH
            grp = ysq.rearrange("p i (g d) -> p (i g) d", g=GRP)
            link(V.tensor_reduce(gss, grp, AX.X, ALU.add))
            V.tensor_scalar(gms, gss, 1.0 / GW, EPS, ALU.mult, ALU.add).then_inc(S("gms"), 1)
            dve.wait_ge(S("gsd"), 1)
            link(V.reciprocal(gss, gms))
            for i in range(NT):
                yg = ys[:, i].rearrange("p (g d) -> p g d", g=GRP)
                V.tensor_tensor(yg, yg, cast(gss[:, GRP * i:GRP * i + GRP].unsqueeze(2), P, GRP, GW), ALU.mult).then_inc(S("ys"), 1)
            for c in (4, 5, 10, 11):
                drained(dve, ("as", c))
            for n in range(2):
                f = slice(512 * n, 512 * n + 512)
                for i in range(NT):
                    ps = filled(dve, ("mx", i, n))
                    V.tensor_tensor(gtmp, ps[:, :], g1[:, f], ALU.mult).then_inc(*free(("mx", i, n)))
                    drained(dve, ("mx", i, n))
                    ins = V.tensor_tensor(xres[:, i, f], xres[:, i, f], gtmp, ALU.add)
                    if n == 1:
                        ins.then_inc(S("x_new"), 1)
                        dve.wait_ge(S("x_new"), 5 + i)
                    else:
                        link(ins)
            dve.wait_ge(S("x_new"), 6)
            pre_norm(5, 3)
            transposed(3, lambda k: modc[:, 32 + k:33 + k], lambda k: modc[:, 24 + k:25 + k])
            V.memset(junk[0:1, 0:512], 0.0)
            V.memset(rs[0:1, 0:1], 0.0).then_inc(S("zero"), 1)
            ps = filled(dve, ("rt",))
            V.tensor_tensor(lg, ps[:, 0:NT * 64].rearrange("p (i c) -> p i c", i=NT)[:, :, 0:36], cast(rbias.unsqueeze(1), P, NT, 36),
                            ALU.add).then_inc(*free(("rt",)))
            drained(dve, ("rt",))

            def first_max(hot, vals, best, rev, n, keep):
                flag, top = keep
                link(V.tensor_reduce(best, vals, AX.X, ALU.max))
                link(V.tensor_tensor(flag, vals, cast(best.unsqueeze(2), P, NT, n), ALU.is_ge))
                link(V.tensor_tensor(flag, flag, rev, ALU.mult))
                link(V.tensor_reduce(top, flag, AX.X, ALU.max))
                link(V.tensor_tensor(hot, flag, cast(top.unsqueeze(2), P, NT, n), ALU.is_equal))

            def wide(buf, n):
                return buf[:, 0:NT * n].rearrange("p (i c) -> p i c", i=NT)

            best_g, v1, v2, top, gsum = (rtb[7][:, 2 * n:2 * n + 2] for n in range(5))
            hot_g = wide(rtb[2], EG)
            flag = wide(rtb[3], EG)
            first_max(hot_g, lg[:, :, 0:EG], best_g, wide(K("rev_group"), EG), EG, (flag, top))
            ex_g = wide(rtb[0], EG)
            V.tensor_tensor(ex_g, lg[:, :, 0:EG], cast(best_g.unsqueeze(2), P, NT, EG), ALU.subtract).then_inc(S("g_shift"), 1)
            link(V.tensor_scalar(hot_g, hot_g, 1.0, BIG, ALU.subtract, ALU.mult))
            inside = wide(rtb[4], EXPERTS)
            link(V.tensor_tensor(inside.rearrange("p i (g e) -> p i g e", g=EG),
                                 lg[:, :, EG:36].rearrange("p i (g e) -> p i g e", g=EG),
                                 cast(hot_g.unsqueeze(3), P, NT, EG, EPG), ALU.add))
            hot1, hot2, flag = wide(rtb[5], EXPERTS), wide(rtb[6], EXPERTS), wide(rtb[3], EXPERTS)
            rev = wide(K("rev_expert"), EXPERTS)
            first_max(hot1, inside, v1, rev, EXPERTS, (flag, top))
            link(V.scalar_tensor_tensor(inside, hot1, -3.0 * BIG, inside, ALU.mult, ALU.add))
            first_max(hot2, inside, v2, rev, EXPERTS, (flag, top))
            V.tensor_tensor(rtb[1][:, 0:NT], v2, v1, ALU.subtract).then_inc(S("v_gap"), 1)
            dve.wait_ge(S("g_exp"), 1)
            link(V.tensor_reduce(gsum, ex_g, AX.X, ALU.add))
            dve.wait_ge(S("v_exp"), 1)
            link(V.scalar_tensor_tensor(top, rtb[1][:, 0:NT], 1.0, gsum, ALU.add, ALU.mult))
            link(V.reciprocal(top, top))
            sel = wide(rtb[4], EXPERTS)
            V.tensor_tensor(sel, hot1, hot2, ALU.add).then_inc(S("chosen"), 1)
            dve.wait_ge(S("chosen"), 1)
            link(V.tensor_tensor(hot2, hot2, cast(rtb[1][:, 0:NT].unsqueeze(2), P, NT, EXPERTS), ALU.mult))
            link(V.tensor_tensor(hot1, hot1, hot2, ALU.add))
            V.tensor_tensor(gate, hot1, cast(top.unsqueeze(2), P, NT, EXPERTS), ALU.mult).then_inc(S("gate"), 1)
            dve.wait_ge(S("gate"), 1)
            def by_pair(buf):
                return buf.rearrange("p (q i x) -> p i q x", q=EP, i=NT)

            def pairs(buf):
                return buf.rearrange("p i (q x) -> p i q x", q=EP)

            for i in range(NT):
                link(V.tensor_copy(by_pair(gateq)[:, i], pairs(gate)[:, i]))
            ps = filled(dve, ("rk",))
            ranks = ps[:, 0:NT * EXPERTS].rearrange("p (i c) -> p i c", i=NT)
            for i in range(NT):
                link(V.scalar_tensor_tensor(by_pair(posq)[:, i], pairs(ranks)[:, i], 1.0, pairs(sel)[:, i], ALU.add, ALU.mult))
            most = rtb[7][:, 10:11]
            V.tensor_reduce(most, ps[:, NT * EXPERTS:(NT + 1) * EXPERTS], AX.X, ALU.max).then_inc(*free(("rk",)))
            drained(dve, ("rk",))
            V.tensor_scalar(crowded[:, :], most, CAP + 0.5, None, ALU.is_gt).then_inc(S("crowded"), 1)
            dve.wait_ge(S("crowded"), 1)
            many = dve.value_load(crowded[0:1, 0:1])
            with dve.If(many > 0):
                with dve.Fori(0, EP) as it:
                    for x in range(2):
                        for i in range(NT):
                            dve.wait_ge(S("sa"), it * 4 + (2 * x + i + 1))
                            V.scalar_tensor_tensor(ac[:, i, :], sa[:, i, :], gate[:, i, bass.ds(it * 2 + x, 1)],
                                                   bank[5 + 2 * i][:, :], ALU.mult, ALU.mult).then_inc(S("act_out"), 1)
                dve.wait_ge(S("w2_used"), 2 * EP)
            with dve.Else():
                slot = K("slot").unsqueeze(1).to_broadcast([P, 2 * NT, CAP])

                def of_pair(buf, p):
                    return buf[:, bass.ds(p * 4, 4)].unsqueeze(2).to_broadcast([P, 2 * NT, CAP])

                def choose(p):
                    if not isinstance(p, int) or p > 0:
                        dve.wait_ge(S("gathered"), p * 2)
                        dve.wait_ge(S("onew"), p)
                    V.tensor_tensor(one, slot, of_pair(posq, p), ALU.is_equal).then_inc(S("one"), 1)

                def weigh(p):
                    dve.wait_ge(S("one"), p + 1)
                    if not isinstance(p, int) or p > 0:
                        dve.wait_ge(S("w_turns"), p)
                    V.tensor_tensor(onew, one, of_pair(gateq, p), ALU.mult).then_inc(S("onew"), 1)

                def gathered(p):
                    dve.wait_ge(S("gathered"), p * 2 + 2)
                    for k in range(4, KD):
                        ins = V.tensor_scalar(hg[:, k, :], bank[5][:, (k - 4) * P:(k - 3) * P], modc[:, 32 + k:33 + k],
                                              modc[:, 24 + k:25 + k], ALU.mult, ALU.add)
                    ins.then_inc(S("hg"), 1)

                def activate(p):
                    dve.wait_ge(S("sa"), p + 1)
                    V.tensor_tensor(ac[:, 0, :], sa[:, 0, :], bank[7][:, :], ALU.mult).then_inc(S("ac"), 1)

                def weights_turned(p):
                    dve.wait_ge(S("w_turns"), p + 1)
                    V.tensor_copy(onewT, bank[7][:, 0:SEQ]).then_inc(S("w_turned"), 1)

                def slots_out(p):
                    dve.wait_ge(S("w2_used"), p * 2 + 2)
                    V.tensor_copy(yslot[:, 512:D], bank[5][:, :]).then_inc(S("y_slots"), 1)

                choose(0)
                gathered(0)
                weigh(0)
                choose(1)
                activate(0)
                gathered(1)
                weights_turned(0)
                slots_out(0)
                with dve.Fori(1, EP - 1) as it:
                    weigh(it)
                    choose(it + 1)
                    activate(it)
                    gathered(it + 1)
                    weights_turned(it)
                    slots_out(it)
                weigh(EP - 1)
                activate(EP - 1)
                weights_turned(EP - 1)
                slots_out(EP - 1)
                dve.wait_ge(S("combined"), EP)
            for i in range(NT):
                for n in range(2):
                    f = slice(512 * n, 512 * n + 512)
                    link(V.tensor_tensor(gtmp, bank[2 * i + n][:, :], g2[:, f], ALU.mult))
                    ins = V.tensor_tensor(xres[:, i, f], xres[:, i, f], gtmp, ALU.add)
                    if n == 1:
                        ins.then_inc(S("x_new"), 1)
                        dve.wait_ge(S("x_new"), 7 + i)
                    else:
                        link(ins)
            dve.wait_ge(S("x_new"), 8)
            inverse_root(6, 1)
            dve.wait_ge(S("fin_in"), 16)
            for i in range(NT):
                V.scalar_tensor_tensor(xres[:, i, :], xres[:, i, :], rstd[6][:, i:i + 1], fin, ALU.mult, ALU.mult).then_inc(S("y_out"), 1)


_INS = ['x', 'norm_mix_pre', 'w_in', 'b_gate', 'mu_rw', 'w0', 'w_up', 'a0', 'a_up', 'g_up', 'k_k', 'k_a', 'r_k',
        'lnx_w', 'lnx_b', 'w_sb_out', 'w_rw_out', 'w_o', 'norm_mix_post', 'norm_ffn_pre', 'w_ffn_gate', 'w_ffn_up',
        'w_ffn_down', 'norm_ffn_post', 'c_2', 'w_ada_2', 'b_ada_2', 'w_in_2', 'w_pool_2', 'pool_scale_2', 'conv_w_2',
        'conv_b_2', 'dt_bias_2', 'a_log_2', 'd_skip_2', 'ssd_norm_w_2', 'w_out_2', 'w_group_2', 'b_group_2',
        'w_router_2', 'b_router_2', 'w13_2', 'w2_2', 'final_norm_w_2']


def kernel(**inputs):
    import numpy as _np
    import concourse.bacc as _bacc
    from concourse import mybir as _mybir
    from concourse.bass_utils import run_bass_kernel_spmd as _run

    nc = _bacc.Bacc("TRN2", target_bir_lowering=False, num_devices=1)
    arrays, args = {}, {}
    for name in _INS:
        a = _np.ascontiguousarray(inputs[name])
        arrays[f"in_{name}"] = a
        args[name] = nc.dram_tensor(f"in_{name}", a.shape, _mybir.dt.from_np(a.dtype), kind="ExternalInput").ap()
    for name, a in (("consts", host_constants()), ("levels", host_level_masks()), ("bands", host_bands())):
        arrays[name] = a
        args[name] = nc.dram_tensor(name, a.shape, _mybir.dt.from_np(a.dtype), kind="ExternalInput").ap()
    args["final_norm_w"] = args["final_norm_w_2"]
    out = nc.dram_tensor("out", (1, SEQ, D), _mybir.dt.from_np(_np.dtype("float32")), kind="ExternalOutput").ap()
    build(nc, args, out)
    r = _run(nc, [arrays], core_ids=[0])
    return r.results[0]["out"]
```

```python
import numpy as np
import concourse.bass as bass
from concourse import mybir
from contextlib import ExitStack

F32 = mybir.dt.float32
F32R = mybir.dt.float32r
U8 = mybir.dt.uint8
I32 = mybir.dt.int32
ALU = mybir.AluOpType
ACT = mybir.ActivationFunctionType
AX = mybir.AxisListType

P = 128
SEQ = 256
NT = SEQ // P
D = 1024
KD = D // P
HEADS = 8
DH = 64
WID = HEADS * DH
PAIRS = HEADS // 2
CH = 64
SB_COLS = 3 * WID
RW_COLS = 3 * WID + 256
FF = 2816
KF = FF // P
GN_EPS = DH * 1e-5
EPS = 1e-6
DECAY = -float(np.exp(-0.5))
GRP = 4
SH = 12
SR = SH // GRP
POOL = 256
SSD = 768
XBC = SSD + 2 * GRP * P
MX = XBC // P
WINDOWS = (2, 4, 8, 16)
EXPERTS = 32
EG = 4
EPG = EXPERTS // EG
EF = 512
KE = EF // P
BIG = 1e30

SLOT = 4096
CAP = 64
RING = 3
LEVELS = 6
NPAR = 3


def const_layout():
    names = [("ident", P), ("ones", P), ("neg_suffix", P), ("neg_ones", P), ("strict", P), ("gram_mask", 4 * P),
             ("head_block", P), ("head_mean", P), ("scan_reset", SEQ), ("head_sum", PAIRS * HEADS),
             ("head_spread", PAIRS * P), ("causal", P), ("after", P), ("thirty_second", P),
             ("rev_group", NT * EG), ("rev_expert", NT * EXPERTS), ("slot", CAP)]
    at, out = 0, {}
    for n, w in names:
        out[n] = (at, at + w)
        at += w
    return out, at


CONST, NCONST = const_layout()


def host_constants():
    c = np.zeros((P, NCONST), np.float32)
    i, j = np.arange(P)[:, None], np.arange(P)[None, :]
    same = (i // CH) == (j // CH)

    def put(name, v):
        a, b = CONST[name]
        c[:, a:b] = v

    put("ident", i == j)
    put("ones", 1.0)
    put("neg_suffix", -1.0 * (i >= j))
    put("neg_ones", -1.0)
    put("strict", i < j)
    put("gram_mask", np.concatenate([same & (i < j), same & (i <= j)] * 2, axis=1))
    put("head_block", same)
    put("head_mean", same / DH)
    put("scan_reset", (np.arange(SEQ) % CH != 0)[None, :])
    a, b = CONST["head_sum"]
    s = np.zeros((P, PAIRS, HEADS), np.float32)
    t = np.zeros((P, PAIRS, P), np.float32)
    for p in range(PAIRS):
        for h in range(2):
            s[h * DH:(h + 1) * DH, p, 2 * p + h] = 1
            t[2 * p + h, p, h * DH:(h + 1) * DH] = 1
    c[:, a:b] = s.reshape(P, -1)
    a, b = CONST["head_spread"]
    c[:, a:b] = t.reshape(P, -1)
    put("causal", i <= j)
    put("after", i > j)
    put("thirty_second", 1.0 / 32)
    put("rev_group", np.tile(EG - np.arange(EG), NT)[None, :])
    put("rev_expert", np.tile(EXPERTS - np.arange(EXPERTS), NT)[None, :])
    put("slot", 1.0 + np.arange(CAP)[None, :])
    return c


def host_level_masks():
    i, j = np.arange(P)[:, None], np.arange(P)[None, :]
    m = np.zeros((P, 2, LEVELS, P), np.float32)
    for n in range(LEVELS):
        s = 1 << n
        low = (i // (2 * s) == j // (2 * s)) & ((i // s) % 2 == 1) & ((j // s) % 2 == 0)
        m[:, 0, n] = low
        m[:, 1, n] = low.T
    return m.reshape(P, -1)


def host_bands():
    t, s = np.arange(SEQ)[None, :], np.arange(SEQ)[:, None]
    out = np.zeros((P, GRP, SEQ + P), np.float32)
    for g, w in enumerate(WINDOWS):
        band = ((s <= t) & (s > t - w)) / np.minimum(t + 1, w) - (s == t)
        out[:, g, :SEQ] = band[:P]
        out[:, g, SEQ:] = band[P:, P:]
    return out.reshape(P, -1)


PAR = [
    [("norm_mix_pre", 8), ("mu_rw", 14)],
    [("w0", 4), ("a0", 4), ("k_k", 4), ("k_a", 4), ("r_k", 4), ("lnx_w", 4), ("lnx_b", 4), ("b_gate", 16),
     ("norm_ffn_pre", 8), ("c_2", 8), ("b_ada_2", 48)],
    [("pool_scale_2", 2), ("conv_w_2", 4 * MX), ("conv_b_2", MX), ("ssd_norm_w_2", 6)],
]


def par_columns():
    out, block, at = {}, [], 0
    for rows in PAR:
        block.append(at)
        for name, r in rows:
            out[name] = at
            at += r
    return out, block + [at]


PARCOL, PARBLOCK = par_columns()


def ada_banks(c):
    return ([("as", c - 1)] if c else []) + ([("ad", c)] if c < ADA_CHUNKS else [])


def plan_banks():
    o = [("par", 0)] + [("hT", 0, kk) for kk in range(4)]
    o += [("rw", RW_ORDER[0])] + [("par", n) for n in range(1, NPAR)] + [("rw", mm) for mm in RW_ORDER[1:]]
    o += [(n, mm) for n in ("lw", "la", "lg") for mm in range(2)]
    o += [("qk", mm) for mm in range(4)] + [("v", 0), ("kn",), ("v", 1)]
    o += [("kb", mm) for mm in range(2)]
    o += [("z", h) for h in range(HEADS)]
    o += [("bn", mm) for mm in range(2)]
    o += [("ga", mm) for mm in range(2)] + [("tok", i, a) for i in range(NT) for a in range(4)]
    o += [("l", h) for h in range(HEADS)]
    o += [("o", 0), ("o", 1)] + ada_banks(0) + [("o", 2), ("o", 3)]
    ada = 1
    for i in range(NT):
        o += [("g", i, h) for h in range(HEADS)]
        o += [("n", i, q) for q in range(2)]
        for lv in range(1, LEVELS):
            o += [("x", i, lv, q) for q in range(2)]
            o += ada_banks(ada)
            ada += 1
            for q in range(2):
                o += ([("d", i, lv, q)] if lv < LEVELS - 1 else []) + [("dt", i, lv, q)]
        o += [("w1", i, q) for q in range(2)]
        o += ada_banks(ada)
        ada += 1
        o += [("u", i, q) for q in range(2)]
        if i == 0:
            o += [("ry", 0), ("psi", 0), ("psi", 1), ("phi", 1), ("y", 0), ("s", 1)]
        else:
            o += [("ry", 1), ("psi", 2), ("phi", 2), ("s", 2), ("y", 1)]
    o += [("m", mm) for mm in range(2)]
    o += [("ga", mm) for mm in range(2, 5)] + [("vn",)]
    o += [("ga", mm) for mm in range(5, 7)] + [("vb", mm) for mm in range(2)] + [("ga", 7)]
    o += [("mg", dm) for dm in range(KD)]
    o += [("mo", i, n) for n in range(2) for i in range(NT)]
    o += [("hT", 1, kk) for kk in range(4)]
    o += [("ff", m) for m in range(KF)]
    o += [("dn", i, n) for n in range(2) for i in range(NT)]
    o += [("hT", 2, kk) for kk in range(4)]
    o += [("uz", i, n) for n in range(2) for i in range(NT)]
    o += [("xb", mm) for mm in range(7)]
    o += [("dt2",), ("pl",), ("cs",), ("pm",)]
    o += [("rb", i, q) for i in range(NT) for q in range(3)]
    o += [("cb", i) for i in range(NT)]
    o += [("xt", i, a) for i in range(NT) for a in range(2)] + [("bt",)]
    o += [("yd", 0, a) for a in range(2)] + [("cst", a) for a in range(2)]
    o += [("yd", 1, a) for a in range(2)] + [("yo", a) for a in range(2)]
    for i in range(NT):
        o += [("mt", i, a) for a in range(2)] + [("mx", i, n) for n in range(2)]
    o += [("hT", 3, kk) for kk in range(4)]
    o += [("rt",), ("rk",)]
    assert len(set(o)) == len(o)
    return {k: (n % 8, n // 8) for n, k in enumerate(o)}


RW_ORDER = (6, 2, 3, 0, 1, 4, 5)
ADA_CHUNKS = 12
COLUMN_CHUNKS = (0, 1, 2, 3, 6, 7, 8, 9)
QTOK = 4 * SEQ

NORM1, RW, PROJ, PREP, TOKENS, WKV, GATES, MERGE, POST1, FFN, DOWN, PROJ2, CONV, SCAN, MIXED, MOE = range(16)
BUFFERS = [
    ("junk", D, NORM1, MOE), ("parrow", NPAR * P, NORM1, RW), ("g1", D, NORM1, MIXED), ("g2", D, NORM1, MOE),
    ("wua", WID, NORM1, PROJ), ("gup", WID, NORM1, PROJ), ("cb", KD * 32, NORM1, WKV), ("npost", D, MERGE, POST1),
    ("xn0", NT * D, NORM1, NORM1), ("lvlf", 2 * LEVELS * P, RW, PREP),
    ("osb", QTOK, PREP, MERGE), ("gT", QTOK, PROJ, GATES), ("bon", QTOK, PREP, GATES),
    ("tmp", QTOK, RW, GATES), ("nmr", SEQ, PREP, GATES),
    ("kr", 2 * QTOK, PREP, WKV), ("bh", QTOK, PREP, WKV), ("kh", QTOK, PREP, WKV),
    ("kT", QTOK, RW, TOKENS), ("vT", QTOK, RW, TOKENS), ("b", QTOK, PREP, TOKENS),
    ("rT", QTOK, RW, PREP), ("lora", 2 * SEQ, RW, PREP), ("a", QTOK, PROJ, PREP), ("lw", QTOK, PROJ, PREP),
    ("kk", QTOK, RW, PREP), ("cum", QTOK, PREP, PREP), ("qk", 2 * QTOK, PROJ, TOKENS), ("v", NT * WID, PROJ, TOKENS),
    ("az", HEADS * 384, PREP, TOKENS), ("rz", HEADS * 384, PREP, TOKENS),
    ("vp", NT * HEADS * P, TOKENS, WKV), ("btok", NT * WID, TOKENS, WKV), ("ktok", NT * WID, TOKENS, WKV),
    ("zb", NT * HEADS * P, TOKENS, WKV),
    ("modp", 2 * 512, TOKENS, GATES), ("gm", HEADS * 4 * P, WKV, WKV), ("dd", HEADS * P, WKV, WKV),
    ("ddT", HEADS * P, WKV, WKV), ("xx", HEADS * P, WKV, WKV), ("up", HEADS * DH, WKV, WKV),
    ("tk", HEADS * DH, WKV, WKV), ("phi", 2 * PAIRS * P, WKV, WKV), ("psi", 3 * PAIRS * P, WKV, WKV),
    ("ry", QTOK, WKV, WKV), ("y", QTOK, WKV, GATES),
    ("orw", QTOK, GATES, MERGE), ("gates0", 4 * SEQ, TOKENS, POST1), *[(f"gates{n}", 4 * SEQ, GATES, POST1) for n in range(1, 4)],
    ("mo", NT * D, POST1, POST1), ("xn1", NT * D, POST1, FFN), ("fpost", D, FFN, DOWN),
    ("fT", KF * SEQ, FFN, DOWN), ("fh", KF * SEQ, FFN, DOWN), *[(f"hrw{n}", SLOT, RW, RW) for n in range(3)], ("hh0", KD * SEQ, RW, RW), ("hl0", KD * SEQ, RW, RW),
    *[(f"hi{n}", SLOT, GATES, PROJ2) for n in range(3)],
    ("hh3", KD * SEQ, GATES, GATES), ("hl3", KD * SEQ, GATES, GATES), ("osbh", QTOK, GATES, MERGE), ("orwh", QTOK, MERGE, MERGE), ("hh1", KD * SEQ, FFN, FFN),
    ("hh2", KD * SEQ, PROJ2, PROJ2),
    ("sil", 2 * SEQ, FFN, FFN), ("dno", NT * D, DOWN, DOWN),
    ("xn2", NT * D, DOWN, PROJ2),
    ("u", NT * POOL, PROJ2, SCAN), ("sz", NT * SSD, PROJ2, MIXED), ("xraw", MX * SEQ, PROJ2, CONV),
    ("xs", MX * SEQ, PROJ2, SCAN), ("band", GRP * (SEQ + P), PROJ2, CONV), ("wp", P, PROJ2, SCAN),
    ("dif", 2 * SEQ, CONV, SCAN), ("dt", 32, CONV, SCAN), ("dtmp", 32, CONV, SCAN), ("da", 32, CONV, SCAN),
    ("acs", 48, CONV, SCAN), ("ea", 32, CONV, SCAN),
    ("dec", NT * SH * P, SCAN, SCAN), ("cbm", NT * GRP * P, SCAN, SCAN), ("xtok", NT * SSD, SCAN, SCAN),
    ("btk", GRP * P, SCAN, SCAN), ("xc", NT * SSD, SCAN, SCAN), ("xde", SSD, SCAN, SCAN), ("st", SSD, SCAN, SCAN),
    ("yo", SSD, SCAN, SCAN), ("ys", NT * SSD, SCAN, MIXED), ("ysq", NT * SSD, SCAN, MIXED),
    ("mixT", KD * SEQ, CONV, MIXED), ("gtmp", 512, MIXED, MOE),
    ("xn3", NT * D, MIXED, MOE), ("ew", 3 * SLOT, MIXED, MOE), ("sa", 2 * EF, MOE, MOE), ("ac", 2 * EF, MOE, MOE),
    ("acT", 2 * EF, MOE, MOE), ("lg", NT * 36, MOE, MOE), ("rt", 8 * 64, MOE, MOE), ("gate", 64, MOE, MOE),
    ("rs", 64, MOE, MOE), ("fin", D, MOE, MOE), ("posq", 64, MOE, MOE), ("gateq", 64, MOE, MOE),
    ("hg", KD * P, MOE, MOE), ("one", 2 * P, MOE, MOE), ("onew", 2 * P, MOE, MOE), ("onewT", SEQ, MOE, MOE),
    *[(f"ew2_{n}", SLOT // 2, MOE, MOE) for n in range(4)],
]


def place(limit):
    def first_fit(buffers):
        at, spans = {}, []
        for name, w, first, last in buffers:
            pos = 0
            for a, b in sorted((a, a + x) for a, x, f, l in spans if f <= last and first <= l):
                if pos + w <= a:
                    break
                pos = max(pos, b)
            spans.append((pos, w, first, last))
            at[name] = (pos, pos + w)
        return at

    draw = np.random.RandomState(0)
    for trial in range(2000):
        weight = np.exp(draw.standard_normal(len(BUFFERS)) * (0.5 if trial else 0))
        at = first_fit([BUFFERS[n] for n in sorted(range(len(BUFFERS)), key=lambda n: -BUFFERS[n][1] * weight[n])])
        if max(b for _, b in at.values()) <= limit:
            return at
    raise ValueError("the buffers don't fit")


def build(nc, A, out):
    BANK = plan_banks()
    ctx = ExitStack()
    with ctx:
        sems = {}

        def S(name):
            if name not in sems:
                sems[name] = ctx.enter_context(nc.semaphore(name))
            return sems[name]

        start = {}

        def sb(name, shape, dt=F32):
            start[name] = -(-nc.sbuf_base // 32) * 32
            return ctx.enter_context(nc.sbuf_tensor(name, shape, dt))

        def rounded(name, shape, buffer, words=0):
            return nc.alloc_sbuf_tensor_at(name, [P] + shape, F32R, offset=start[buffer] + 4 * words)

        con = sb("con", [P, NCONST])
        lvl = sb("lvl", [P, 2 * LEVELS * P], U8)
        parcol = sb("parcol", [P, PARBLOCK[-1]])
        xres = sb("xres", [P, NT, D])
        hT = sb("hT", [P, KD, SEQ])
        small = sb("small", [P, 600])
        crowded = sb("crowded", [P, 1], I32)
        ring = sb("ring", [P, RING, SLOT])
        words = nc.sbuf_bytes_remaining // 4 - 16
        arena = sb("arena", [P, words])
        where = place(words)
        bank = [ctx.enter_context(nc.psum_tensor(f"bank{b}", [P, 512], F32)) for b in range(8)]
        bank_full = [S(f"bank_full{b}") for b in range(8)]
        bank_free = [S(f"bank_free{b}") for b in range(8)]

        def K(name):
            a, b = CONST[name]
            return con[:, a:b]

        def par(name, n=0, w=1):
            return parcol[:, PARCOL[name] + n:PARCOL[name] + n + w]

        def lmask(lv, turned):
            m = lvl[:, (turned * LEVELS + lv) * P:(turned * LEVELS + lv + 1) * P]
            return m.unsqueeze(1).to_broadcast([P, 4, P])

        at = [0]

        def tiny(w):
            at[0] += w
            assert at[0] <= 600
            return small[:, at[0] - w:at[0]]

        ss, ms, sd, rstd = ([tiny(4) for _ in range(7)] for _ in range(4))
        omu, total, pc, modc = tiny(14), tiny(16), tiny(16), tiny(48)
        wgr = tiny(KD * 36).rearrange("p (k e) -> p k e", k=KD)
        rbias, dtb, alog, dsk, csil = tiny(36), tiny(SH), tiny(SH), tiny(SH), tiny(KD)
        gss, gms, spare = tiny(8), tiny(8), tiny(3)

        def B(name, *dims):
            a, b = where[name]
            ap = arena[:, a:b]
            if len(dims) == 1:
                return ap.rearrange("p (a b) -> p a b", a=dims[0])
            if len(dims) == 2:
                return ap.rearrange("p (a b c) -> p a b c", a=dims[0], b=dims[1])
            if len(dims) == 3:
                return ap.rearrange("p (a b c d) -> p a b c d", a=dims[0], b=dims[1], c=dims[2])
            return ap

        junk, parrow, cb = B("junk"), B("parrow", NPAR), B("cb", KD)
        g1, g2, wua, gup, npost, fpost, fin = (B(n) for n in ("g1", "g2", "wua", "gup", "npost", "fpost", "fin"))
        xn = [B(f"xn{n}", NT) for n in range(4)]
        osb, gT, bon, tmp, bh, kh, kT, vT, bT = (B(n, 4) for n in ("osb", "gT", "bon", "tmp", "bh", "kh", "kT", "vT", "b"))
        rT, lora, aT, lw, kkT, cum, qk, vtok = (B(n, d) for n, d in (
            ("rT", 4), ("lora", 2), ("a", 4), ("lw", 4), ("kk", 4), ("cum", 4), ("qk", 8), ("v", NT)))
        nmr = B("nmr")
        kr = B("kr", PAIRS, NT, 2)
        az, rz = B("az", HEADS), B("rz", HEADS)
        vp, zb = B("vp", NT, HEADS), B("zb", NT, HEADS)
        btok, ktok, modp = B("btok", NT), B("ktok", NT), B("modp", 2)
        gm, dd, ddT, xx, up, tk = (B(n, HEADS) for n in ("gm", "dd", "ddT", "xx", "up", "tk"))
        phi, psi = B("phi", 2, PAIRS), B("psi", 3, PAIRS)
        ryT, yT, orw = B("ry", PAIRS), B("y", PAIRS), B("orw", PAIRS)
        gates = [B(f"gates{j // 4}", 4)[:, j % 4] for j in range(16)]
        mo, dno, fT, sil = B("mo", NT), B("dno", NT), B("fT", KF), B("sil", 2)
        hi, hi_rw = ([rounded(f"{b}_high{n}", [SLOT], "arena", where[f"{b}{n}"][0]) for n in range(3)] for b in ("hi", "hrw"))
        fh, fT_lo = (rounded(n, [KF, SEQ], "arena", where[b][0]) for n, b in (("f_high", "fh"), ("f_low", "fT")))
        hT_hi = {n: rounded(f"h{n}_high", [KD, SEQ], "arena", where[f"hh{n}"][0]) for n in (0, 1, 2, 3)}
        hT0_lo, hT3_lo = (rounded(f"h{n}_low", [KD, SEQ], "arena", where[f"hl{n}"][0]) for n in (0, 3))
        osb_hi, osb_lo, orw_hi, orw_lo = (rounded(n, [PAIRS, SEQ], "arena", where[b][0]) for n, b in (
            ("osb_high", "osbh"), ("osb_low", "osb"), ("orw_high", "orwh"), ("orw_low", "orw")))
        hT_lo, ring_lo = rounded("h_low", [KD, SEQ], "hT"), rounded("ring_low", [RING, SLOT], "ring")
        u, sz, xraw, xs, band = B("u", NT), B("sz", NT), B("xraw", MX), B("xs", MX), B("band", GRP)
        wp, dif = B("wp", 2), B("dif", 2)
        dtr, dtmp, da = (B(n, NT)[:, :, 0:SH] for n in ("dt", "dtmp", "da"))
        acs, ea = B("acs", 3), B("ea", 2)
        dec, cbm = B("dec", NT, SH), B("cbm", NT, GRP)
        xtok, btk, xc, xde, st, yo = B("xtok", NT), B("btk"), B("xc", NT), B("xde"), B("st"), B("yo")
        ys, ysq, mixT, gtmp = B("ys", NT), B("ysq", NT), B("mixT", KD), B("gtmp")
        ew = B("ew", 3)
        sa, ac, acT = B("sa", NT), B("ac", NT), B("acT", NT, KE)
        lg, gate, rs = B("lg", NT), B("gate", NT), B("rs")
        posq, gateq, hg = B("posq"), B("gateq"), B("hg", KD)
        yslot = (sa[:, 1, :], ac[:, 1, :])
        one, onew, onewT = B("one", 2 * NT), B("onew", 2 * NT), B("onewT")
        rtb = [B("rt", 8)[:, n] for n in range(8)]

        def write(pe, key):
            b, turn = BANK[key]
            if turn:
                pe.wait_ge(bank_free[b], turn)
            return bank[b]

        def full(key):
            return bank_full[BANK[key][0]], 1

        def filled(eng, key):
            b, turn = BANK[key]
            eng.wait_ge(bank_full[b], turn + 1)
            return bank[b]

        def free(key):
            return bank_free[BANK[key][0]], 1

        def drained(eng, key):
            b, turn = BANK[key]
            eng.wait_ge(bank_free[b], turn + 1)

        def cols(w, c0, c1):
            return w[:, c0:c1].rearrange("(k p) c -> p k c", p=P)

        w_in, w_in2 = A["w_in"][0], A["w_in_2"][0]
        W = []

        def stream(key, parts, last):
            W.append((key, parts, last))

        for c in (3, 1, 0, 2):
            a, b = SB_COLS + c * 512, min(SB_COLS + c * 512 + 512, SB_COLS + RW_COLS)
            stream(("rw", c), [(0, cols(w_in, a, b))], ("rw", min(2 * c + 1, 6)))
        for c, last in enumerate((("qk", 1), ("qk", 3), ("v", 1))):
            stream(("sb", c), [(0, cols(w_in, c * 512, c * 512 + 512))], last)
        def gate_columns(c):
            a = SB_COLS + RW_COLS + c * 512
            stream(("gate", c), [(0, cols(w_in, a, a + 512))], ("ga", 2 * c + 1))

        gate_columns(0)
        for c in range(ADA_CHUNKS):
            stream(("ada", c), [(0, cols(A["w_ada_2"][0], c * 512, c * 512 + 512))], ("ad", c))
        for c in range(1, 4):
            gate_columns(c)
        stream("sb_out", [(0, cols(A["w_sb_out"][0], 0, D))], ("mg", KD - 1))
        stream("rw_out", [(0, cols(A["w_rw_out"][0], 0, D))], ("mg", KD - 1))
        for n in range(2):
            stream(("wo", n), [(0, cols(A["w_o"][0], n * 512, n * 512 + 512))], ("mo", 1, n))
        for c in range(KF // 2):
            stream(("ff", c), [(0, cols(A["w_ffn_gate"][0], c * 256, c * 256 + 256)),
                               (2048, cols(A["w_ffn_up"][0], c * 256, c * 256 + 256))], ("ff", 2 * c + 1))
        n_down = -(-KF // 4)
        for c in range(n_down):
            r0, r1 = c * 512, min(c * 512 + 512, FF)
            stream(("down", c), [(0, cols(A["w_ffn_down"][0][r0:r1, :], 0, D))],
                   ("dn", 1, 1) if c == n_down - 1 else ("sem", "down_used", c + 1))
        for c in range(6):
            stream(("in2", c), [(0, cols(w_in2, c * 512, min(c * 512 + 512, w_in2.shape[1])))],
                   ("uz", 1, c) if c < 2 else ("xb", 2 * c - 3) if c < 5 else ("dt2",))
        for n in range(2):
            stream(("out2", n), [(0, cols(A["w_out_2"][0], n * 512, n * 512 + 512))], ("mx", 1, n))
        slot_full = [S(f"slot_full{r}") for r in range(RING)]
        SLOTS, loads = {}, [0] * RING
        for n, (key, parts, last) in enumerate(W):
            loads[n % RING] += 16 * len(parts)
            SLOTS[key] = (n % RING, loads[n % RING])

        def slot_view(key, k):
            r = SLOTS[key][0]
            parts = [p for q, p, _ in W if q == key][0]
            w = parts[0][1].shape[2]
            return ring[:, r, 0:k * w].rearrange("p (k c) -> p k c", k=k)

        def arrived(eng, key):
            r, count = SLOTS[key]
            eng.wait_ge(slot_full[r], count)

        SPLIT = [(key, last) for key, _, last in W if key[0] in ("ff", "down", "in2") or key[0] == "rw" and key[1] < 3
                 or key in (("gate", 2), ("gate", 3), "sb_out", "rw_out")]
        N_RW = sum(key[0] == "rw" for key, _ in SPLIT)
        N_FF = sum(key[0] not in ("ff", "down", "in2") for key, _ in SPLIT)
        split_at = {key: n for n, (key, _) in enumerate(SPLIT)}
        BY_TWO = sum(key[0] != "in2" for key, _ in SPLIT)

        def split_words(n):
            key = SPLIT[n][0]
            parts = [p for q, p, _ in W if q == key][0]
            return SLOTS[key][0], sum(src.shape[1] * src.shape[2] for _, src in parts)

        def high_of(n):
            return (hi_rw if n < N_RW else hi)[n % 3]

        def parts_view(key, pattern, **dims):
            n = split_at[key]
            r, words = split_words(n)
            return [x.rearrange(pattern, **dims) for x in (high_of(n)[:, 0:words], ring_lo[:, r, 0:words])]

        def low_part(eng, n, c0, c1):
            r, _ = split_words(n)
            return eng.tensor_tensor(ring_lo[:, r, c0:c1], ring[:, r, c0:c1], high_of(n)[:, c0:c1].bitcast(F32), ALU.subtract)

        def consumed(eng, last):
            if last[0] == "sem":
                eng.wait_ge(S(last[1]), last[2])
            else:
                filled(eng, last)

        EP = EXPERTS // 2
        w13_full = [S(f"w13_full{c}") for c in range(KD // 2)]
        w2_full = [[S(f"w2_full{q}{c}") for c in range(KE // 2)] for q in range(2)]
        base = ring[:, :, :].rearrange("p r w -> p (r w)")
        other = ew.rearrange("p r w -> p (r w)")
        w13s = [x[:, 0:2 * SLOT].rearrange("p (k c) -> p k c", k=KD) for x in (base, other)]
        w2s = [[[x[:, 2 * SLOT + c * SLOT // 2:2 * SLOT + (c + 1) * SLOT // 2] for c in range(2)] for x in (base, other)],
               [[B(f"ew2_{2 * x + c}") for c in range(2)] for x in range(2)]]
        w2s = [[[c.rearrange("p (k c) -> p k c", k=2) for c in x] for x in q] for q in w2s]
        w13_d = A["w13_2"][0].rearrange("e (k p) c -> p e k c", p=P)
        w2_d = A["w2_2"][0].rearrange("e (k p) c -> p e k c", p=P)
        x_tok = A["x"][0].rearrange("(i p) d -> p i d", p=P)
        out_tok = out[0].rearrange("(i p) d -> p i d", p=P)

        block = ctx.enter_context(nc.Block())

        @block.sync
        def _(sp):
            sp.dma_start(xres[:, :, :], x_tok).then_inc(S("x_in"), 16)

            def parameters(t):
                a = 0
                for name, r in PAR[t]:
                    src = A[name].rearrange("x y z -> (x y z)") if len(A[name].shape) == 3 else \
                        A[name].rearrange("x y -> (x y)")
                    sp.dma_start(parrow[a:a + r, t, :], src.rearrange("(r c) -> r c", c=P)).then_inc(S(f"par_in{t}"), 16)
                    a += r

            parameters(0)
            sp.dma_start(con[:, 0:P], A["consts"][:, 0:P]).then_inc(S("ident_in"), 16)
            freed_by = {}
            for n, (key, parts, last) in enumerate(W):
                r = n % RING
                if n == 2:
                    sp.dma_start(con[:, P:NCONST], A["consts"][:, P:NCONST]).then_inc(S("con_in"), 16)
                    for t in range(1, NPAR):
                        parameters(t)
                if r in freed_by:
                    consumed(sp, freed_by[r])
                for c0, src in parts:
                    k, w = src.shape[1], src.shape[2]
                    dst = ring[:, r, c0:c0 + k * w].rearrange("p (k c) -> p k c", k=k)
                    sp.dma_start(dst, src).then_inc(slot_full[r], 16)
                freed_by[r] = last

            def load_w13(p, c, x):
                e = p * 2 + x
                sp.dma_start(w13s[x][:, 2 * c:2 * c + 2, :],
                             w13_d[:, bass.ds(e, 1), 2 * c:2 * c + 2, :].rearrange("p e k c -> p (e k) c")
                             ).then_inc(w13_full[c], 16)

            def load_w2(p, q, c, x):
                e = p * 2 + x
                sp.dma_start(w2s[q][x][c],
                             w2_d[:, bass.ds(e, 1), 2 * c:2 * c + 2, :].rearrange("p e k c -> p (e k) c")
                             ).then_inc(w2_full[q][c], 16)

            sp.wait_ge(S("gms"), NT)
            drained(sp, ("pm",))
            for x in (1, 0):
                if x == 0:
                    for r in range(RING):
                        filled(sp, freed_by[r])
                for c in range(KD // 2):
                    load_w13(0, c, x)
                for c in range(KE // 2):
                    load_w2(0, 0, c, x)
            sp.wait_ge(S("xn"), 8)
            for c in range(KE // 2):
                for x in range(2):
                    load_w2(1, 1, c, x)

            def next_w13(p):
                for c in range(KD // 2):
                    sp.wait_ge(S("w13_used"), p * 4 + (c + 1))
                    for x in range(2):
                        load_w13(p + 1, c, x)

            def next_w2(p, q, used):
                for c in range(KE // 2):
                    sp.wait_ge(S("w2_used"), used + (c + 1))
                    for x in range(2):
                        load_w2(p + 2, q, c, x)

            with sp.Fori(0, EP // 2 - 2) as it:
                for q in range(2):
                    next_w13(it * 2 + q)
                    next_w2(it * 2 + q, q, it * 4 + 2 * q)
            next_w13(EP - 4)
            next_w2(EP - 4, 0, 2 * (EP - 4))
            next_w13(EP - 3)
            next_w13(EP - 2)
            next_w2(EP - 3, 1, 2 * (EP - 3))
            for i in range(NT):
                sp.wait_ge(S("y_out"), i + 1)
                sp.dma_start(out_tok[:, i, :], xres[:, i, :]).then_inc(S("stored"), 16)
            sp.wait_ge(S("stored"), 16 * NT)

        @block.tensor
        def _(pe):
            mm = nc.tensor.matmul
            ident = K("ident")

            def norm_transposes(s):
                for kk in range(4):
                    ps = write(pe, ("hT", s, kk))
                    for k2 in range(2):
                        for i in range(NT):
                            if kk == 0 and k2 == 0:
                                pe.wait_ge(S("xn"), 2 * s + i + 1)
                            k = 2 * kk + k2
                            last = nc.tensor.transpose(ps[:, (k2 * NT + i) * P:(k2 * NT + i + 1) * P],
                                                       xn[s][:, i, k * P:(k + 1) * P], ident)
                    last.then_inc(*full(("hT", s, kk)))

            def normed(s, k):
                if k % 2 == 0:
                    drained(pe, ("hT", s, k // 2))

            def feature_major(key, wkey, m_in_slot, first=None):
                ps = write(pe, key)
                w = slot_view(wkey, KD)
                for j in range(2):
                    for k in range(KD):
                        if first is not None and j == 0:
                            normed(first, k)
                        c = (m_in_slot + j) * P
                        last = mm(ps[:, j * SEQ:(j + 1) * SEQ], w[:, k, c:c + P], hT[:, k, :],
                                  start=(k == 0), stop=(k == KD - 1))
                last.then_inc(*full(key))

            def token_major(key, wkey, i, lhs, nk=KD):
                ps = write(pe, key)
                w = slot_view(wkey, nk)
                for k in range(nk):
                    last = mm(ps[:, 0:512], lhs[k][:, i * P:(i + 1) * P], w[:, k, 0:512],
                              start=(k == 0), stop=(k == nk - 1))
                last.then_inc(*full(key))

            def halved(key):
                n = split_at[key]
                pe.wait_ge(S("low"), n + 1)
                if n < BY_TWO:
                    pe.wait_ge(S("low2"), n + 1)

            def by_parts(ps, a, b, start, stop):
                mm(ps, a[0], b[0], start=start, stop=False)
                mm(ps, a[0], b[1], start=False, stop=False)
                return mm(ps, a[1], b[0], start=False, stop=stop)

            def feature_major_by_parts(key, wkey, m_in_slot, x_hi, x_lo):
                ps = write(pe, key)
                w = parts_view(wkey, "p (k c) -> p k c", k=KD)
                for h in range(2):
                    c = (m_in_slot + h) * P
                    for k in range(KD):
                        last = by_parts(ps[:, h * SEQ:(h + 1) * SEQ], [x[:, k, c:c + P] for x in w], (x_hi[:, k, :], x_lo[:, k, :]),
                                        k == 0, k == KD - 1)
                last.then_inc(*full(key))

            pe.wait_ge(S("ident_in"), 16)

            def to_columns(t):
                rows = sum(r for _, r in PAR[t])
                pe.wait_ge(S(f"par_in{t}"), 16 * len(PAR[t]))
                ps = write(pe, ("par", t))
                nc.tensor.transpose(ps[:, 0:rows], parrow[0:rows, t, :], ident[0:rows, 0:rows]).then_inc(*full(("par", t)))

            to_columns(0)
            norm_transposes(0)
            for j in RW_ORDER:
                c = j // 2
                if c == 3:
                    arrived(pe, ("rw", c))
                    feature_major(("rw", j), ("rw", c), 0, 0)
                else:
                    halved(("rw", c))
                    pe.wait_ge(S("h0_low"), 1)
                    feature_major_by_parts(("rw", j), ("rw", c), 2 * (j % 2), hT_hi[0], hT0_lo)
                if j == RW_ORDER[0]:
                    for t in range(1, NPAR):
                        to_columns(t)
            pe.wait_ge(S("small_in"), 16 * 3)
            for key, lo, hi, part, wt in (("lw", 0, 64, 0, wua), ("la", 64, 128, 0, wua), ("lg", 0, 128, 1, gup)):
                if key == "la":
                    drained(pe, ("rw", 6))
                else:
                    pe.wait_ge(S("lora"), 1 + part)
                for j in range(2):
                    ps = write(pe, (key, j))
                    for h in range(2):
                        mt = 2 * j + h
                        last = mm(ps[:, h * SEQ:(h + 1) * SEQ], wt[lo:hi, mt * P:(mt + 1) * P], lora[lo:hi, part, :],
                                  start=True, stop=True)
                    last.then_inc(*full((key, j)))
            for j in range(4):
                arrived(pe, ("sb", j // 2))
                feature_major(("qk", j), ("sb", j // 2), 2 * (j % 2))
            arrived(pe, ("sb", 2))
            token_major(("v", 0), ("sb", 2), 0, [hT[:, k, :] for k in range(KD)])
            pe.wait_ge(S("kk_sq"), 1)
            pe.wait_ge(S("con_in"), 16)
            ps = write(pe, ("kn",))
            for p in range(PAIRS):
                last = mm(ps[0:HEADS, 0:SEQ], K("head_sum")[:, p * HEADS:(p + 1) * HEADS], tmp[:, p, :],
                          start=(p == 0), stop=(p == PAIRS - 1))
            last.then_inc(*full(("kn",)))
            token_major(("v", 1), ("sb", 2), 1, [hT[:, k, :] for k in range(KD)])

            def spread(name, sem):
                pe.wait_ge(S(sem), 1)
                for j in range(2):
                    ps = write(pe, (name, j))
                    for h in range(2):
                        p = 2 * j + h
                        last = mm(ps[:, h * SEQ:(h + 1) * SEQ], K("head_spread")[0:HEADS, p * P:(p + 1) * P],
                                  nmr[0:HEADS, :], start=True, stop=True)
                    last.then_inc(*full((name, j)))

            spread("kb", "kk_inv")

            def scores(ps, h, alone):
                o = DH * (h % 2)
                q, k = qk[o:o + DH, h // 2, :], qk[o:o + DH, PAIRS + h // 2, :]
                mm(ps[:, 0:SEQ], k[:, 0:P], q, start=True, stop=alone, skip_group_check=True)
                return mm(ps[:, SEQ:SEQ + P], k[:, P:SEQ], q[:, P:SEQ], start=alone, stop=alone, skip_group_check=True)

            for j in range(4):
                drained(pe, ("qk", j))
            for h in range(HEADS):
                ps = write(pe, ("z", h))
                scores(ps, h, True).then_inc(*full(("z", h)))
            pe.wait_ge(S("bon_raw"), 1)
            for j in range(2):
                ps = write(pe, ("bn", j))
                for h in range(2):
                    last = mm(ps[:, h * SEQ:(h + 1) * SEQ], K("head_block"), bon[:, 2 * j + h, :], start=True, stop=True)
                last.then_inc(*full(("bn", j)))
            def gates_of(j):
                if j < 4:
                    arrived(pe, ("gate", j // 2))
                    feature_major(("ga", j), ("gate", j // 2), 2 * (j % 2))
                else:
                    pe.wait_ge(S("h3_low"), 1)
                    halved(("gate", j // 2))
                    feature_major_by_parts(("ga", j), ("gate", j // 2), 2 * (j % 2), hT_hi[3], hT3_lo)

            def ada_sum(c):
                drained(pe, ("ad", c))
                ps = write(pe, ("as", c))
                if c in COLUMN_CHUNKS:
                    for j in range(4):
                        last = mm(ps[:, j:j + 1], modp[:, c % 2, j * P:(j + 1) * P], K("thirty_second")[:, 0:1],
                                  start=True, stop=True)
                else:
                    last = mm(ps[:, 0:512], K("thirty_second"), modp[:, c % 2, :], start=True, stop=True)
                last.then_inc(*full(("as", c)))

            def ada(c):
                if c:
                    ada_sum(c - 1)
                if c == ADA_CHUNKS:
                    return
                arrived(pe, ("ada", c))
                pe.wait_ge(S("cb"), 1)
                ps = write(pe, ("ad", c))
                w = slot_view(("ada", c), KD)
                for kk in range(2):
                    for j in range(4):
                        k = 2 * j + kk
                        last = mm(ps[32 * j:32 * j + 32, 0:512], cb[:, k, :], w[:, k, :], start=(kk == 0),
                                  stop=(kk == 1))
                last.then_inc(*full(("ad", c)))

            gates_of(0)
            gates_of(1)
            pe.wait_ge(S("kr_k"), 1)
            pe.wait_ge(S("bk_bar"), 1)
            for i in range(NT):
                for a in range(4):
                    ps = write(pe, ("tok", i, a))
                    for p in range(PAIRS):
                        t = slice(i * P, (i + 1) * P)
                        src = (kr[:, p, i, 0, :], bT[:, p, t], kT[:, p, t], vT[:, p, t])[a]
                        last = nc.tensor.transpose(ps[:, p * P:(p + 1) * P], src, ident)
                    last.then_inc(*full(("tok", i, a)))
            for h in range(HEADS):
                pe.wait_ge(S("att_sp"), h // 4 + 1)
                ps = write(pe, ("l", h))
                scores(ps, h, False)
                mm(ps[:, 0:SEQ], K("neg_suffix"), rz[:, h, 0:SEQ], start=False, stop=False, skip_group_check=True)
                mm(ps[:, P:SEQ], K("neg_ones"), rz[:, h, SEQ:SEQ + P], start=False, stop=False, skip_group_check=True)
                mm(ps[:, SEQ:SEQ + P], K("neg_suffix"), rz[:, h, SEQ:SEQ + P], start=False, stop=True,
                   skip_group_check=True).then_inc(*full(("l", h)))
            for i in range(NT):
                drained(pe, ("v", i))
            for p in range(PAIRS):
                if p == 2:
                    ada(0)
                pe.wait_ge(S("att_w"), p // 2 + 1)
                ps = write(pe, ("o", p))
                for h in range(2):
                    d = DH * h
                    n = 2 * p + h
                    mm(ps[d:d + DH, 0:SEQ], vtok[:, 0, n * DH:(n + 1) * DH], az[:, n, 0:SEQ], start=True, stop=False,
                       skip_group_check=True)
                    last = mm(ps[d:d + DH, P:SEQ], vtok[:, 1, n * DH:(n + 1) * DH], az[:, n, SEQ:SEQ + P],
                              start=False, stop=True, skip_group_check=True)
                last.then_inc(*full(("o", p)))

            pe.wait_ge(S("bk_hat"), 1)
            pe.wait_ge(S("kr_r"), 1)
            chunk = 1
            for i in range(NT):
                for h in range(HEADS):
                    o, p = DH * (h % 2), h // 2
                    ps = write(pe, ("g", i, h))
                    right = kr[o:o + DH, p, i, :, :].rearrange("p s t -> p (s t)")
                    mm(ps[:, 0:2 * P], bh[o:o + DH, p, i * P:(i + 1) * P], right, start=True, stop=True)
                    mm(ps[:, 2 * P:4 * P], kh[o:o + DH, p, i * P:(i + 1) * P], right, start=True,
                       stop=True).then_inc(*full(("g", i, h)))

                def group(key, q, left, right):
                    ps = write(pe, key)
                    for j in range(4):
                        last = mm(ps[:, j * P:(j + 1) * P], left(4 * q + j), right(4 * q + j), start=True, stop=True)
                    last.then_inc(*full(key))

                for q in range(2):
                    for h in range(4):
                        drained(pe, ("g", i, 4 * q + h))
                    group(("n", i, q), q, lambda h: gm[:, h, 0:P], lambda h: ident)
                for lv in range(1, LEVELS):
                    for q in range(2):
                        if lv == 1:
                            drained(pe, ("n", i, q))
                            pe.wait_ge(S("dt_first"), 2 * i + q + 1)
                        else:
                            drained(pe, ("d", i, lv - 1, q))
                            drained(pe, ("dt", i, lv - 1, q))
                        group(("x", i, lv, q), q, lambda h: gm[:, h, 0:P], lambda h: dd[:, h, :])
                    ada(chunk)
                    chunk += 1
                    for q in range(2):
                        drained(pe, ("x", i, lv, q))
                        if lv < LEVELS - 1:
                            group(("d", i, lv, q), q, lambda h: ddT[:, h, :], lambda h: xx[:, h, :])
                        group(("dt", i, lv, q), q, lambda h: xx[:, h, :], lambda h: ddT[:, h, :])
                for a in range(4):
                    drained(pe, ("tok", i, a))
                for q in range(2):
                    group(("w1", i, q), q, lambda h: gm[:, h, 2 * P:3 * P], lambda h: vp[:, i, h, :])
                ada(chunk)
                chunk += 1
                for q in range(2):
                    drained(pe, ("w1", i, q))
                    drained(pe, ("dt", i, LEVELS - 1, q))
                    group(("u", i, q), q, lambda h: ddT[:, h, :], lambda h: zb[:, i, h, :])
                for q in range(2):
                    drained(pe, ("u", i, q))
                ps = write(pe, ("ry", i))
                for h in range(HEADS):
                    o, p = DH * (h % 2), h // 2
                    last = mm(ps[o:o + DH, p * P:(p + 1) * P], tk[:, h, :], gm[:, h, P:2 * P], start=True, stop=True)
                last.then_inc(*full(("ry", i)))

                def psi_of(c):
                    r = slice(CH * (c % 2), CH * (c % 2) + CH)
                    ps = write(pe, ("psi", c))
                    for p in range(PAIRS):
                        f = slice(p * P, (p + 1) * P)
                        mm(ps[:, f], btok[r, i, f], up[r, 2 * p:2 * p + 2, :].rearrange("p h d -> p (h d)"),
                           start=True, stop=False)
                        last = mm(ps[:, f], ktok[r, i, f], vp[r, i, 2 * p:2 * p + 2, 0:DH], start=False, stop=True)
                    last.then_inc(*full(("psi", c)))

                def phi_of(c):
                    r = slice(CH * (c % 2), CH * (c % 2) + CH)
                    ps = write(pe, ("phi", c))
                    for p in range(PAIRS):
                        f = slice(p * P, (p + 1) * P)
                        last = mm(ps[:, f], tk[r, 2 * p:2 * p + 2, :].rearrange("p h d -> p (h d)"), btok[r, i, f],
                                  start=True, stop=True)
                    last.then_inc(*full(("phi", c)))

                def state(c):
                    drained(pe, ("s", c - 1) if c > 1 else ("psi", 0))
                    drained(pe, ("psi", c))
                    pe.wait_ge(S("phi"), c)
                    ps = write(pe, ("s", c))
                    for p in range(PAIRS):
                        last = mm(ps[:, p * P:(p + 1) * P], phi[:, c - 1, p, :], psi[:, c - 1, p, :], start=True, stop=True)
                    last.then_inc(*full(("s", c)))

                def y_of():
                    ps = write(pe, ("y", i))
                    for h in range(HEADS):
                        o, p = DH * (h % 2), h // 2
                        dst = ps[o:o + DH, p * P:(p + 1) * P]
                        mm(dst, up[:, h, :], gm[:, h, P:2 * P], start=(p == 0), stop=False, skip_group_check=True)
                        mm(dst, vp[:, i, h, 0:DH], gm[:, h, 3 * P:4 * P], start=False, stop=False, skip_group_check=True)
                    drained(pe, ("ry", i))
                    for c in (2 * i, 2 * i + 1):
                        if c == 0:
                            continue
                        drained(pe, ("psi", 0) if c == 1 else ("s", c - 1))
                        for p in range(PAIRS):
                            t = slice(p * P + CH * (c % 2), p * P + CH * (c % 2) + CH)
                            last = mm(ps[:, t], psi[:, c - 1, p, :], ryT[:, p, c * CH:(c + 1) * CH], start=False,
                                      stop=True, skip_group_check=True)
                    last.then_inc(*full(("y", i)))

                if i == 0:
                    psi_of(0)
                    psi_of(1)
                    phi_of(1)
                    y_of()
                    state(1)
                else:
                    psi_of(2)
                    phi_of(2)
                    state(2)
                    y_of()

            for i in range(NT):
                drained(pe, ("y", i))
            for j in range(2):
                ps = write(pe, ("m", j))
                for h in range(2):
                    last = mm(ps[:, h * SEQ:(h + 1) * SEQ], K("head_mean"), yT[:, 2 * j + h, :], start=True, stop=True)
                last.then_inc(*full(("m", j)))
            for j in range(2, 5):
                gates_of(j)
            pe.wait_ge(S("y_sq"), 1)
            ps = write(pe, ("vn",))
            for p in range(PAIRS):
                last = mm(ps[0:HEADS, 0:SEQ], K("head_sum")[:, p * HEADS:(p + 1) * HEADS], tmp[:, p, :],
                          start=(p == 0), stop=(p == PAIRS - 1))
            last.then_inc(*full(("vn",)))
            for j in range(5, 7):
                gates_of(j)
            spread("vb", "y_inv")
            gates_of(7)

            def branch_out(dm, half):
                ps = write(pe, ("mg", dm)) if half == 0 else bank[BANK["mg", dm][0]]
                wkey, src = (("sb_out", (osb_hi, osb_lo)), ("rw_out", (orw_hi, orw_lo)))[half]
                w = parts_view(wkey, "p (k c) -> p k c", k=PAIRS)
                for k in range(PAIRS):
                    last = by_parts(ps[:, half * SEQ:(half + 1) * SEQ], [x[:, k, dm * P:(dm + 1) * P] for x in w],
                                    [x[:, k, :] for x in src], k == 0, k == PAIRS - 1)
                if half:
                    last.then_inc(*full(("mg", dm)))

            halved("sb_out")
            pe.wait_ge(S("osb_low"), 1)
            for dm in range(KD):
                branch_out(dm, 0)
            halved("rw_out")
            pe.wait_ge(S("orw_low"), 1)
            for dm in range(KD):
                branch_out(dm, 1)
            pe.wait_ge(S("merged"), KD)
            for n in range(2):
                arrived(pe, ("wo", n))
                for i in range(NT):
                    token_major(("mo", i, n), ("wo", n), i, gates[0:KD])
            norm_transposes(1)
            for f in range(KF):
                c = f // 2
                halved(("ff", c))
                ps = write(pe, ("ff", f))
                w = parts_view(("ff", c), "p (g k c) -> p g k c", g=2, k=KD)
                for gu in range(2):
                    for k in range(KD):
                        if f == 0 and gu == 0:
                            normed(1, k)
                        last = by_parts(ps[:, gu * SEQ:(gu + 1) * SEQ], [x[:, gu, k, (f % 2) * P:(f % 2 + 1) * P] for x in w],
                                        (hT_hi[1][:, k, :], hT_lo[:, k, :]), k == 0, k == KD - 1)
                last.then_inc(*full(("ff", f)))
            ps = {}
            for n in range(2):
                for i in range(NT):
                    ps[i, n] = write(pe, ("dn", i, n))
            for c in range(n_down):
                halved(("down", c))
                nk = min(4, KF - 4 * c)
                w = parts_view(("down", c), "p (k c) -> p k c", k=nk)
                order = [(kk, i, n) for kk in range(nk) for n in range(2) for i in range(NT)]
                if c == n_down - 1:
                    order = [(kk, i, n) for i in range(NT) for n in range(2) for kk in range(nk)]
                for kk in range(0, nk, 2):
                    pe.wait_ge(S("f_low"), (4 * c + kk) // 2 + 1)
                for kk, i, n in order:
                    k = 4 * c + kk
                    last = by_parts(ps[i, n][:, 0:512], [x[:, k, i * P:(i + 1) * P] for x in (fh, fT_lo)],
                                    [x[:, kk, n * 512:(n + 1) * 512] for x in w], k == 0, k == KF - 1)
                    if k == KF - 1:
                        last.then_inc(*full(("dn", i, n)))
                if c < n_down - 1:
                    last.then_inc(S("down_used"), 1)

            norm_transposes(2)
            for n in range(2):
                halved(("in2", n))
                w = parts_view(("in2", n), "p (k c) -> p k c", k=KD)
                for i in range(NT):
                    ps = write(pe, ("uz", i, n))
                    for k in range(KD):
                        if n == 0 and i == 0:
                            normed(2, k)
                        last = by_parts(ps[:, 0:512], [x[:, k, i * P:(i + 1) * P] for x in (hT_hi[2], hT_lo)],
                                        [x[:, k, :] for x in w], k == 0, k == KD - 1)
                    last.then_inc(*full(("uz", i, n)))
            for j in range(7):
                c = 2 + j // 2
                halved(("in2", c))
                w = parts_view(("in2", c), "p (k c) -> p k c", k=KD)
                ps = write(pe, ("xb", j))
                for h in range(2):
                    m = 2 * (j % 2) + h
                    for k in range(KD):
                        last = by_parts(ps[:, h * SEQ:(h + 1) * SEQ], [x[:, k, m * P:(m + 1) * P] for x in w],
                                        (hT_hi[2][:, k, :], hT_lo[:, k, :]), k == 0, k == KD - 1)
                last.then_inc(*full(("xb", j)))
            ps = write(pe, ("dt2",))
            for i in range(NT):
                for k in range(KD):
                    last = by_parts(ps[:, i * 16:i * 16 + SH], [x[:, k, i * P:(i + 1) * P] for x in (hT_hi[2], hT_lo)],
                                    [x[:, k, 256:256 + SH] for x in w], k == 0, k == KD - 1)
            last.then_inc(*full(("dt2",)))
            pe.wait_ge(S("pool_in"), 16 * 5)
            for i in range(NT):
                drained(pe, ("uz", i, 0))
            ps = write(pe, ("pl",))
            for g in range(GRP):
                o, c0 = 64 * (g % 2), SEQ * (g // 2)
                mm(ps[o:o + 64, c0:c0 + SEQ], u[:, 0, g * 64:(g + 1) * 64], band[:, g, 0:SEQ], start=(g < 2), stop=False,
                   skip_group_check=True)
                last = mm(ps[o:o + 64, c0 + P:c0 + SEQ], u[:, 1, g * 64:(g + 1) * 64], band[:, g, SEQ:SEQ + P],
                          start=False, stop=True, skip_group_check=True)
            last.then_inc(*full(("pl",)))
            pe.wait_ge(S("da"), 1)
            ps = write(pe, ("cs",))
            for i in range(NT):
                mm(ps[:, i * 16:i * 16 + SH], K("causal"), da[:, i, :], start=True, stop=True)
            mm(ps[:, 32:32 + SH], K("after"), da[:, 0, :], start=True, stop=True).then_inc(*full(("cs",)))
            drained(pe, ("pl",))
            ps = write(pe, ("pm",))
            for g in range(GRP):
                o, c0 = 64 * (g % 2), SEQ * (g // 2)
                last = mm(ps[o:o + 64, c0:c0 + SEQ], wp[o:o + 64, g // 2, :], dif[o:o + 64, g // 2, :], start=True,
                          stop=True)
            last.then_inc(*full(("pm",)))
            for i in range(NT):
                for q in range(3):
                    ps = write(pe, ("rb", i, q))
                    for j in range(4):
                        last = mm(ps[:, j * P:(j + 1) * P], da[:, i, 4 * q + j:4 * q + j + 1].to_broadcast([P, P]),
                                  K("causal"), start=True, stop=True)
                    last.then_inc(*full(("rb", i, q)))
            pe.wait_ge(S("xs"), 7)
            for i in range(NT):
                ps = write(pe, ("cb", i))
                for g in range(GRP):
                    t = slice(i * P, (i + 1) * P)
                    last = mm(ps[:, g * P:(g + 1) * P], xs[:, 6 + g, t], xs[:, 10 + g, t], start=True, stop=True)
                last.then_inc(*full(("cb", i)))

            def transposes(key, pairs):
                ps = write(pe, key)
                for c, src in pairs:
                    last = nc.tensor.transpose(ps[:, c * P:(c + 1) * P], src, ident)
                last.then_inc(*full(key))

            for i in range(NT):
                for a in range(2):
                    transposes(("xt", i, a), [(c, xs[:, 4 * a + c, i * P:(i + 1) * P]) for c in range(4 if a == 0 else 2)])
            transposes(("bt",), [(g, xs[:, 6 + g, 0:P]) for g in range(GRP)])

            def y_diag(i):
                pe.wait_ge(S("dec"), i + 1)
                pe.wait_ge(S("xc"), i + 1)
                for a in range(2):
                    ps = write(pe, ("yd", i, a))
                    for h in range(8 * a, min(8 * a + 8, SH)):
                        c = (h - 8 * a) * DH
                        last = mm(ps[:, c:c + DH], dec[:, i, h, :], xc[:, i, h * DH:(h + 1) * DH], start=True, stop=True)
                    last.then_inc(*full(("yd", i, a)))

            GW = SR * DH
            y_diag(0)
            pe.wait_ge(S("xde"), 1)
            drained(pe, ("bt",))
            for a in range(2):
                ps = write(pe, ("cst", a))
                for g in range(2 * a, 2 * a + 2):
                    c = (g - 2 * a) * GW
                    last = mm(ps[:, c:c + GW], btk[:, g * P:(g + 1) * P], xde[:, g * GW:(g + 1) * GW], start=True, stop=True)
                last.then_inc(*full(("cst", a)))
            y_diag(1)
            for a in range(2):
                drained(pe, ("cst", a))
                ps = write(pe, ("yo", a))
                for g in range(2 * a, 2 * a + 2):
                    c = (g - 2 * a) * GW
                    last = mm(ps[:, c:c + GW], xs[:, 10 + g, P:SEQ], st[:, g * GW:(g + 1) * GW], start=True, stop=True)
                last.then_inc(*full(("yo", a)))
            for i in range(NT):
                pe.wait_ge(S("ys"), i + 1)
                for a in range(2):
                    transposes(("mt", i, a), [(c, ys[:, i, (4 * a + c) * P:(4 * a + c + 1) * P])
                                              for c in range(4 if a == 0 else 2)])
                if i == 0:
                    drained(pe, ("pm",))
                for a in range(2):
                    drained(pe, ("mt", i, a))
                for n in range(2):
                    arrived(pe, ("out2", n))
                    token_major(("mx", i, n), ("out2", n), i, [mixT[:, k, :] for k in range(KD)])
            norm_transposes(3)
            pe.wait_ge(S("router_in"), 16 * 4)
            ps = write(pe, ("rt",))
            for i in range(NT):
                for k in range(KD):
                    if i == 0:
                        normed(3, k)
                    last = mm(ps[:, i * 64:i * 64 + 36], hT[:, k, i * P:(i + 1) * P], wgr[:, k, :], start=(k == 0),
                              stop=(k == KD - 1))
            last.then_inc(*full(("rt",)))

            pe.wait_ge(S("chosen"), 1)
            ps = write(pe, ("rk",))
            sel = rtb[4][:, 0:NT * EXPERTS].rearrange("p (i c) -> p i c", i=NT)
            for n, terms in enumerate(((("strict", 0),), (("ones", 0), ("strict", 1)), (("ones", 0), ("ones", 1)))):
                for j, (name, i) in enumerate(terms):
                    last = mm(ps[:, n * EXPERTS:(n + 1) * EXPERTS], K(name), sel[:, i, :], start=(j == 0),
                              stop=(j == len(terms) - 1))
            last.then_inc(*full(("rk",)))

            for b in range(8):
                uses = max(t for bb, t in BANK.values() if bb == b) + 1
                pe.wait_ge(bank_free[b], uses)

            def clear_sums():
                pe.wait_ge(S("zero"), 1)
                for b in range(4):
                    mm(bank[b][:, 0:512], rs[0:1, 0:1].to_broadcast([1, P]), junk[0:1, 0:512], start=True, stop=False,
                       skip_group_check=True)

            def gather(p):
                pe.wait_ge(S("one"), p + 1)
                if not isinstance(p, int) or p > 1:
                    pe.wait_ge(S("y_slots"), p * 2 - 2)
                for k in range(KD):
                    for i in range(NT):
                        last = mm(bank[4 + k // 4][:, (k % 4) * P:(k % 4 + 1) * P], xn[3][:, i, k * P:(k + 1) * P],
                                  one[:, 2 * i:2 * i + 2, :].rearrange("p x s -> p (x s)"), start=(i == 0), stop=(i == NT - 1))
                    if k % 4 == 3:
                        last.then_inc(S("gathered"), 1)

            def both(b, x):
                return bank[b][x * CAP:(x + 1) * CAP, 0:512]

            def hidden(p):
                pe.wait_ge(S("hg"), p * 2 + 2)
                if not isinstance(p, int) or p > 0:
                    pe.wait_ge(S("ac_turned"), p)
                    pe.wait_ge(S("w_turned"), p)
                for c in range(KD // 2):
                    pe.wait_ge(w13_full[c], p * 32 + 32)
                    for k in (2 * c, 2 * c + 1):
                        for half in range(2):
                            for x in range(2):
                                last = mm(both(6 + half, x), hg[:, k, x * CAP:(x + 1) * CAP],
                                          w13s[x][:, k, half * EF:(half + 1) * EF], start=(k == 0), stop=(k == KD - 1))
                    last.then_inc(S("w13_used"), 1)

            def turn_ac(p):
                pe.wait_ge(S("ac"), p + 1)
                for f in range(KE):
                    last = nc.tensor.transpose(bank[6][:, f * P:(f + 1) * P], ac[:, 0, f * P:(f + 1) * P], ident)
                last.then_inc(S("turns"), 1)

            def turn_weights(p):
                pe.wait_ge(S("onew"), p + 1)
                for i in range(NT):
                    last = nc.tensor.transpose(bank[7][:, i * P:(i + 1) * P],
                                               onew[:, 2 * i:2 * i + 2, :].rearrange("p x s -> p (x s)"), ident)
                last.then_inc(S("w_turns"), 1)

            def expert_out(p, q, turn):
                pe.wait_ge(S("ac_turned"), p + 1)
                pe.wait_ge(S("hg"), p * 2 + 4 if not isinstance(p, int) or p < EP - 1 else 2 * EP)
                for c in range(KE // 2):
                    pe.wait_ge(w2_full[q][c], turn * 32 + 32)
                    for f in (2 * c, 2 * c + 1):
                        for n in range(2):
                            for x in range(2):
                                last = mm(both(4 + n, x), acT[:, 0, f, x * CAP:(x + 1) * CAP],
                                          w2s[q][x][f // 2][:, f % 2, n * 512:(n + 1) * 512], start=(f == 0), stop=(f == KE - 1))
                    last.then_inc(S("w2_used"), 1)

            def combine(p):
                pe.wait_ge(S("y_slots"), p * 2 + 2)
                pe.wait_ge(S("w_turned"), p + 1)
                for i in range(NT):
                    for n in range(2):
                        last = mm(bank[2 * i + n][:, 0:512], onewT[:, i * P:(i + 1) * P], yslot[n],
                                  start=False, stop=False, skip_group_check=True)
                    if isinstance(p, int) and p == EP - 1:
                        last.then_inc(S("summed"), 1)

            pe.wait_ge(S("crowded"), 1)
            many = pe.value_load(crowded[0:1, 0:1])
            with pe.If(many > 0):
                clear_sums()
                with pe.Fori(0, EP // 2) as two:
                    for q in range(2):
                        it = two * 2 + q
                        for c in range(KD // 2):
                            pe.wait_ge(w13_full[c], it * 32 + 32)
                        for x in range(2):
                            for i in range(NT):
                                for half in range(2):
                                    for k in range(KD):
                                        last = mm(bank[4 + 2 * i + half][:, 0:512], hT[:, k, i * P:(i + 1) * P],
                                                  w13s[x][:, k, half * EF:(half + 1) * EF], start=(k == 0), stop=(k == KD - 1))
                                    last.then_inc(S("hidden"), 1)
                            for i in range(NT):
                                pe.wait_ge(S("act_out"), it * 4 + (2 * x + i + 1))
                                for f in range(KE):
                                    last = nc.tensor.transpose(bank[4 + 2 * i][:, f * P:(f + 1) * P],
                                                               ac[:, i, f * P:(f + 1) * P], ident)
                                last.then_inc(S("turns"), 1)
                            for c in range(KE // 2):
                                pe.wait_ge(w2_full[q][c], two * 32 + 32)
                            for i in range(NT):
                                pe.wait_ge(S("turned"), it * 4 + (2 * x + i + 1))
                                for n in range(2):
                                    for f in range(KE):
                                        last = mm(bank[2 * i + n][:, 0:512], acT[:, i, f, :],
                                                  w2s[q][x][f // 2][:, f % 2, n * 512:(n + 1) * 512],
                                                  start=False, stop=False, skip_group_check=True)
                                if x == 1:
                                    last.then_inc(*((S("w13_used"), 4) if i == 0 else (S("w2_used"), 2)))
            with pe.Else():
                gather(0)
                hidden(0)
                clear_sums()
                gather(1)
                turn_ac(0)
                turn_weights(0)
                expert_out(0, 0, 0)
                with pe.Fori(0, EP // 2 - 1) as it:
                    for q in (1, 0):
                        p = it * 2 + (2 - q)
                        hidden(p)
                        gather(p + 1)
                        turn_ac(p)
                        combine(p - 1)
                        turn_weights(p)
                        expert_out(p, q, it + (1 - q))
                hidden(EP - 1)
                turn_ac(EP - 1)
                combine(EP - 2)
                turn_weights(EP - 1)
                expert_out(EP - 1, 1, EP // 2 - 1)
                combine(EP - 1)

        @block.scalar
        def _(act):
            A_ = nc.scalar.activation

            def bcast(dst, src, n):
                return act.dma_start(dst, src.partition_broadcast(P)).then_inc(S(n), 16)

            squares = [0]

            def next_square():
                if squares[0]:
                    act.wait_ge(S("sq"), squares[0])
                squares[0] += 1

            def pre_norm(n, ready):
                for i in range(NT):
                    ready(i)
                    next_square()
                    A_(junk, xres[:, i, :], ACT.Square, accum_out=ss[n][:, i:i + 1]).then_inc(S("sq"), 1)

            def root(n):
                act.wait_ge(S("ms"), n + 1)
                A_(sd[n][:, 0:NT], ms[n][:, 0:NT], ACT.Sqrt).then_inc(S("sd"), 1)

            def load_root(n):
                act.wait_ge(S("sd"), 1)
                A_(spare[:, n:n + 1], sd[0][:, 0:1], ACT.Sqrt)

            def transposed(s, scale, bias):
                for kk in (0, 2):
                    ps = filled(act, ("hT", s, kk))
                    for k2 in range(2):
                        k = 2 * kk + k2
                        kw = {"bias": bias(k)} if bias else {}
                        ins = A_(hT[:, k, :], ps[:, k2 * SEQ:(k2 + 1) * SEQ], ACT.Identity, scale=scale(k), **kw)
                    ins.then_inc(*free(("hT", s, kk)))

            def post_norm(n, name):
                for j in range(4):
                    half, i = (j // 2, j % 2) if name == "mo" else (j % 2, j // 2)
                    ps = filled(act, (name, i, half))
                    next_square()
                    A_(junk[:, 0:512], ps[:, :], ACT.Square, accum_out=ss[n][:, 2 * i + half:2 * i + half + 1]
                       ).then_inc(S("sq"), 1)
                root(n)

            def high_parts(n):
                arrived(act, SPLIT[n][0])
                if n >= 3:
                    consumed(act, SPLIT[n - 3][1])
                r, words = split_words(n)
                for a in range(2):
                    f = slice(a * words // 2, (a + 1) * words // 2)
                    A_(high_of(n)[:, f], ring[:, r, f], ACT.Copy).then_inc(S("high"), 1)

            def transposed_high(s, scale, bias):
                for kk in range(4):
                    ps = filled(act, ("hT", s, kk))
                    for k2 in range(2):
                        k = 2 * kk + k2
                        kw = {"bias": bias(k)} if bias else {}
                        ins = A_(hT_hi[s][:, k, :], ps[:, k2 * SEQ:(k2 + 1) * SEQ], ACT.Identity, scale=scale(k), **kw)
                    ins.then_inc(S("h_high"), 1)

            pre_norm(0, lambda i: act.wait_ge(S("x_in"), 16))
            root(0)
            drained(act, ("par", 0))
            transposed(0, lambda k: par("norm_mix_pre", k), None)
            for kk in range(4):
                drained(act, ("hT", 0, kk))
            A_(hT_hi[0][:, :, :], hT[:, :, :], ACT.Copy).then_inc(S("h0_high"), 1)
            high_parts(0)
            act.dma_start(B("lvlf"), A["levels"]).then_inc(S("lvl_in"), 16)
            act.dma_start(wua[0:64, :], A["w_up"][0]).then_inc(S("small_in"), 16)
            act.dma_start(wua[64:128, :], A["a_up"][0]).then_inc(S("small_in"), 16)
            act.dma_start(gup[:, :], A["g_up"][0]).then_inc(S("small_in"), 16)
            bcast(g1, A["b_ada_2"][0, 2 * D:3 * D], "gate_in")
            bcast(g2, A["b_ada_2"][0, 5 * D:6 * D], "gate_in")
            bcast(dtb, A["dt_bias_2"][0], "router_in")
            act.dma_start(wgr[:, :, 0:EG], A["w_group_2"][0].rearrange("(k p) c -> p k c", p=P)).then_inc(S("router_in"), 16)
            act.dma_start(wgr[:, :, EG:36], A["w_router_2"][0].rearrange("(k p) c -> p k c", p=P)).then_inc(S("router_in"), 16)
            bcast(rbias[:, 0:EG], A["b_group_2"][0], "router_in")
            bcast(rbias[:, EG:36], A["b_router_2"][0], "par2_in")
            bcast(alog, A["a_log_2"][0], "par2_in")
            bcast(dsk, A["d_skip_2"][0], "par2_in")
            act.wait_ge(S("omu"), 1)

            def shifted(m):
                if m < 4:
                    return rT[:, m, :]
                if m < 8:
                    return kT[:, m - 4, :]
                return vT[:, m - 8, :] if m < 12 else lora[:, m - 12, :]

            for j in RW_ORDER:
                ps = filled(act, ("rw", j))
                for h in range(2):
                    ins = A_(shifted(2 * j + h), ps[:, h * SEQ:(h + 1) * SEQ], ACT.Identity, scale=omu[:, 2 * j + h:2 * j + h + 1])
                ins.then_inc(S("rw_own"), 1)
                if j in (6, 3):
                    high_parts(1 if j == 6 else 2)
            for t in range(1, NPAR):
                drained(act, ("par", t))
            drained(act, ("rw", 6))
            A_(lora[0:64, 0, :], lora[0:64, 0, :], ACT.Tanh).then_inc(S("lora"), 1)
            A_(lora[:, 1, :], lora[:, 1, :], ACT.Sigmoid).then_inc(S("lora"), 1)
            for key, dst, bias in (("lw", lw, "w0"), ("la", aT, "a0")):
                for j in range(2):
                    ps = filled(act, (key, j))
                    for h in range(2):
                        ins = A_(dst[:, 2 * j + h, :], ps[:, h * SEQ:(h + 1) * SEQ], ACT.Sigmoid, bias=par(bias, 2 * j + h))
                    ins.then_inc(*free((key, j)))
            for j in range(2):
                ps = filled(act, ("lg", j))
                A_(gT[:, 2 * j:2 * j + 2, :].rearrange("p a b -> p (a b)"), ps[:, :], ACT.Copy).then_inc(*free(("lg", j)))
            act.wait_ge(S("kk_raw"), 1)
            A_(tmp, kkT, ACT.Square).then_inc(S("kk_sq"), 1)
            for j in range(2):
                ps = filled(act, ("qk", j))
                A_(qk[:, 2 * j:2 * j + 2, :].rearrange("p a b -> p (a b)"), ps[:, :], ACT.Copy, scale=DH ** -0.5
                   ).then_inc(*free(("qk", j)))
            ps = filled(act, ("kn",))
            A_(nmr[0:HEADS, :], ps[0:HEADS, 0:SEQ], ACT.Sqrt).then_inc(*free(("kn",)))
            A_(csil, par("c_2", 0, KD), ACT.Silu).then_inc(S("csil"), 1)
            act.wait_ge(S("ex"), 1)
            A_(aT, cum, ACT.Exp, scale=DECAY).then_inc(S("e_inc"), 1)
            A_(lw, lw, ACT.Exp, scale=DECAY).then_inc(S("e_exc"), 1)
            A_(tmp, cum, ACT.Exp, scale=-DECAY).then_inc(S("e_inv"), 1)
            A_(pc, total, ACT.Exp, scale=DECAY).then_inc(S("pc"), 1)
            for half in range(2):
                for h in range(4):
                    drained(act, ("z", 4 * half + h))
                A_(az[:, 4 * half:4 * half + 4, :], az[:, 4 * half:4 * half + 4, :], ACT.Exp).then_inc(S("att_e"), 1)
            act.wait_ge(S("to_end"), 1)
            A_(cum, cum, ACT.Exp, scale=DECAY).then_inc(S("e_suf"), 1)
            for half in range(2):
                act.wait_ge(S("att_e"), half + 1)
                A_(az[:, 4 * half:4 * half + 4, :], az[:, 4 * half:4 * half + 4, :], ACT.Ln, bias=1.0).then_inc(S("att_ln"), 1)
            def gates_of(j):
                ps = filled(act, ("ga", j))
                for h in range(2):
                    ins = A_(gates[2 * j + h], ps[:, h * SEQ:(h + 1) * SEQ], ACT.Sigmoid, bias=par("b_gate", 2 * j + h))
                ins.then_inc(*free(("ga", j)))

            gates_of(0)
            gates_of(1)
            for i in range(NT):
                ps = filled(act, ("tok", i, 0))
                A_(zb[:, i, :, DH:P], ps[:, :].rearrange("p (h d) -> p h d", h=HEADS), ACT.Copy).then_inc(*free(("tok", i, 0)))
                ps = filled(act, ("tok", i, 1))
                A_(btok[:, i, :], ps[:, :], ACT.Copy).then_inc(*free(("tok", i, 1)))
            for half in range(2):
                for h in range(4):
                    drained(act, ("l", 4 * half + h))
                A_(az[:, 4 * half:4 * half + 4, :], az[:, 4 * half:4 * half + 4, :], ACT.Exp).then_inc(S("att_x"), 1)
            def ada_rows(c):
                ps = filled(act, ("ad", c))
                A_(modp[:, c % 2, :], ps[:, :], ACT.Copy).then_inc(*free(("ad", c)))

            for p in range(PAIRS):
                if p == 2:
                    ada_rows(0)
                ps = filled(act, ("o", p))
                A_(osb[:, p, :], ps[:, 0:SEQ], ACT.Copy).then_inc(*free(("o", p)))

            c = 1
            for i in range(NT):
                for lv in range(1, LEVELS):
                    for q in range(2):
                        ps = filled(act, ("x", i, lv, q))
                        A_(xx[:, 4 * q:4 * q + 4, :], ps[:, :].rearrange("p (h t) -> p h t", h=4), ACT.Copy
                           ).then_inc(*free(("x", i, lv, q)))
                    ada_rows(c)
                    c += 1
                for q in range(2):
                    ps = filled(act, ("w1", i, q))
                    A_(zb[:, i, 4 * q:4 * q + 4, 0:DH], ps[:, :].rearrange("p (h t) -> p h t", h=4)[:, :, 0:DH], ACT.Copy
                       ).then_inc(*free(("w1", i, q)))
                if c < ADA_CHUNKS:
                    ada_rows(c)
                c += 1
                for q in range(2):
                    ps = filled(act, ("u", i, q))
                    v = ps[:, :].rearrange("p (h t) -> p h t", h=4)
                    A_(up[:, 4 * q:4 * q + 4, :], v[:, :, 0:DH], ACT.Copy)
                    A_(tk[:, 4 * q:4 * q + 4, :], v[:, :, DH:P], ACT.Copy).then_inc(*free(("u", i, q)))
                ps = filled(act, ("y", i))
                A_(yT[:, :, i * P:(i + 1) * P], ps[:, :].rearrange("p (h t) -> p h t", h=4), ACT.Copy).then_inc(*free(("y", i)))

            for j in range(2):
                drained(act, ("m", j))
            A_(tmp, yT, ACT.Square).then_inc(S("y_sq"), 1)
            A_(hT_hi[3][:, :, :], hT[:, :, :], ACT.Copy).then_inc(S("h3_high"), 1)
            high_parts(N_RW)
            high_parts(N_RW + 1)
            for p in range(PAIRS):
                drained(act, ("o", p))
            A_(osb_hi[:, :, :], osb, ACT.Copy).then_inc(S("osb_high"), 1)
            for j in range(2, 5):
                gates_of(j)
            drained(act, ("vn",))
            A_(nmr[0:HEADS, :], nmr[0:HEADS, :], ACT.Sqrt).then_inc(S("y_sd"), 1)
            high_parts(N_RW + 2)
            for j in range(5, 7):
                gates_of(j)
            high_parts(N_RW + 3)
            gates_of(7)
            act.wait_ge(S("orw"), 1)
            A_(orw_hi[:, :, :], orw, ACT.Copy).then_inc(S("orw_high"), 1)
            drained(act, ("mg", 0))
            bcast(npost, A["norm_mix_post"][0], "npost_in")
            filled(act, ("mg", KD - 1))
            high_parts(N_FF)
            load_root(0)
            post_norm(1, "mo")
            pre_norm(2, lambda i: act.wait_ge(S("x_new"), i + 1))
            root(2)
            bcast(fpost, A["norm_ffn_post"][0], "post_in")
            transposed_high(1, lambda k: par("norm_ffn_pre", k), None)
            high_parts(N_FF + 1)
            high_parts(N_FF + 2)
            for f in range(KF):
                ps = filled(act, ("ff", f))
                if f >= 2:
                    drained(act, ("ff", f - 2))
                A_(sil[:, f % 2, :], ps[:, 0:SEQ], ACT.Silu).then_inc(S("sil"), 1)
                if f % 2:
                    drained(act, ("ff", f - 1))
                    drained(act, ("ff", f))
                    A_(fh[:, f - 1:f + 1, :], fT[:, f - 1:f + 1, :], ACT.Copy).then_inc(S("f_high"), 1)
                    high_parts(N_FF + f // 2 + 3)
            for n in range(N_FF + KF // 2 + 3, BY_TWO + 1):
                high_parts(n)
            load_root(1)
            post_norm(3, "dn")
            pre_norm(4, lambda i: act.wait_ge(S("x_new"), 2 + i + 1))
            root(4)
            act.wait_ge(S("mod"), 1)
            act.dma_start(band, A["bands"].rearrange("p (g t) -> p g t", g=GRP)).then_inc(S("pool_in"), 16)
            for g in range(GRP):
                act.dma_start(wp[64 * (g % 2):64 * (g % 2) + 64, g // 2, :], A["w_pool_2"][0, g]).then_inc(S("pool_in"), 16)
            transposed_high(2, lambda k: modc[:, 8 + k:9 + k], lambda k: modc[:, k:k + 1])
            high_parts(BY_TWO + 1)
            high_parts(BY_TWO + 2)
            for n in range(2):
                for i in range(NT):
                    ps = filled(act, ("uz", i, n))
                    if n == 0:
                        A_(u[:, i, :], ps[:, 0:POOL], ACT.Copy)
                        A_(sz[:, i, 0:256], ps[:, POOL:512], ACT.Silu).then_inc(*free(("uz", i, 0)))
                    else:
                        A_(sz[:, i, 256:SSD], ps[:, :], ACT.Silu).then_inc(*free(("uz", i, 1)))
                high_parts(BY_TWO + 3 + n)
            for j in range(7):
                ps = filled(act, ("xb", j))
                A_(xraw[:, 2 * j:2 * j + 2, :], ps[:, :].rearrange("p (m t) -> p m t", m=2), ACT.Copy)
                for h in range(2):
                    m = 2 * j + h
                    ins = A_(xs[:, m, :], ps[:, h * SEQ:(h + 1) * SEQ], ACT.Identity, scale=par("conv_w_2", 3 * MX + m),
                             bias=par("conv_b_2", m))
                ins.then_inc(*free(("xb", j)))
                if j == 1:
                    high_parts(BY_TWO + 5)
                if j >= 1:
                    act.wait_ge(S("conv"), j)
                    A_(xs[:, 2 * j - 2:2 * j, :], xs[:, 2 * j - 2:2 * j, :], ACT.Silu).then_inc(S("xs"), 1)
            act.wait_ge(S("conv"), 7)
            A_(xs[:, 12:14, :], xs[:, 12:14, :], ACT.Silu).then_inc(S("xs"), 1)
            act.wait_ge(S("par2_in"), 16 * 3)
            act.wait_ge(S("dt_abs"), 1)
            A_(alog, alog, ACT.Exp).then_inc(S("alog"), 1)
            A_(dtmp, dtmp, ACT.Exp, scale=-1.0).then_inc(S("dt_e"), 1)
            act.wait_ge(S("dt_e"), 1)
            A_(dtmp, dtmp, ACT.Ln, bias=1.0).then_inc(S("dt_ln"), 1)
            drained(act, ("cs",))
            A_(ea[:, 0, 0:SH], acs[:, 1, 0:SH], ACT.Exp)
            A_(ea[:, 1, 0:SH], acs[:, 2, 0:SH], ACT.Exp).then_inc(S("ea"), 1)
            ps = filled(act, ("pm",))
            for h in range(2):
                ins = A_(mixT[:, h, :], ps[:, h * SEQ:(h + 1) * SEQ], ACT.Copy, scale=par("pool_scale_2", h))
            ins.then_inc(*free(("pm",)))
            for i in range(NT):
                for q in range(3):
                    drained(act, ("rb", i, q))
                A_(dec[:, i], dec[:, i], ACT.Exp).then_inc(S("dec_e"), 1)
            for i in range(NT):
                for a in range(2):
                    ps = filled(act, ("xt", i, a))
                    w = 512 if a == 0 else 256
                    A_(xtok[:, i, 512 * a:512 * a + w], ps[:, 0:w], ACT.Copy).then_inc(*free(("xt", i, a)))
            ps = filled(act, ("bt",))
            A_(btk, ps[:, :], ACT.Copy).then_inc(*free(("bt",)))
            for a in range(2):
                ps = filled(act, ("cst", a))
                A_(st[:, 384 * a:384 * a + 384], ps[:, 0:384], ACT.Copy).then_inc(*free(("cst", a)))
            for i in range(NT):
                act.wait_ge(S("gms"), i + 1)
                A_(gms[:, GRP * i:GRP * i + GRP], gms[:, GRP * i:GRP * i + GRP], ACT.Sqrt).then_inc(S("gsd"), 1)
                for a in range(2):
                    ps = filled(act, ("mt", i, a))
                    for c in range(4 if a == 0 else 2):
                        m = 4 * a + c
                        ins = A_(mixT[:, 2 + m, i * P:(i + 1) * P], ps[:, c * P:(c + 1) * P], ACT.Copy,
                                 scale=par("ssd_norm_w_2", m))
                    ins.then_inc(*free(("mt", i, a)))
            pre_norm(5, lambda i: act.wait_ge(S("x_new"), 4 + i + 1))
            root(5)
            transposed(3, lambda k: modc[:, 32 + k:33 + k], lambda k: modc[:, 24 + k:25 + k])
            act.wait_ge(S("xn"), 8)
            bcast(fin, A["final_norm_w"], "fin_in")
            act.wait_ge(S("g_shift"), 1)
            A_(rtb[0][:, 0:NT * EG], rtb[0][:, 0:NT * EG], ACT.Exp).then_inc(S("g_exp"), 1)
            act.wait_ge(S("v_gap"), 1)
            A_(rtb[1][:, 0:NT], rtb[1][:, 0:NT], ACT.Exp).then_inc(S("v_exp"), 1)
            act.wait_ge(S("crowded"), 1)
            many = act.value_load(crowded[0:1, 0:1])
            with act.If(many > 0):
                with act.Fori(0, EP) as it:
                    for x in range(2):
                        for i in range(NT):
                            act.wait_ge(S("hidden"), it * 8 + (4 * x + 2 * i + 2))
                            A_(sa[:, i, :], bank[4 + 2 * i][:, :], ACT.Silu).then_inc(S("sa"), 1)
                        for i in range(NT):
                            act.wait_ge(S("turns"), it * 4 + (2 * x + i + 1))
                            A_(acT[:, i, :, :], bank[4 + 2 * i][:, :].rearrange("p (f t) -> p f t", f=KE), ACT.Copy
                               ).then_inc(S("turned"), 1)
            with act.Else():
                def gathered(p):
                    act.wait_ge(S("gathered"), p * 2 + 1)
                    for k in range(4):
                        ins = A_(hg[:, k, :], bank[4][:, k * P:(k + 1) * P], ACT.Identity, bias=modc[:, 24 + k:25 + k],
                                 scale=modc[:, 32 + k:33 + k])
                    ins.then_inc(S("hg"), 1)

                def silu(p):
                    act.wait_ge(S("w13_used"), p * 4 + 4)
                    A_(sa[:, 0, :], bank[6][:, :], ACT.Silu).then_inc(S("sa"), 1)

                def turned(p):
                    act.wait_ge(S("turns"), p + 1)
                    A_(acT[:, 0, :, :], bank[6][:, :].rearrange("p (f t) -> p f t", f=KE), ACT.Copy).then_inc(S("ac_turned"), 1)

                def slots_out(p):
                    act.wait_ge(S("w2_used"), p * 2 + 2)
                    A_(yslot[0], bank[4][:, :], ACT.Copy).then_inc(S("y_slots"), 1)

                gathered(0)
                with act.Fori(0, EP - 1) as it:
                    silu(it)
                    gathered(it + 1)
                    turned(it)
                    slots_out(it)
                silu(EP - 1)
                turned(EP - 1)
                slots_out(EP - 1)
            load_root(2)
            pre_norm(6, lambda i: act.wait_ge(S("x_new"), 6 + i + 1))
            root(6)

        @block.gpsimd
        def _(pool):
            def first_low(n):
                _, words = split_words(n)
                two = n < BY_TWO
                pool.wait_ge(S("high"), 2 * n + (1 if two else 2))
                low_part(nc.gpsimd, n, 0, words // 2 if two else words).then_inc(S("low"), 1)

            for n in range(N_RW):
                first_low(n)
            pool.wait_ge(S("csil"), 1)
            nc.gpsimd.tensor_copy(cb, csil.unsqueeze(2).to_broadcast([P, KD, 32])).then_inc(S("cb"), 1)
            strict = K("strict").unsqueeze(1).unsqueeze(1).to_broadcast([P, 4, 2, P])

            def diagonal(buf, half):
                return buf[:, 4 * half:4 * half + 4, :].rearrange("p h (b t) -> p h b t", b=3)[:, :, 0:3:2, :]

            pool.wait_ge(S("con_in"), 16)
            for half in range(2):
                pool.wait_ge(S("att_ln"), half + 1)
                hs = slice(4 * half, 4 * half + 4)
                nc.gpsimd.tensor_tensor(rz[:, hs, :], rz[:, hs, :], az[:, hs, :], ALU.add).then_inc(S("att_sum"), 1)
                pool.wait_ge(S("att_sum"), half + 1)
                nc.gpsimd.tensor_tensor(diagonal(rz, half), diagonal(rz, half), strict, ALU.mult).then_inc(S("att_sp"), 1)
            for half in range(2):
                pool.wait_ge(S("att_x"), half + 1)
                nc.gpsimd.tensor_tensor(diagonal(az, half), diagonal(az, half), strict, ALU.mult).then_inc(S("att_w"), 1)
            eye = K("ident").unsqueeze(1).to_broadcast([P, HEADS, P])
            for i in range(NT):
                for key in [("o", p) for p in range(PAIRS)] if i == 0 else [("y", 0)]:
                    drained(pool, key)
                nc.gpsimd.tensor_copy(dd, eye).then_inc(S("eye"), 1)
                nc.gpsimd.tensor_copy(ddT, eye).then_inc(S("eye"), 1)
            for n in range(N_RW, N_FF):
                first_low(n)
            for dm in range(KD):
                drained(pool, ("mg", dm))
                nc.gpsimd.tensor_tensor(gates[dm], gates[dm], gates[KD + dm], ALU.add).then_inc(S("merged"), 1)
            for n in range(N_FF, len(SPLIT)):
                first_low(n)
                c = n - N_FF - 3
                if 0 <= c < KF // 2:
                    pool.wait_ge(S("f_high"), c + 1)
                    f = slice(2 * c, 2 * c + 2)
                    nc.gpsimd.tensor_tensor(fT_lo[:, f, :], fT[:, f, :], fh[:, f, :].bitcast(F32), ALU.subtract).then_inc(S("f_low"), 1)

        @block.vector
        def _(dve):
            V = nc.vector
            steps = [0]

            def link(ins):
                steps[0] += 1
                ins.then_inc(S("dve_step"), 1)
                dve.wait_ge(S("dve_step"), steps[0])

            def cast(ap, *shape):
                return ap.to_broadcast(list(shape))

            sq_seen = [0]

            def inverse_root(n, halves):
                sq_seen[0] += NT * halves
                dve.wait_ge(S("sq"), sq_seen[0])
                src = ss[n][:, 0:NT]
                if halves == 2:
                    v = ss[n].rearrange("p (i h) -> p i h", h=2)
                    link(V.tensor_tensor(ms[n][:, 0:NT], v[:, :, 0], v[:, :, 1], ALU.add))
                    src = ms[n][:, 0:NT]
                V.tensor_scalar(ms[n][:, 0:NT], src, 1.0 / D, EPS, ALU.mult, ALU.add).then_inc(S("ms"), 1)
                dve.wait_ge(S("sd"), n + 1)
                link(V.reciprocal(rstd[n][:, 0:NT], sd[n][:, 0:NT]))

            def pre_norm(n, s):
                inverse_root(n, 1)
                for i in range(NT):
                    V.tensor_scalar(xn[s][:, i, :], xres[:, i, :], rstd[n][:, i:i + 1], None, ALU.mult).then_inc(S("xn"), 1)

            def transposed(s, scale, bias):
                for kk in (1, 3):
                    ps = filled(dve, ("hT", s, kk))
                    for k2 in range(2):
                        k = 2 * kk + k2
                        ins = V.tensor_scalar(hT[:, k, :], ps[:, k2 * SEQ:(k2 + 1) * SEQ], scale(k), bias(k) if bias else None,
                                              ALU.mult, ALU.add if bias else ALU.bypass)
                    ins.then_inc(*free(("hT", s, kk)))

            low_seen = [0]

            def transposed_low(s, scale, bias):
                for kk in range(4):
                    ps = filled(dve, ("hT", s, kk))
                    low_seen[0] += 1
                    dve.wait_ge(S("h_high"), low_seen[0])
                    two = slice(2 * kk, 2 * kk + 2)
                    for k2 in range(2):
                        k = 2 * kk + k2
                        cols = ps[:, k2 * SEQ:(k2 + 1) * SEQ]
                        if bias:
                            ins = V.tensor_scalar(hT[:, k, :], cols, scale(k), bias(k), ALU.mult, ALU.add)
                        else:
                            ins = V.scalar_tensor_tensor(hT_lo[:, k, :], cols, scale(k), hT_hi[s][:, k, :].bitcast(F32), ALU.mult, ALU.subtract)
                    if bias:
                        link(ins)
                        ins = V.tensor_tensor(hT_lo[:, two, :], hT[:, two, :], hT_hi[s][:, two, :].bitcast(F32), ALU.subtract)
                    ins.then_inc(*free(("hT", s, kk)))

            def second_low(n):
                dve.wait_ge(S("high"), 2 * n + 2)
                _, words = split_words(n)
                low_part(V, n, words // 2, words).then_inc(S("low2"), 1)

            def post_norm(n, name, buf, weight):
                for j in range(4):
                    half, i = (j // 2, j % 2) if name == "mo" else (j % 2, j // 2)
                    ps = filled(dve, (name, i, half))
                    dve.wait_ge(S("sq"), sq_seen[0] + j + 1)
                    V.tensor_tensor(buf[:, i, 512 * half:512 * half + 512], ps[:, :], weight[:, 512 * half:512 * half + 512], ALU.mult).then_inc(*free((name, i, half)))
                inverse_root(n, 2)
                for j in range(4):
                    drained(dve, (name, j % 2, j // 2))
                for i in range(NT):
                    V.scalar_tensor_tensor(xres[:, i, :], buf[:, i, :], rstd[n][:, i:i + 1], xres[:, i, :], ALU.mult, ALU.add
                                           ).then_inc(S("x_new"), 1)

            def columns(t):
                n = sum(r for _, r in PAR[t])
                ps = filled(dve, ("par", t))
                V.tensor_copy(parcol[:, PARBLOCK[t]:PARBLOCK[t + 1]], ps[:, 0:n]).then_inc(*free(("par", t)))

            dve.wait_ge(S("x_in"), 16)
            pre_norm(0, 0)
            columns(0)
            drained(dve, ("par", 0))
            V.tensor_scalar(omu, par("mu_rw", 0, 14), -1.0, 1.0, ALU.mult, ALU.add).then_inc(S("omu"), 1)
            transposed(0, lambda k: par("norm_mix_pre", k), None)
            dve.wait_ge(S("h0_high"), 1)
            V.tensor_tensor(hT0_lo[:, :, :], hT[:, :, :], hT_hi[0][:, :, :].bitcast(F32), ALU.subtract).then_inc(S("h0_low"), 1)
            second_low(0)

            def shifted(m):
                if m < 4:
                    return rT[:, m, :]
                if m < 8:
                    return kT[:, m - 4, :]
                return vT[:, m - 8, :] if m < 12 else lora[:, m - 12, :]

            for n, j in enumerate(RW_ORDER):
                ps = filled(dve, ("rw", j))
                dve.wait_ge(S("rw_own"), n + 1)
                for h in range(2):
                    m = 2 * j + h
                    dst = shifted(m)[:, 1:SEQ]
                    ins = V.scalar_tensor_tensor(dst, ps[:, h * SEQ:(h + 1) * SEQ - 1], par("mu_rw", m), dst, ALU.mult, ALU.add)
                ins.then_inc(*free(("rw", j)))
                if n == 0:
                    for t in range(1, NPAR):
                        columns(t)
                    for t in range(1, NPAR):
                        drained(dve, ("par", t))
                    second_low(1)
                if j == 3:
                    drained(dve, ("rw", 2))
                    drained(dve, ("rw", 3))
                    for m in range(4):
                        ins = V.tensor_scalar(kkT[:, m, :], kT[:, m, :], par("k_k", m), None, ALU.mult)
                    ins.then_inc(S("kk_raw"), 1)
                    second_low(2)
                    dve.wait_ge(S("lvl_in"), 16)
                    link(V.tensor_copy(lvl[:, :], B("lvlf")))
            dve.wait_ge(S("con_in"), 16)
            for j in range(2):
                drained(dve, ("lw", j))
                for h in range(2):
                    m = 2 * j + h
                    ins = V.tensor_tensor_scan(cum[:, m, :], K("scan_reset"), lw[:, m, :], 0.0, ALU.mult, ALU.add)
            link(ins)
            ch = cum.rearrange("p m (c t) -> p m c t", t=CH)
            tot = total.rearrange("p (m c) -> p m c", c=4)
            V.tensor_copy(tot.unsqueeze(3), ch[:, :, :, CH - 1:CH])
            for j in range(2):
                drained(dve, ("la", j))
            drained(dve, ("kn",))
            for m in range(4):
                ins = V.tensor_scalar(tmp[:, m, :], aT[:, m, :], -1.0, par("k_a", m), ALU.add, ALU.mult)
            link(ins)
            link(V.scalar_tensor_tensor(kT, tmp, 1.0, kT, ALU.add, ALU.mult))
            link(V.tensor_scalar(nmr[0:HEADS, :], nmr[0:HEADS, :], 1e-12, None, ALU.max))
            V.reciprocal(nmr[0:HEADS, :], nmr[0:HEADS, :]).then_inc(S("kk_inv"), 1)
            for m in range(4):
                ins = V.scalar_tensor_tensor(bon[:, m, :], rT[:, m, :], par("r_k", m), kT[:, m, :], ALU.mult, ALU.mult)
            ins.then_inc(S("bon_raw"), 1)
            for j in range(2, 4):
                ps = filled(dve, ("qk", j))
                V.tensor_copy(qk[:, 2 * j:2 * j + 2, :].rearrange("p a b -> p (a b)"), ps[:, :]).then_inc(*free(("qk", j)))
            for i in range(NT):
                ps = filled(dve, ("v", i))
                V.tensor_copy(vtok[:, i, :], ps[:, :]).then_inc(*free(("v", i)))
            for j in range(2):
                ps = filled(dve, ("kb", j))
                V.tensor_tensor(kkT[:, 2 * j:2 * j + 2, :], kkT[:, 2 * j:2 * j + 2, :],
                                ps[:, :].rearrange("p (a b) -> p a b", a=2), ALU.mult).then_inc(*free(("kb", j)))
            for j in range(2):
                drained(dve, ("kb", j))
            V.tensor_tensor(bT, kkT, aT, ALU.mult)
            V.tensor_tensor(lw, cum, lw, ALU.subtract).then_inc(S("ex"), 1)
            for h in range(HEADS):
                ps = filled(dve, ("z", h))
                link(V.tensor_scalar(rz[:, h, :], ps[:, 0:384], 0.0, None, ALU.max))
                V.scalar_tensor_tensor(az[:, h, :], rz[:, h, :], -2.0, ps[:, 0:384], ALU.mult, ALU.add).then_inc(*free(("z", h)))

            def by_tile(x):
                return x.rearrange("p a (i t) -> p a i t", i=NT)

            dve.wait_ge(S("e_inc"), 1)
            V.tensor_tensor(kr[:, :, :, 1, :], by_tile(rT), by_tile(aT), ALU.mult).then_inc(S("kr_r"), 1)
            dve.wait_ge(S("e_exc"), 1)
            V.scalar_tensor_tensor(kr[:, :, :, 0, :], by_tile(kkT), -1.0, by_tile(lw), ALU.mult, ALU.mult).then_inc(S("kr_k"), 1)
            dve.wait_ge(S("e_inv"), 1)
            V.tensor_tensor(bh, bT, tmp, ALU.mult)
            V.tensor_tensor(kh, kT, tmp, ALU.mult).then_inc(S("bk_hat"), 1)
            V.tensor_tensor(ch, cast(tot.unsqueeze(3), P, 4, 4, CH), ch, ALU.subtract).then_inc(S("to_end"), 1)
            for j in range(2):
                ps = filled(dve, ("bn", j))
                V.tensor_tensor(bon[:, 2 * j:2 * j + 2, :], ps[:, :].rearrange("p (a b) -> p a b", a=2),
                                vT[:, 2 * j:2 * j + 2, :], ALU.mult).then_inc(*free(("bn", j)))
            dve.wait_ge(S("e_suf"), 1)
            V.tensor_tensor(bT, bT, cum, ALU.mult)
            V.tensor_tensor(kT, kT, cum, ALU.mult).then_inc(S("bk_bar"), 1)
            for i in range(NT):
                ps = filled(dve, ("tok", i, 2))
                V.tensor_copy(ktok[:, i, :], ps[:, :]).then_inc(*free(("tok", i, 2)))
                ps = filled(dve, ("tok", i, 3))
                V.memset(vp[:, i, :, DH:P], 0.0)
                V.tensor_copy(vp[:, i, :, 0:DH], ps[:, :].rearrange("p (h d) -> p h d", h=HEADS)).then_inc(*free(("tok", i, 3)))
            for h in range(HEADS):
                ps = filled(dve, ("l", h))
                V.tensor_scalar(az[:, h, :], ps[:, 0:384], 0.0, None, ALU.min).then_inc(*free(("l", h)))

            def heads4(ps):
                return ps[:, :].rearrange("p (h t) -> p h t", h=4)

            blocks = cast(K("head_block").unsqueeze(1), P, PAIRS, P)

            def ada_sum(c):
                ps = filled(dve, ("as", c))
                if c in COLUMN_CHUNKS:
                    V.tensor_tensor(modc[:, 4 * c:4 * c + 4], ps[:, 0:4], par("b_ada_2", 4 * c, 4), ALU.add).then_inc(*free(("as", c)))
                else:
                    g = (g1 if c < 6 else g2)[:, 512 * (c % 2):512 * (c % 2) + 512]
                    V.tensor_tensor(g, g, ps[:, :], ALU.add).then_inc(*free(("as", c)))

            dve.wait_ge(S("gate_in"), 32)
            dve.wait_ge(S("pc"), 1)
            c = 1
            for i in range(NT):
                for h in range(HEADS):
                    ps = filled(dve, ("g", i, h))
                    V.tensor_tensor(gm[:, h, :], ps[:, :], K("gram_mask"), ALU.mult).then_inc(*free(("g", i, h)))
                dve.wait_ge(S("eye"), 2 * i + 2)
                for q in range(2):
                    hs = slice(4 * q, 4 * q + 4)
                    ps = filled(dve, ("n", i, q))
                    V.copy_predicated(dd[:, hs, :], lmask(0, 0), heads4(ps)).then_inc(*free(("n", i, q)))
                    drained(dve, ("g", i, 4 * q + 3))
                    V.copy_predicated(ddT[:, hs, :], lmask(0, 1), gm[:, hs, 0:P]).then_inc(S("dt_first"), 1)
                for lv in range(1, LEVELS):
                    ada_sum(c - 1)
                    c += 1
                    for q in range(2):
                        hs = slice(4 * q, 4 * q + 4)
                        if lv < LEVELS - 1:
                            ps = filled(dve, ("d", i, lv, q))
                            V.copy_predicated(dd[:, hs, :], lmask(lv, 0), heads4(ps)).then_inc(*free(("d", i, lv, q)))
                        ps = filled(dve, ("dt", i, lv, q))
                        V.copy_predicated(ddT[:, hs, :], lmask(lv, 1), heads4(ps)).then_inc(*free(("dt", i, lv, q)))
                ada_sum(c - 1)
                c += 1
                ps = filled(dve, ("ry", i))
                V.tensor_tensor(ryT[:, :, i * P:(i + 1) * P], heads4(ps), kr[:, :, i, 1, :], ALU.add).then_inc(*free(("ry", i)))
                for k in (2 * i, 2 * i + 1):
                    if k == 3:
                        continue
                    ps = filled(dve, ("psi", k))
                    V.tensor_tensor(psi[:, k], heads4(ps), blocks, ALU.mult).then_inc(*free(("psi", k)))
                k = i + 1
                ps = filled(dve, ("phi", k))
                V.tensor_tensor(phi[:, k - 1], heads4(ps), blocks, ALU.mult).then_inc(*free(("phi", k)))
                drained(dve, ("phi", k))
                for p in range(PAIRS):
                    ins = V.scalar_tensor_tensor(phi[:, k - 1, p, :], K("ident"), pc[:, 4 * p + k:4 * p + k + 1],
                                                 phi[:, k - 1, p, :], ALU.mult, ALU.add)
                ins.then_inc(S("phi"), 1)
                ps = filled(dve, ("s", k))
                drained(dve, ("psi", k))
                V.tensor_tensor(psi[:, k], psi[:, k], heads4(ps), ALU.add).then_inc(*free(("s", k)))
            for c in COLUMN_CHUNKS:
                drained(dve, ("as", c))
            link(V.tensor_scalar(modc[:, 8:16], modc[:, 8:16], 1.0, None, ALU.add))
            V.tensor_scalar(modc[:, 32:40], modc[:, 32:40], 1.0, None, ALU.add).then_inc(S("mod"), 1)
            for i in range(NT):
                drained(dve, ("y", i))
            for j in range(2):
                ps = filled(dve, ("m", j))
                V.tensor_tensor(yT[:, 2 * j:2 * j + 2, :], yT[:, 2 * j:2 * j + 2, :],
                                ps[:, :].rearrange("p (a b) -> p a b", a=2), ALU.subtract).then_inc(*free(("m", j)))
            dve.wait_ge(S("h3_high"), 1)
            V.tensor_tensor(hT3_lo[:, :, :], hT[:, :, :], hT_hi[3][:, :, :].bitcast(F32), ALU.subtract).then_inc(S("h3_low"), 1)
            second_low(N_RW)
            second_low(N_RW + 1)
            dve.wait_ge(S("osb_high"), 1)
            V.tensor_tensor(osb_lo[:, :, :], osb, osb_hi[:, :, :].bitcast(F32), ALU.subtract).then_inc(S("osb_low"), 1)
            ps = filled(dve, ("vn",))
            V.tensor_scalar(nmr[0:HEADS, :], ps[0:HEADS, 0:SEQ], 1.0 / DH, GN_EPS, ALU.mult, ALU.add).then_inc(*free(("vn",)))
            dve.wait_ge(S("y_sd"), 1)
            V.reciprocal(nmr[0:HEADS, :], nmr[0:HEADS, :]).then_inc(S("y_inv"), 1)
            second_low(N_RW + 2)
            for j in range(2):
                drained(dve, ("m", j))
                ps = filled(dve, ("vb", j))
                V.tensor_tensor(yT[:, 2 * j:2 * j + 2, :], yT[:, 2 * j:2 * j + 2, :],
                                ps[:, :].rearrange("p (a b) -> p a b", a=2), ALU.mult).then_inc(*free(("vb", j)))
            for j in range(2):
                drained(dve, ("vb", j))
            for m in range(4):
                ins = V.tensor_scalar(yT[:, m, :], yT[:, m, :], par("lnx_w", m), par("lnx_b", m), ALU.mult, ALU.add)
            link(ins)
            for j in range(2):
                drained(dve, ("bn", j))
            link(V.tensor_tensor(yT, yT, bon, ALU.add))
            V.tensor_tensor(orw, yT, gT, ALU.mult).then_inc(S("orw"), 1)
            dve.wait_ge(S("orw_high"), 1)
            V.tensor_tensor(orw_lo[:, :, :], orw, orw_hi[:, :, :].bitcast(F32), ALU.subtract).then_inc(S("orw_low"), 1)
            second_low(N_RW + 3)
            for j in range(8):
                drained(dve, ("ga", j))
            for dm in range(KD):
                ps = filled(dve, ("mg", dm))
                V.tensor_tensor(gates[dm], gates[dm], ps[:, 0:SEQ], ALU.mult)
                V.tensor_tensor(gates[KD + dm], gates[KD + dm], ps[:, SEQ:2 * SEQ], ALU.mult).then_inc(*free(("mg", dm)))
            dve.wait_ge(S("npost_in"), 16)
            second_low(N_FF)
            post_norm(1, "mo", mo, npost)
            for i in range(NT):
                dve.wait_ge(S("x_new"), i + 1)
            pre_norm(2, 1)
            transposed_low(1, lambda k: par("norm_ffn_pre", k), None)
            second_low(N_FF + 1)
            second_low(N_FF + 2)
            for f in range(KF):
                ps = filled(dve, ("ff", f))
                dve.wait_ge(S("sil"), f + 1)
                V.tensor_tensor(fT[:, f, :], sil[:, f % 2, :], ps[:, SEQ:2 * SEQ], ALU.mult).then_inc(*free(("ff", f)))
                if f % 2:
                    second_low(N_FF + f // 2 + 3)
            for n in range(N_FF + KF // 2 + 3, BY_TWO):
                second_low(n)
            dve.wait_ge(S("post_in"), 16)
            post_norm(3, "dn", dno, fpost)
            dve.wait_ge(S("x_new"), 4)
            pre_norm(4, 2)
            dve.wait_ge(S("mod"), 1)
            transposed_low(2, lambda k: modc[:, 8 + k:9 + k], lambda k: modc[:, k:k + 1])
            for j in range(7):
                drained(dve, ("xb", j))
                for d in range(1, 4):
                    for h in range(2):
                        m = 2 * j + h
                        ins = V.scalar_tensor_tensor(xs[:, m, d:SEQ], xraw[:, m, 0:SEQ - d], par("conv_w_2", (3 - d) * MX + m),
                                                     xs[:, m, d:SEQ], ALU.mult, ALU.add)
                    if d < 3:
                        link(ins)
                    else:
                        ins.then_inc(S("conv"), 1)
            dve.wait_ge(S("router_in"), 64)
            ps = filled(dve, ("dt2",))
            V.tensor_tensor(dtr, ps[:, 0:32].rearrange("p (i c) -> p i c", i=NT)[:, :, 0:SH], cast(dtb.unsqueeze(1), P, NT, SH),
                            ALU.add).then_inc(*free(("dt2",)))
            drained(dve, ("dt2",))
            V.scalar_tensor_tensor(dtmp, dtr, -1.0, dtr, ALU.mult, ALU.max).then_inc(S("dt_abs"), 1)
            ps = filled(dve, ("pl",))
            V.tensor_copy(dif.rearrange("p a b -> p (a b)"), ps[:, :]).then_inc(*free(("pl",)))
            dve.wait_ge(S("dt_ln"), 1)
            link(V.scalar_tensor_tensor(dtr, dtr, 0.0, dtmp, ALU.max, ALU.add))
            dve.wait_ge(S("alog"), 1)
            V.scalar_tensor_tensor(da, dtr, -1.0, cast(alog.unsqueeze(1), P, NT, SH), ALU.mult, ALU.mult).then_inc(S("da"), 1)
            ps = filled(dve, ("cs",))
            V.tensor_copy(acs[:, :, 0:SH], ps[:, 0:48].rearrange("p (i c) -> p i c", i=3)[:, :, 0:SH]).then_inc(*free(("cs",)))
            drained(dve, ("cs",))
            for i in range(NT):
                for q in range(3):
                    ps = filled(dve, ("rb", i, q))
                    for j in range(4):
                        h = 4 * q + j
                        ins = V.tensor_scalar(dec[:, i, h, :], ps[:, j * P:(j + 1) * P], acs[:, i, h:h + 1], 0.0, ALU.subtract, ALU.min)
                    ins.then_inc(*free(("rb", i, q)))
            def by_head(x):
                return x.rearrange("p (h d) -> p h d", h=SH)

            for i in range(NT):
                ps = filled(dve, ("cb", i))
                V.tensor_tensor(cbm[:, i], heads4(ps), cast(K("causal").unsqueeze(1), P, GRP, P), ALU.mult).then_inc(*free(("cb", i)))
                dve.wait_ge(S("dec_e"), i + 1)
                drained(dve, ("cb", i))
                d4 = dec[:, i].rearrange("p (g r) t -> p g r t", g=GRP)
                V.tensor_tensor(d4, d4, cast(cbm[:, i].unsqueeze(2), P, GRP, SR, P), ALU.mult).then_inc(S("dec"), 1)
                dve.wait_ge(S("ea"), 1)
                for a in range(2):
                    drained(dve, ("xt", i, a))
                V.tensor_tensor(by_head(xc[:, i]), by_head(xtok[:, i]), cast(dtr[:, i, :].unsqueeze(2), P, SH, DH), ALU.mult
                                ).then_inc(S("xc"), 1)
                if i == 0:
                    dve.wait_ge(S("xc"), 1)
                    V.tensor_tensor(by_head(xde), by_head(xc[:, 0]), cast(ea[:, 1, 0:SH].unsqueeze(2), P, SH, DH), ALU.mult
                                    ).then_inc(S("xde"), 1)
            dve.wait_ge(S("par2_in"), 48)
            GW = SR * DH

            def skip_and_diagonal(i):
                link(V.tensor_tensor(by_head(ys[:, i]), by_head(xtok[:, i]), cast(dsk.unsqueeze(2), P, SH, DH), ALU.mult))
                for a in range(2):
                    w = 512 if a == 0 else 256
                    f = slice(512 * a, 512 * a + w)
                    ps = filled(dve, ("yd", i, a))
                    V.tensor_tensor(ys[:, i, f], ys[:, i, f], ps[:, 0:w], ALU.add).then_inc(*free(("yd", i, a)))
                for a in range(2):
                    drained(dve, ("yd", i, a))

            def gated_norm(i):
                g = slice(GRP * i, GRP * i + GRP)
                link(V.tensor_tensor(ys[:, i], ys[:, i], sz[:, i], ALU.mult))
                link(V.tensor_tensor(ysq[:, i], ys[:, i], ys[:, i], ALU.mult))
                link(V.tensor_reduce(gss[:, g], ysq[:, i].rearrange("p (g d) -> p g d", g=GRP), AX.X, ALU.add))
                V.tensor_scalar(gms[:, g], gss[:, g], 1.0 / GW, EPS, ALU.mult, ALU.add).then_inc(S("gms"), 1)
                dve.wait_ge(S("gsd"), i + 1)
                link(V.reciprocal(gss[:, g], gms[:, g]))
                yg = ys[:, i].rearrange("p (g d) -> p g d", g=GRP)
                V.tensor_tensor(yg, yg, cast(gss[:, g].unsqueeze(2), P, GRP, GW), ALU.mult).then_inc(S("ys"), 1)

            skip_and_diagonal(0)
            gated_norm(0)
            skip_and_diagonal(1)
            for a in range(2):
                ps = filled(dve, ("yo", a))
                f = slice(384 * a, 384 * a + 384)
                V.tensor_tensor(yo[:, f].rearrange("p (h d) -> p h d", d=DH), ps[:, 0:384].rearrange("p (h d) -> p h d", d=DH),
                                cast(ea[:, 0, 6 * a:6 * a + 6].unsqueeze(2), P, 6, DH), ALU.mult).then_inc(*free(("yo", a)))
            for a in range(2):
                drained(dve, ("yo", a))
            link(V.tensor_tensor(ys[:, 1], ys[:, 1], yo, ALU.add))
            gated_norm(1)
            for c in (4, 5, 10, 11):
                drained(dve, ("as", c))
            for i in range(NT):
                for n in range(2):
                    f = slice(512 * n, 512 * n + 512)
                    ps = filled(dve, ("mx", i, n))
                    V.tensor_tensor(gtmp, ps[:, :], g1[:, f], ALU.mult).then_inc(*free(("mx", i, n)))
                    drained(dve, ("mx", i, n))
                    ins = V.tensor_tensor(xres[:, i, f], xres[:, i, f], gtmp, ALU.add)
                    if n == 1:
                        ins.then_inc(S("x_new"), 1)
                        dve.wait_ge(S("x_new"), 5 + i)
                    else:
                        link(ins)
            dve.wait_ge(S("x_new"), 6)
            pre_norm(5, 3)
            transposed(3, lambda k: modc[:, 32 + k:33 + k], lambda k: modc[:, 24 + k:25 + k])
            V.memset(junk[0:1, 0:512], 0.0)
            V.memset(rs[0:1, 0:1], 0.0).then_inc(S("zero"), 1)
            ps = filled(dve, ("rt",))
            V.tensor_tensor(lg, ps[:, 0:NT * 64].rearrange("p (i c) -> p i c", i=NT)[:, :, 0:36], cast(rbias.unsqueeze(1), P, NT, 36),
                            ALU.add).then_inc(*free(("rt",)))
            drained(dve, ("rt",))

            def first_max(hot, vals, best, rev, n, keep):
                flag, top = keep
                link(V.tensor_reduce(best, vals, AX.X, ALU.max))
                link(V.tensor_tensor(flag, vals, cast(best.unsqueeze(2), P, NT, n), ALU.is_ge))
                link(V.tensor_tensor(flag, flag, rev, ALU.mult))
                link(V.tensor_reduce(top, flag, AX.X, ALU.max))
                link(V.tensor_tensor(hot, flag, cast(top.unsqueeze(2), P, NT, n), ALU.is_equal))

            def wide(buf, n):
                return buf[:, 0:NT * n].rearrange("p (i c) -> p i c", i=NT)

            best_g, v1, v2, top, gsum = (rtb[7][:, 2 * n:2 * n + 2] for n in range(5))
            hot_g = wide(rtb[2], EG)
            flag = wide(rtb[3], EG)
            first_max(hot_g, lg[:, :, 0:EG], best_g, wide(K("rev_group"), EG), EG, (flag, top))
            ex_g = wide(rtb[0], EG)
            V.tensor_tensor(ex_g, lg[:, :, 0:EG], cast(best_g.unsqueeze(2), P, NT, EG), ALU.subtract).then_inc(S("g_shift"), 1)
            link(V.tensor_scalar(hot_g, hot_g, 1.0, BIG, ALU.subtract, ALU.mult))
            inside = wide(rtb[4], EXPERTS)
            link(V.tensor_tensor(inside.rearrange("p i (g e) -> p i g e", g=EG),
                                 lg[:, :, EG:36].rearrange("p i (g e) -> p i g e", g=EG),
                                 cast(hot_g.unsqueeze(3), P, NT, EG, EPG), ALU.add))
            hot1, hot2, flag = wide(rtb[5], EXPERTS), wide(rtb[6], EXPERTS), wide(rtb[3], EXPERTS)
            rev = wide(K("rev_expert"), EXPERTS)
            first_max(hot1, inside, v1, rev, EXPERTS, (flag, top))
            link(V.scalar_tensor_tensor(inside, hot1, -3.0 * BIG, inside, ALU.mult, ALU.add))
            first_max(hot2, inside, v2, rev, EXPERTS, (flag, top))
            V.tensor_tensor(rtb[1][:, 0:NT], v2, v1, ALU.subtract).then_inc(S("v_gap"), 1)
            sel = wide(rtb[4], EXPERTS)
            V.tensor_tensor(sel, hot1, hot2, ALU.add).then_inc(S("chosen"), 1)
            dve.wait_ge(S("chosen"), 1)
            dve.wait_ge(S("g_exp"), 1)
            link(V.tensor_reduce(gsum, ex_g, AX.X, ALU.add))
            dve.wait_ge(S("v_exp"), 1)
            link(V.scalar_tensor_tensor(top, rtb[1][:, 0:NT], 1.0, gsum, ALU.add, ALU.mult))
            link(V.reciprocal(top, top))
            link(V.tensor_tensor(hot2, hot2, cast(rtb[1][:, 0:NT].unsqueeze(2), P, NT, EXPERTS), ALU.mult))
            link(V.tensor_tensor(hot1, hot1, hot2, ALU.add))
            V.tensor_tensor(gate, hot1, cast(top.unsqueeze(2), P, NT, EXPERTS), ALU.mult).then_inc(S("gate"), 1)
            dve.wait_ge(S("gate"), 1)
            def by_pair(buf):
                return buf.rearrange("p (q i x) -> p i q x", q=EP, i=NT)

            def pairs(buf):
                return buf.rearrange("p i (q x) -> p i q x", q=EP)

            for i in range(NT):
                link(V.tensor_copy(by_pair(gateq)[:, i], pairs(gate)[:, i]))
            ps = filled(dve, ("rk",))
            ranks = ps[:, 0:NT * EXPERTS].rearrange("p (i c) -> p i c", i=NT)
            for i in range(NT):
                link(V.scalar_tensor_tensor(by_pair(posq)[:, i], pairs(ranks)[:, i], 1.0, pairs(sel)[:, i], ALU.add, ALU.mult))
            most = rtb[7][:, 10:11]
            V.tensor_reduce(most, ps[:, NT * EXPERTS:(NT + 1) * EXPERTS], AX.X, ALU.max).then_inc(*free(("rk",)))
            drained(dve, ("rk",))
            V.tensor_scalar(crowded[:, :], most, CAP + 0.5, None, ALU.is_gt).then_inc(S("crowded"), 1)
            dve.wait_ge(S("crowded"), 1)
            many = dve.value_load(crowded[0:1, 0:1])
            with dve.If(many > 0):
                with dve.Fori(0, EP) as it:
                    for x in range(2):
                        for i in range(NT):
                            dve.wait_ge(S("sa"), it * 4 + (2 * x + i + 1))
                            V.scalar_tensor_tensor(ac[:, i, :], sa[:, i, :], gate[:, i, bass.ds(it * 2 + x, 1)],
                                                   bank[5 + 2 * i][:, :], ALU.mult, ALU.mult).then_inc(S("act_out"), 1)
                dve.wait_ge(S("w2_used"), 2 * EP)
                V.memset(rs[0:1, 0:1], 0.0).then_inc(S("summed"), NT)
            with dve.Else():
                slot = K("slot").unsqueeze(1).to_broadcast([P, 2 * NT, CAP])

                def of_pair(buf, p):
                    return buf[:, bass.ds(p * 4, 4)].unsqueeze(2).to_broadcast([P, 2 * NT, CAP])

                def choose(p):
                    if not isinstance(p, int) or p > 0:
                        dve.wait_ge(S("gathered"), p * 2)
                        dve.wait_ge(S("onew"), p)
                    V.tensor_tensor(one, slot, of_pair(posq, p), ALU.is_equal).then_inc(S("one"), 1)

                def weigh(p):
                    dve.wait_ge(S("one"), p + 1)
                    if not isinstance(p, int) or p > 0:
                        dve.wait_ge(S("w_turns"), p)
                    V.tensor_tensor(onew, one, of_pair(gateq, p), ALU.mult).then_inc(S("onew"), 1)

                def gathered(p):
                    dve.wait_ge(S("gathered"), p * 2 + 2)
                    for k in range(4, KD):
                        ins = V.tensor_scalar(hg[:, k, :], bank[5][:, (k - 4) * P:(k - 3) * P], modc[:, 32 + k:33 + k],
                                              modc[:, 24 + k:25 + k], ALU.mult, ALU.add)
                    ins.then_inc(S("hg"), 1)

                def activate(p):
                    dve.wait_ge(S("sa"), p + 1)
                    V.tensor_tensor(ac[:, 0, :], sa[:, 0, :], bank[7][:, :], ALU.mult).then_inc(S("ac"), 1)

                def weights_turned(p):
                    dve.wait_ge(S("w_turns"), p + 1)
                    V.tensor_copy(onewT, bank[7][:, 0:SEQ]).then_inc(S("w_turned"), 1)

                def slots_out(p):
                    dve.wait_ge(S("w2_used"), p * 2 + 2)
                    V.tensor_copy(yslot[1], bank[5][:, :]).then_inc(S("y_slots"), 1)

                choose(0)
                gathered(0)
                weigh(0)
                choose(1)
                activate(0)
                gathered(1)
                weights_turned(0)
                slots_out(0)
                with dve.Fori(1, EP - 1) as it:
                    weigh(it)
                    choose(it + 1)
                    activate(it)
                    gathered(it + 1)
                    weights_turned(it)
                    slots_out(it)
                weigh(EP - 1)
                activate(EP - 1)
                weights_turned(EP - 1)
                slots_out(EP - 1)
            for i in range(NT):
                dve.wait_ge(S("summed"), i + 1)
                for n in range(2):
                    f = slice(512 * n, 512 * n + 512)
                    link(V.tensor_tensor(gtmp, bank[2 * i + n][:, :], g2[:, f], ALU.mult))
                    ins = V.tensor_tensor(xres[:, i, f], xres[:, i, f], gtmp, ALU.add)
                    if n == 1:
                        ins.then_inc(S("x_new"), 1)
                        dve.wait_ge(S("x_new"), 7 + i)
                    else:
                        link(ins)
            dve.wait_ge(S("x_new"), 8)
            inverse_root(6, 1)
            dve.wait_ge(S("fin_in"), 16)
            for i in range(NT):
                V.scalar_tensor_tensor(xres[:, i, :], xres[:, i, :], rstd[6][:, i:i + 1], fin, ALU.mult, ALU.mult).then_inc(S("y_out"), 1)


_INS = ['x', 'norm_mix_pre', 'w_in', 'b_gate', 'mu_rw', 'w0', 'w_up', 'a0', 'a_up', 'g_up', 'k_k', 'k_a', 'r_k',
        'lnx_w', 'lnx_b', 'w_sb_out', 'w_rw_out', 'w_o', 'norm_mix_post', 'norm_ffn_pre', 'w_ffn_gate', 'w_ffn_up',
        'w_ffn_down', 'norm_ffn_post', 'c_2', 'w_ada_2', 'b_ada_2', 'w_in_2', 'w_pool_2', 'pool_scale_2', 'conv_w_2',
        'conv_b_2', 'dt_bias_2', 'a_log_2', 'd_skip_2', 'ssd_norm_w_2', 'w_out_2', 'w_group_2', 'b_group_2',
        'w_router_2', 'b_router_2', 'w13_2', 'w2_2', 'final_norm_w_2']


def kernel(**inputs):
    import numpy as _np
    import concourse.bacc as _bacc
    from concourse import mybir as _mybir
    from concourse.bass_utils import run_bass_kernel_spmd as _run

    nc = _bacc.Bacc("TRN2", target_bir_lowering=False, num_devices=1)
    arrays, args = {}, {}
    for name in _INS:
        a = _np.ascontiguousarray(inputs[name])
        arrays[f"in_{name}"] = a
        args[name] = nc.dram_tensor(f"in_{name}", a.shape, _mybir.dt.from_np(a.dtype), kind="ExternalInput").ap()
    for name, a in (("consts", host_constants()), ("levels", host_level_masks()), ("bands", host_bands())):
        arrays[name] = a
        args[name] = nc.dram_tensor(name, a.shape, _mybir.dt.from_np(a.dtype), kind="ExternalInput").ap()
    args["final_norm_w"] = args["final_norm_w_2"]
    out = nc.dram_tensor("out", (1, SEQ, D), _mybir.dt.from_np(_np.dtype("float32")), kind="ExternalOutput").ap()
    build(nc, args, out)
    r = _run(nc, [arrays], core_ids=[0])
    return r.results[0]["out"]
```
